# Optimizing a Trainium2 kernel written in Bass

```python
import math
import jax, jax.numpy as jnp
from jax import lax
import numpy as np

D_MODEL = 1024
BATCH = 1
SEQ = 256
DEPTH = 1

MEM_LEN = 256
HEAD_DIM = 64
MIX_WIDTH = D_MODEL
DA_WIDTH = MIX_WIDTH // 2
SB_WIDTH = MIX_WIDTH - DA_WIDTH
DA_HEADS = DA_WIDTH // (2 * HEAD_DIM)
DA_V = 2 * HEAD_DIM
SB_HEADS = SB_WIDTH // HEAD_DIM
DA_Q_COLS = DA_HEADS * 2 * HEAD_DIM
DA_K_COLS = DA_HEADS * 2 * HEAD_DIM
DA_V_COLS = DA_HEADS * DA_V
SB_COLS = SB_HEADS * HEAD_DIM
IN_COLS = DA_Q_COLS + DA_K_COLS + DA_V_COLS + 3 * SB_COLS
ROT_DIM = HEAD_DIM // 4
ROPE_THETA = 500000.0
X_HEADS = 4
X_HEAD_DIM = D_MODEL // X_HEADS
D_FF = 4 * D_MODEL
Q_BLOCK = 128
EPS = 1e-6


def rms_norm(x, g):
    xf = x.astype(jnp.float32)
    y = xf * lax.rsqrt(jnp.mean(xf * xf, axis=-1, keepdims=True) + EPS)
    return (y * g.astype(jnp.float32)).astype(x.dtype)

def rope_tables(positions, dtype):
    inv_freq = ROPE_THETA ** (-jnp.arange(0, ROT_DIM, 2, dtype=jnp.float32) / ROT_DIM)
    ang = positions.astype(jnp.float32)[..., None] * inv_freq
    return jnp.cos(ang).astype(dtype), jnp.sin(ang).astype(dtype)

def apply_partial_rope(x, cos, sin):
    extra = x.ndim - 3
    c = cos.reshape(cos.shape[:2] + (1,) * extra + cos.shape[-1:])
    s = sin.reshape(sin.shape[:2] + (1,) * extra + sin.shape[-1:])
    half = ROT_DIM // 2
    x1, x2, xp = x[..., :half], x[..., half:ROT_DIM], x[..., ROT_DIM:]
    return jnp.concatenate([x1 * c - x2 * s, x2 * c + x1 * s, xp], axis=-1)

def diff_attention(q, k, v, lam, g_subln, lam_init):
    B, S, H = q.shape[0], q.shape[1], q.shape[2]
    nb = S // Q_BLOCK
    scale = 1.0 / math.sqrt(HEAD_DIM)
    kh = k.transpose(0, 2, 3, 1, 4)
    vh = v.transpose(0, 2, 1, 3).astype(jnp.float32)
    qb = q.transpose(0, 2, 3, 1, 4).reshape(B, H, 2, nb, Q_BLOCK, HEAD_DIM)
    qb = jnp.moveaxis(qb, 3, 0)
    qidx = jnp.arange(S, dtype=jnp.int32).reshape(nb, Q_BLOCK)
    kidx = jnp.arange(S, dtype=jnp.int32)

    def block(args):
        qblk, qi = args
        s = jnp.einsum('bhcqd,bhckd->bhcqk', qblk, kh).astype(jnp.float32) * scale
        mask = kidx[None, :] <= qi[:, None]
        p = jax.nn.softmax(jnp.where(mask, s, -jnp.inf), axis=-1)
        w = p[:, :, 0] - lam * p[:, :, 1]
        return jnp.einsum('bhqk,bhkv->bhqv', w, vh)

    o = lax.map(block, (qb, qidx))
    o = o.transpose(1, 0, 3, 2, 4).reshape(B, S, H, DA_V)
    o = rms_norm(o, g_subln) * (1.0 - lam_init)
    return o.reshape(B, S, H * DA_V)

def stick_breaking_attention(q, k, v):
    B, S, H = q.shape[0], q.shape[1], q.shape[2]
    nb = S // Q_BLOCK
    scale = 1.0 / math.sqrt(HEAD_DIM)
    kh = k.transpose(0, 2, 1, 3)
    vh = v.transpose(0, 2, 1, 3).astype(jnp.float32)
    qb = q.transpose(0, 2, 1, 3).reshape(B, H, nb, Q_BLOCK, HEAD_DIM)
    qb = jnp.moveaxis(qb, 2, 0)
    qidx = jnp.arange(S, dtype=jnp.int32).reshape(nb, Q_BLOCK)
    kidx = jnp.arange(S, dtype=jnp.int32)

    def block(args):
        qblk, qi = args
        z = jnp.einsum('bhqd,bhkd->bhqk', qblk, kh).astype(jnp.float32) * scale
        strict = kidx[None, :] < qi[:, None]
        log_beta = jax.nn.log_sigmoid(z)
        log_1mb = jnp.where(strict, jax.nn.log_sigmoid(-z), 0.0)
        between = lax.cumsum(log_1mb, axis=3, reverse=True) - log_1mb
        a = jnp.exp(jnp.where(strict, log_beta + between, -jnp.inf))
        return jnp.einsum('bhqk,bhkd->bhqd', a, vh)

    o = lax.map(block, (qb, qidx))
    return o.transpose(1, 0, 3, 2, 4).reshape(B, S, H * HEAD_DIM)

def cross_attention(h, memn, w_xq, w_xkv, w_xo):
    B, S, _ = h.shape
    q = (h @ w_xq).reshape(B, S, X_HEADS, X_HEAD_DIM)
    kv = memn @ w_xkv
    k = kv[..., :D_MODEL].reshape(B, MEM_LEN, X_HEADS, X_HEAD_DIM)
    v = kv[..., D_MODEL:].reshape(B, MEM_LEN, X_HEADS, X_HEAD_DIM).astype(jnp.float32)
    s = jnp.einsum('bqhd,bkhd->bhqk', q, k).astype(jnp.float32) / math.sqrt(X_HEAD_DIM)
    p = jax.nn.softmax(s, axis=-1)
    o = jnp.einsum('bhqk,bkhd->bqhd', p, v).reshape(B, S, D_MODEL).astype(h.dtype)
    return o @ w_xo

def first_inputs(seed: int = 0) -> dict:
    key = jax.random.key(seed)
    ks = jax.random.split(key, 24)
    f32 = jnp.float32

    def w(k, shape, fan_in):
        return jax.random.normal(k, shape, f32) * (fan_in ** -0.5)

    def gain(k, shape):
        return 1.0 + 0.02 * jax.random.normal(k, shape, f32)

    L = DEPTH
    return {
        "x": jax.random.normal(ks[0], (BATCH, SEQ, D_MODEL), f32),
        "mem": jax.random.normal(ks[1], (BATCH, MEM_LEN, D_MODEL), f32),
        "positions": jnp.broadcast_to(jnp.arange(SEQ, dtype=jnp.int32), (BATCH, SEQ)),
        "g_mix": gain(ks[2], (L, D_MODEL)),
        "w_in": w(ks[3], (L, D_MODEL, IN_COLS), D_MODEL),
        "lambda_q1": 0.1 * jax.random.normal(ks[4], (L, HEAD_DIM), f32),
        "lambda_k1": 0.1 * jax.random.normal(ks[5], (L, HEAD_DIM), f32),
        "lambda_q2": 0.1 * jax.random.normal(ks[6], (L, HEAD_DIM), f32),
        "lambda_k2": 0.1 * jax.random.normal(ks[7], (L, HEAD_DIM), f32),
        "g_subln": gain(ks[8], (L, DA_V)),
        "w_out": w(ks[9], (L, MIX_WIDTH, D_MODEL), MIX_WIDTH),
        "g_cross": gain(ks[10], (L, D_MODEL)),
        "g_mem": gain(ks[11], (L, D_MODEL)),
        "w_xq": w(ks[12], (L, D_MODEL, D_MODEL), D_MODEL),
        "w_xkv": w(ks[13], (L, D_MODEL, 2 * D_MODEL), D_MODEL),
        "w_xo": w(ks[14], (L, D_MODEL, D_MODEL), D_MODEL),
        "g_mlp": gain(ks[15], (L, D_MODEL)),
        "w_up": w(ks[16], (L, D_MODEL, D_FF), D_MODEL),
        "w_down": w(ks[17], (L, D_FF, D_MODEL), D_FF),
        "g_final": gain(ks[18], (D_MODEL,)),
    }

def first_block(x, mem, positions, g_mix, w_in, lambda_q1, lambda_k1, lambda_q2, lambda_k2,
              g_subln, w_out, g_cross, g_mem, w_xq, w_xkv, w_xo, g_mlp, w_up, w_down,
              g_final):
    B, S, _ = x.shape
    cos, sin = rope_tables(positions, x.dtype)
    h = x
    for l in range(DEPTH):
        lam_init = 0.8 - 0.6 * math.exp(-0.3 * l)
        u = rms_norm(h, g_mix[l]) @ w_in[l]
        o0 = 0
        qa = u[..., o0:o0 + DA_Q_COLS].reshape(B, S, DA_HEADS, 2, HEAD_DIM); o0 += DA_Q_COLS
        ka = u[..., o0:o0 + DA_K_COLS].reshape(B, S, DA_HEADS, 2, HEAD_DIM); o0 += DA_K_COLS
        va = u[..., o0:o0 + DA_V_COLS].reshape(B, S, DA_HEADS, DA_V); o0 += DA_V_COLS
        qs = u[..., o0:o0 + SB_COLS].reshape(B, S, SB_HEADS, HEAD_DIM); o0 += SB_COLS
        ksb = u[..., o0:o0 + SB_COLS].reshape(B, S, SB_HEADS, HEAD_DIM); o0 += SB_COLS
        vs = u[..., o0:o0 + SB_COLS].reshape(B, S, SB_HEADS, HEAD_DIM)
        qa = apply_partial_rope(qa, cos, sin)
        ka = apply_partial_rope(ka, cos, sin)
        lam = (jnp.exp(jnp.sum(lambda_q1[l].astype(jnp.float32) * lambda_k1[l].astype(jnp.float32)))
               - jnp.exp(jnp.sum(lambda_q2[l].astype(jnp.float32) * lambda_k2[l].astype(jnp.float32)))
               + lam_init)
        ya = diff_attention(qa, ka, va, lam, g_subln[l], lam_init)
        yb = stick_breaking_attention(qs, ksb, vs)
        y = jnp.concatenate([ya.astype(h.dtype), yb.astype(h.dtype)], axis=-1)
        h = h + y @ w_out[l]
        h = h + cross_attention(rms_norm(h, g_cross[l]), rms_norm(mem, g_mem[l]),
                                w_xq[l], w_xkv[l], w_xo[l])
        a = jnp.square(jax.nn.relu(rms_norm(h, g_mlp[l]) @ w_up[l]))
        h = h + a @ w_down[l]
    return rms_norm(h, g_final)


CHUNK = 64

MLA_HEADS = 8
MLA_Q_RANK = 384
MLA_KV_RANK = 256
MLA_NOPE = 64
MLA_ROPE = 32
MLA_V = 64
MLA_QK = MLA_NOPE + MLA_ROPE
ROPE_THETA_2 = 10000.0

RWKV_HEADS = 8
RWKV_HEAD = 64
RWKV_DIM = RWKV_HEADS * RWKV_HEAD
W_LORA = 64
A_LORA = 64
G_LORA = 128
LN_X_EPS = 64e-5

MIX_WIDTH_2 = MLA_HEADS * MLA_V + RWKV_DIM
MLA_COLS = MLA_Q_RANK + MLA_KV_RANK + MLA_ROPE
RWKV_COLS = 3 * RWKV_DIM + W_LORA + A_LORA + G_LORA
IN_COLS_2 = MLA_COLS + RWKV_COLS
MLA_SPLITS = (MLA_Q_RANK, MLA_Q_RANK + MLA_KV_RANK)
RWKV_SPLITS = (RWKV_DIM, 2 * RWKV_DIM, 3 * RWKV_DIM, 3 * RWKV_DIM + W_LORA, 3 * RWKV_DIM + W_LORA + A_LORA)

PEER_HEADS = 8
N_KEYS = 128
N_EXPERTS = N_KEYS * N_KEYS
PEER_DQ = 256
PEER_DHALF = PEER_DQ // 2
PEER_TOPK = 16
TOK_BLOCK = 128


def rms_norm_2(x, g, eps=EPS):
    xf = x.astype(jnp.float32)
    y = xf * lax.rsqrt(jnp.mean(xf * xf, axis=-1, keepdims=True) + eps)
    return (y * g.astype(jnp.float32)).astype(x.dtype)

def apply_rope(t, positions):
    half = MLA_ROPE // 2
    inv = ROPE_THETA_2 ** (-jnp.arange(half, dtype=jnp.float32) / half)
    ang = positions.astype(jnp.float32)[..., None] * inv
    cos = jnp.cos(ang)[:, :, None, :]
    sin = jnp.sin(ang)[:, :, None, :]
    tf = t.astype(jnp.float32)
    t1, t2 = tf[..., :half], tf[..., half:]
    out = jnp.concatenate([t1 * cos - t2 * sin, t1 * sin + t2 * cos], axis=-1)
    return out.astype(t.dtype)

def mla_group(p_mla, positions, g_cq, g_ckv, w_uq, w_uk, w_uv, g_qnorm, g_knorm, g_attn_out):
    B, S, _ = p_mla.shape
    c_q, c_kv, k_rope = jnp.split(p_mla, MLA_SPLITS, axis=-1)
    q = (rms_norm_2(c_q, g_cq) @ w_uq).reshape(B, S, MLA_HEADS, MLA_QK)
    c_kv = rms_norm_2(c_kv, g_ckv)
    k_nope = (c_kv @ w_uk).reshape(B, S, MLA_HEADS, MLA_NOPE)
    v = (c_kv @ w_uv).reshape(B, S, MLA_HEADS, MLA_V)
    k = jnp.concatenate([k_nope, jnp.broadcast_to(k_rope[:, :, None, :], (B, S, MLA_HEADS, MLA_ROPE))], axis=-1)
    q = rms_norm_2(q, g_qnorm)
    k = rms_norm_2(k, g_knorm)
    q = jnp.concatenate([q[..., :MLA_NOPE], apply_rope(q[..., MLA_NOPE:], positions)], axis=-1)
    k = jnp.concatenate([k[..., :MLA_NOPE], apply_rope(k[..., MLA_NOPE:], positions)], axis=-1)
    scale = MLA_QK ** -0.5
    n_blk = S // Q_BLOCK
    q_blocks = q.reshape(B, n_blk, Q_BLOCK, MLA_HEADS, MLA_QK).transpose(1, 0, 2, 3, 4)
    key_chunk = jnp.arange(S) // CHUNK

    def attend(args):
        qb, bi = args
        q_chunk = (bi * Q_BLOCK + jnp.arange(Q_BLOCK)) // CHUNK
        s = jnp.einsum('bqhd,bkhd->bhqk', qb, k).astype(jnp.float32) * scale
        mask = key_chunk[None, :] <= q_chunk[:, None]
        s = jnp.where(mask[None, None], s, -jnp.inf)
        pr = jax.nn.softmax(s, axis=-1).astype(v.dtype)
        return jnp.einsum('bhqk,bkhd->bqhd', pr, v)

    o = lax.map(attend, (q_blocks, jnp.arange(n_blk)))
    o = o.transpose(1, 0, 2, 3, 4).reshape(B, S, MLA_HEADS, MLA_V)
    o = rms_norm_2(o, g_attn_out.reshape(MLA_HEADS, MLA_V))
    return o.reshape(B, S, MLA_HEADS * MLA_V)

def rwkv7_step(state, inp):
    r_t, w_t, k_t, v_t, kk_t, a_t = inp
    sk = jnp.einsum('bhij,bhj->bhi', state, kk_t)
    state = (state * w_t[:, :, None, :]
             - sk[..., None] * (kk_t * a_t)[:, :, None, :]
             + v_t[..., None] * k_t[:, :, None, :])
    y = jnp.einsum('bhij,bhj->bhi', state, r_t)
    return state, y

def rwkv7_group(p_rwkv, rwkv_mu, w0, w2, a0, a2, g2, k_k, k_a, r_k, ln_x_w, ln_x_b):
    B, S, _ = p_rwkv.shape
    prev = jnp.pad(p_rwkv, ((0, 0), (1, 0), (0, 0)))[:, :S]
    p = p_rwkv + (prev - p_rwkv) * rwkv_mu
    r, k, v, wl, al, gl = jnp.split(p, RWKV_SPLITS, axis=-1)
    w = -jax.nn.softplus(-(w0 + jnp.tanh(wl) @ w2)) - 0.5
    decay = jnp.exp(-jnp.exp(w.astype(jnp.float32)))
    a = jax.nn.sigmoid(a0 + al @ a2)
    g = jax.nn.sigmoid(gl) @ g2
    heads = lambda t: t.astype(jnp.float32).reshape(B, S, RWKV_HEADS, RWKV_HEAD)
    kk = heads(k * k_k)
    kk = kk / jnp.maximum(jnp.sqrt(jnp.sum(kk * kk, axis=-1, keepdims=True)), 1e-12)
    k = k * (1.0 + (a - 1.0) * k_a)
    r_h, k_h, v_h, a_h, w_h = heads(r), heads(k), heads(v), heads(a), heads(decay)
    xs = tuple(jnp.moveaxis(t, 1, 0) for t in (r_h, w_h, k_h, v_h, kk, a_h))
    state0 = jnp.zeros((B, RWKV_HEADS, RWKV_HEAD, RWKV_HEAD), jnp.float32)
    _, y = lax.scan(rwkv7_step, state0, xs)
    y = jnp.moveaxis(y, 0, 1)
    mu = jnp.mean(y, axis=-1, keepdims=True)
    var = jnp.mean(jnp.square(y - mu), axis=-1, keepdims=True)
    y = ((y - mu) * lax.rsqrt(var + LN_X_EPS) * ln_x_w.astype(jnp.float32).reshape(RWKV_HEADS, RWKV_HEAD)
         + ln_x_b.astype(jnp.float32).reshape(RWKV_HEADS, RWKV_HEAD))
    bonus = jnp.sum(r_h * k_h * r_k.astype(jnp.float32), axis=-1, keepdims=True) * v_h
    y = (y + bonus).reshape(B, S, RWKV_DIM).astype(p_rwkv.dtype)
    return y * g

def peer_ffn(h, w_pq, sub_keys, expert_u, expert_v):
    B, S, D = h.shape
    hb_all = h.reshape(B * S // TOK_BLOCK, TOK_BLOCK, D)

    def block(hb):
        q = (hb @ w_pq).reshape(TOK_BLOCK, PEER_HEADS, 2, PEER_DHALF)
        s = jnp.einsum('thpd,hpnd->thpn', q, sub_keys).astype(jnp.float32)
        s1, i1 = lax.top_k(s[:, :, 0], PEER_TOPK)
        s2, i2 = lax.top_k(s[:, :, 1], PEER_TOPK)
        cand_s = (s1[..., :, None] + s2[..., None, :]).reshape(TOK_BLOCK, PEER_HEADS, PEER_TOPK * PEER_TOPK)
        cand_i = (i1[..., :, None] * N_KEYS + i2[..., None, :]).reshape(TOK_BLOCK, PEER_HEADS, PEER_TOPK * PEER_TOPK)
        top_s, pos = lax.top_k(cand_s, PEER_TOPK)
        idx = jnp.take_along_axis(cand_i, pos, axis=-1)
        gate = jax.nn.softmax(top_s, axis=-1).astype(hb.dtype)
        u = expert_u[idx]
        act = jax.nn.gelu(jnp.einsum('thkd,td->thk', u, hb), approximate=False)
        vv = expert_v[idx]
        return jnp.einsum('thk,thkd->td', gate * act, vv)

    out = lax.map(block, hb_all)
    return out.reshape(B, S, D)

def second_inputs(seed: int = 0) -> dict:
    key = jax.random.key(seed)
    ks = iter(jax.random.split(key, 40))
    f32 = jnp.float32
    nrm = lambda shape, scale: jax.random.normal(next(ks), shape, f32) * scale
    gain = lambda shape: 1.0 + 0.02 * jax.random.normal(next(ks), shape, f32)
    L = DEPTH
    x = jax.random.normal(next(ks), (BATCH, SEQ, D_MODEL), f32)
    offset = jax.random.randint(next(ks), (BATCH, 1), 0, 64, dtype=jnp.int32) * CHUNK
    positions = offset + jnp.arange(SEQ, dtype=jnp.int32)[None, :]
    return {
        'x': x,
        'positions': positions,
        'g_mix': gain((L, D_MODEL)),
        'w_in': nrm((L, D_MODEL, IN_COLS_2), D_MODEL ** -0.5),
        'rwkv_mu': jax.random.uniform(next(ks), (L, RWKV_COLS), f32),
        'g_cq': gain((L, MLA_Q_RANK)),
        'g_ckv': gain((L, MLA_KV_RANK)),
        'w_uq': nrm((L, MLA_Q_RANK, MLA_HEADS * MLA_QK), MLA_Q_RANK ** -0.5),
        'w_uk': nrm((L, MLA_KV_RANK, MLA_HEADS * MLA_NOPE), MLA_KV_RANK ** -0.5),
        'w_uv': nrm((L, MLA_KV_RANK, MLA_HEADS * MLA_V), MLA_KV_RANK ** -0.5),
        'g_qnorm': gain((L, MLA_QK)),
        'g_knorm': gain((L, MLA_QK)),
        'g_attn_out': gain((L, MLA_HEADS * MLA_V)),
        'w0': -6.0 + 5.0 * jax.random.uniform(next(ks), (L, RWKV_DIM), f32),
        'w2': nrm((L, W_LORA, RWKV_DIM), 0.1),
        'a0': nrm((L, RWKV_DIM), 0.1),
        'a2': nrm((L, A_LORA, RWKV_DIM), 0.1),
        'g2': nrm((L, G_LORA, RWKV_DIM), G_LORA ** -0.5),
        'k_k': 0.85 + nrm((L, RWKV_DIM), 0.05),
        'k_a': 1.0 + nrm((L, RWKV_DIM), 0.05),
        'r_k': nrm((L, RWKV_HEADS, RWKV_HEAD), 0.1),
        'ln_x_w': gain((L, RWKV_DIM)),
        'ln_x_b': nrm((L, RWKV_DIM), 0.02),
        'w_o': nrm((L, MIX_WIDTH_2, D_MODEL), MIX_WIDTH_2 ** -0.5),
        'g_ffn': gain((L, D_MODEL)),
        'w_pq': nrm((L, D_MODEL, PEER_HEADS * PEER_DQ), D_MODEL ** -0.5),
        'sub_keys': nrm((L, PEER_HEADS, 2, N_KEYS, PEER_DHALF), PEER_DHALF ** -0.5),
        'expert_u': nrm((L, N_EXPERTS, D_MODEL), D_MODEL ** -0.5),
        'expert_v': nrm((L, N_EXPERTS, D_MODEL), PEER_HEADS ** -0.5),
    }

def second_block(x, positions, g_mix, w_in, rwkv_mu, g_cq, g_ckv, w_uq, w_uk, w_uv, g_qnorm, g_knorm,
              g_attn_out, w0, w2, a0, a2, g2, k_k, k_a, r_k, ln_x_w, ln_x_b, w_o, g_ffn, w_pq,
              sub_keys, expert_u, expert_v):
    for l in range(DEPTH):
        h = rms_norm_2(x, g_mix[l])
        p = h @ w_in[l]
        y_a = mla_group(p[..., :MLA_COLS], positions, g_cq[l], g_ckv[l], w_uq[l], w_uk[l], w_uv[l],
                        g_qnorm[l], g_knorm[l], g_attn_out[l])
        y_b = rwkv7_group(p[..., MLA_COLS:], rwkv_mu[l], w0[l], w2[l], a0[l], a2[l], g2[l], k_k[l], k_a[l],
                          r_k[l], ln_x_w[l], ln_x_b[l])
        x = x + jnp.concatenate([y_a, y_b], axis=-1) @ w_o[l]
        x = x + peer_ffn(rms_norm_2(x, g_ffn[l]), w_pq[l], sub_keys[l], expert_u[l], expert_v[l])
    return x


def setup_inputs(seed=0):
    out = dict(first_inputs(seed))
    for name, value in second_inputs(seed + 1).items():
        if name != "x":
            out[name + "_2"] = value
    return out


def reference(
    x, mem, positions, g_mix, w_in, lambda_q1, lambda_k1, lambda_q2, lambda_k2, g_subln, w_out,
    g_cross, g_mem, w_xq, w_xkv, w_xo, g_mlp, w_up, w_down, g_final, positions_2, g_mix_2,
    w_in_2, rwkv_mu_2, g_cq_2, g_ckv_2, w_uq_2, w_uk_2, w_uv_2, g_qnorm_2, g_knorm_2,
    g_attn_out_2, w0_2, w2_2, a0_2, a2_2, g2_2, k_k_2, k_a_2, r_k_2, ln_x_w_2, ln_x_b_2, w_o_2,
    g_ffn_2, w_pq_2, sub_keys_2, expert_u_2, expert_v_2,
):
    x = first_block(
        x, mem, positions, g_mix, w_in, lambda_q1, lambda_k1, lambda_q2, lambda_k2, g_subln,
        w_out, g_cross, g_mem, w_xq, w_xkv, w_xo, g_mlp, w_up, w_down, g_final,
    )
    return second_block(
        x, positions_2, g_mix_2, w_in_2, rwkv_mu_2, g_cq_2, g_ckv_2, w_uq_2, w_uk_2, w_uv_2,
        g_qnorm_2, g_knorm_2, g_attn_out_2, w0_2, w2_2, a0_2, a2_2, g2_2, k_k_2, k_a_2, r_k_2,
        ln_x_w_2, ln_x_b_2, w_o_2, g_ffn_2, w_pq_2, sub_keys_2, expert_u_2, expert_v_2,
    )


_drawn_inputs = setup_inputs


def setup_inputs(seed=0):
    import zlib

    import numpy as np

    out = dict(_drawn_inputs(seed))
    spreads = {}
    factors = {'g_subln': 2.806,
     'g_cross': 7.766,
     'g_mem': 6.357,
     'g_cq_2': 5.359,
     'g_qnorm_2': 5.255,
     'g_knorm_2': 5.545,
     'g_attn_out_2': 24.994,
     'ln_x_w_2': 51.645,
     'ln_x_b_2': 55.638,
     'g_ffn_2': 18.121,
     'r_k_2': 3.914}
    for name, (base, spread) in spreads.items():
        noise = np.random.default_rng([zlib.crc32(name.encode()), seed]).standard_normal(out[name].shape)
        drawn = base * np.exp(spread * noise) if base else spread * noise
        out[name] = __import__('jax').numpy.asarray(drawn.astype(out[name].dtype))
    for name, factor in factors.items():
        out[name] = (out[name] * factor).astype(out[name].dtype)
    return out
```

```python
import math
from collections import deque
from contextlib import ExitStack

import numpy as np
import concourse.bass as bass
from concourse import mybir

F32 = mybir.dt.float32
I32 = mybir.dt.int32
U32 = mybir.dt.uint32
ALU = mybir.AluOpType
ACT = mybir.ActivationFunctionType
AX = mybir.AxisListType.X
NR = 8
NEG = -1e30


class Op:

    def __init__(self, eng):
        self.eng, self.sem, self.val, self.need, self.dma = eng, None, 0, False, False


class Queues:

    def __init__(self):
        self.last = {}
        self.q = {e: [] for e in ("pe", "dve", "act", "pool", "sp")}

    def add(self, eng, fn, *waits, dma=False):
        op = Op(eng)
        ws = []
        todo = list(waits)
        if eng in ("dve", "act", "pool") and eng in self.last:
            todo.append(self.last[eng])
        while todo:
            w = todo.pop()
            if w is None:
                continue
            if isinstance(w, (list, tuple)):
                todo += w
            else:
                w.need = True
                ws.append(w)
        self.q[eng].append((op, fn, ws))
        if not dma:
            self.last[eng] = op
        return op

    def dma(self, eng, out, in_, sem, val, *waits):
        op = self.add(eng, lambda e: e.dma_start(out, in_), *waits, dma=True)
        op.sem, op.val, op.dma = sem, val, True
        return op

    def number(self, sems):
        for eng, q in self.q.items():
            n = 0
            for op, _, _ in q:
                if op.need and not op.dma:
                    n += 1
                    op.sem, op.val = sems[eng], n

    def emit(self, eng, e):
        seen = {}
        for op, fn, ws in self.q[eng]:
            want = {}
            for w in ws:
                if eng == "pe" and w.eng == "pe":
                    continue
                k = id(w.sem)
                if want.get(k, (None, 0))[1] < w.val:
                    want[k] = (w.sem, w.val)
            for k, (s, v) in want.items():
                if seen.get(k, 0) < v:
                    e.wait_ge(s, v)
                    seen[k] = v
            ins = fn(e)
            if op.dma:
                ins.then_inc(op.sem, 16)
            elif op.need:
                ins.then_inc(op.sem, 1)


def bc(ap, axis, n):
    u = ap.unsqueeze(axis)
    shape = list(u.shape)
    shape[axis] = n
    return u.to_broadcast(shape)


def constants():
    p = np.arange(128)[:, None]
    f = np.arange(128)[None, :]
    one = lambda m: m.astype(np.float32)
    add = lambda m: np.where(m, 0.0, NEG).astype(np.float32)
    c = {"ident": one(p == f), "iota": np.broadcast_to(np.arange(128, dtype=np.float32), (128, 128)),
         "iota16": np.broadcast_to(np.arange(16, dtype=np.float32), (128, 16))}
    d = {}
    z = np.zeros((128, 128), np.float32)
    d["maskA"] = np.concatenate([z, add(f <= p)], 1)
    d["maskM"] = np.concatenate([z, add(f // 64 <= p // 64)], 1)
    d["maskS"] = one(p < f)
    d["negtri"] = -one(p >= f)
    d["negones"] = -np.ones((128, 128), np.float32)
    d["blk"] = one(p // 64 == f // 64)
    d["hsel"] = one(p // 64 == np.arange(2)[None, :])
    same = p // 64 == f // 64
    d["m2"] = np.concatenate([one(same & (p < f)), one(same & (p <= f))], 1)
    d["mt"] = one(same & (f < p))
    for l in range(6):
        m = 1 << l
        lev = (p // (2 * m) == f // (2 * m)) & (p // m % 2 == 1) & (f // m % 2 == 0)
        d[f"lx{l}"] = one(lev)
        d[f"ly{l}"] = one(lev.T)
    d["rst"] = np.broadcast_to(one(np.arange(256)[None, :] % 64 != 0), (128, 256))
    f1 = np.float32(500000.0) ** (-np.arange(0, 16, 2, dtype=np.float32) / np.float32(16))
    f2 = np.float32(10000.0) ** (-np.arange(16, dtype=np.float32) / np.float32(16))
    d["invf"] = np.broadcast_to(np.concatenate([f1, f2]).astype(np.float32), (128, 24))
    return c, d


def offsets(d):
    off, n = {}, 0
    for k, v in d.items():
        off[k] = (n, n + v.shape[1])
        n += v.shape[1]
    return off, n


def build(nc, T, poff, outs, stop=99):
    coff, ncc = offsets(constants()[0])
    doff, ncd = offsets(constants()[1])
    npar = max(b for _, b in poff.values())
    Q = Queues()
    ctx = ExitStack()
    with ctx:
        sems = {e: ctx.enter_context(nc.semaphore("s_" + e)) for e in Q.q}

        def sbuf(st, name, shape, dt=F32):
            return st.enter_context(nc.sbuf_tensor(name, shape, dt))

        def PE(fn, *w): return Q.add("pe", fn, *w)
        def V(fn, *w): return Q.add("dve", fn, *w)
        def A(fn, *w): return Q.add("act", fn, *w)
        def G(fn, *w): return Q.add("pool", fn, *w)

        nload = [0]

        def load(eng, out, in_, *w):
            nload[0] += 1
            return Q.dma(eng, out, in_, ctx.enter_context(nc.semaphore(f"ld{nload[0]}")), 16, *w)

        class Bank:
            pass
        banks = deque()
        for i in range(8):
            b = Bank()
            b.t = ctx.enter_context(nc.psum_tensor(f"ps{i}", [128, 512], F32))
            b.rel = []
            banks.append(b)

        def bank(): return banks.popleft()

        def free(b, *ops):
            b.rel = list(ops)
            banks.append(b)

        P = ctx
        ring = sbuf(P, "ring", [128, NR, 1024])
        rsem = [ctx.enter_context(nc.semaphore(f"ring{i}")) for i in range(NR)]
        nring = [0]
        rdone = {}

        def wnext(src, n=1024):
            i = nring[0]
            nring[0] += 1
            waits = [rdone[i - NR]] if i >= NR else []
            tk = Q.dma("sp", ring[:, i % NR, 0:n], src, rsem[i % NR], 16 * (i // NR + 1), *waits)
            return ring[:, i % NR, 0:n], tk, i

        cst = sbuf(P, "cst", [128, ncc])
        par = sbuf(P, "par", [128, npar])
        hA = sbuf(P, "hA", [128, 2, 1024])
        xT = sbuf(P, "xT", [128, 8, 256])
        stats = sbuf(P, "stats", [128, 96])
        neghalf = sbuf(P, "neghalf", [128, 1])
        S_AD = ctx.enter_context(ExitStack())
        dst = sbuf(S_AD, "dst", [128, ncd])
        rows = sbuf(S_AD, "rows", [128, 2496])
        hB = sbuf(S_AD, "hB", [128, 2, 1024])
        xn = sbuf(S_AD, "xn", [128, 2, 1024])
        junk = sbuf(S_AD, "junk", [128, 1024])
        pos = sbuf(S_AD, "pos", [128, 4], I32)

        def C(k): return cst[:, coff[k][0]:coff[k][1]]
        def D(k): return dst[:, doff[k][0]:doff[k][1]]
        def par_(k): return par[:, poff[k][0]:poff[k][1]]

        ident = C("ident")
        t_half = G(lambda e: e.memset(neghalf[:, :], -0.5))
        x_r = T["x"].rearrange("(t p) d -> p t d", p=128)
        t_x = load("act", hA[:, :, :], x_r)
        t_c = load("act", cst[:, :], T["cst"])
        t_par = load("act", par[:, :], T["par"])
        t_pos = load("act", pos[:, :], T["pos"])
        t_d = load("act", dst[:, :], T["dst"])
        t_rows = load("act", rows[:, :], T["rows"])
        nstat = [0]

        def stat():
            nstat[0] += 1
            return stats[:, nstat[0] - 1:nstat[0]]

        def mm(out, l, r, st, sp, *w):
            return PE(lambda e: e.matmul(out, l, r, start=st, stop=sp), *w)

        def tp(out, in_, *w):
            n = in_.shape[0]
            return PE(lambda e: e.transpose(out, in_, ident[0:n, 0:n]), t_c, *w)

        def vts(out, a, s1, s2, o0, o1, *w):
            return V(lambda e: e.tensor_scalar(out, a, s1, s2, o0, o1), *w)

        def vts1(out, a, s1, o0, *w):
            return V(lambda e: e.tensor_scalar(out, a, s1, None, o0), *w)

        def rsqrt(out, a, *w):
            h = neghalf[:, 0:1].to_broadcast(list(a.shape)) if len(a.shape) == 2 else bc(neghalf[:, 0:1], 1, a.shape[1]).to_broadcast(list(a.shape))
            return G(lambda e: e.tensor_tensor(out, a, h, ALU.pow), t_half, *w)

        def vtt(out, a, b, op, *w):
            return V(lambda e: e.tensor_tensor(out, a, b, op), *w)

        def vstt(out, a, s, b, o0, o1, *w):
            return V(lambda e: e.scalar_tensor_tensor(out, a, s, b, o0, o1), *w)

        def vcopy(out, a, *w):
            return V(lambda e: e.tensor_copy(out, a), *w)

        def vred(out, a, op, *w):
            return V(lambda e: e.tensor_reduce(out, a, AX, op), *w)

        def act(out, a, f, *w, scale=1.0, bias=0.0, acc=None):
            return A(lambda e: e.activation(out, a, f, bias=bias, scale=scale, accum_out=acc), *w)

        def acopy(out, a, *w):
            return A(lambda e: e.activation(out, a, ACT.Copy), *w)

        flip = [0]

        def copy(out, a, *w):
            flip[0] ^= 1
            return (vcopy if flip[0] else acopy)(out, a, *w)

        def rstd(src, n, w):
            s, s2 = stat(), stat()
            a = act(junk[:, 0:src.shape[1]], src, ACT.Square, w, acc=s)
            v = vts(s2, s, 1.0 / n, 1e-6, ALU.mult, ALU.add, a)
            return s2, rsqrt(s2, s2, v)

        def norm(src, out, w):
            r = []
            for tb in range(2):
                s, v = rstd(src[tb], src[tb].shape[1], w[tb])
                r.append(vts1(out[tb], src[tb], s, ALU.mult, v, w[tb]))
            return r

        def to_T(src, out, nk, g, w):
            toks = []
            for j in range(0, nk, 2):
                b = bank()
                n = min(2, nk - j)
                for k in range(n):
                    for tb in range(2):
                        last = tp(b.t[:, k * 256 + tb * 128:k * 256 + tb * 128 + 128],
                                  src[tb][:, (j + k) * 128:(j + k + 1) * 128], b.rel, w[tb])
                flip[0] ^= 1
                for k in range(n):
                    i, o = b.t[:, k * 256:(k + 1) * 256], out[:, j + k, :]
                    s = g[j + k] if g is not None else None
                    if flip[0]:
                        op = vcopy(o, i, last) if s is None else vts1(o, i, s, ALU.mult, last, t_par)
                    else:
                        op = acopy(o, i, last) if s is None else act(o, i, ACT.Copy, last, t_par, scale=s)
                    toks.append(op)
                free(b, op)
            return toks

        def gcols(k):
            return [par[:, c:c + 1] for c in range(*poff[k])]

        def proj512(inT, w, W, g):
            b = [bank(), bank()]
            for j in range(4):
                wt, tk, i = wnext(W[g * 4 + j])
                for k in range(2):
                    for tb in range(2):
                        last = mm(b[tb].t[:, :], inT[:, 2 * j + k, tb * 128:tb * 128 + 128],
                                  wt[:, k * 512:k * 512 + 512], j + k == 0, 2 * j + k == 7,
                                  tk, w[2 * j + k], b[tb].rel if j + k == 0 else None)
                rdone[i] = last
            return b, last

        def projT(inT, w, W, n, evac):
            for j in range(0, n, 2):
                b = bank()
                c = min(2, n - j)
                for q in range(c):
                    wt, tk, i = wnext(W[j + q])
                    for k in range(8):
                        last = mm(b.t[:, q * 256:q * 256 + 256], wt[:, k * 128:k * 128 + 128], inT[:, k, :],
                                  k == 0, k == 7, tk, w[k], b.rel)
                    rdone[i] = last
                free(b, evac(b, j, c, last))

        def residual(out, base, inT, w, W, wb):
            r = [[], []]
            for g in range(2):
                b, last = proj512(inT, w, W, g)
                for tb in range(2):
                    op = vtt(out[:, tb, g * 512:g * 512 + 512], b[tb].t[:, :],
                             base[:, tb, g * 512:g * 512 + 512], ALU.add, last, wb)
                    free(b[tb], op)
                    r[tb].append(op)
            return r

        def softmax(S, n, w, M, L):
            k = S.shape[2]
            v = vred(M, S, ALU.max, w)
            v = vtt(S, S, bc(M, 2, k), ALU.subtract, v)
            a = act(S, S, ACT.Exp, v)
            return a, vred(L, S, ALU.add, a)

        trig = sbuf(S_AD, "trig", [128, 2, 2, 24])
        ang = sbuf(S_AD, "ang", [128, 2, 2, 24])
        kq = sbuf(S_AD, "kq", [128, 2, 2, 24])
        posf = sbuf(S_AD, "posf", [128, 4])
        v = vcopy(posf[:, :], pos[:, :], t_pos)
        last = None
        for tr in range(2):
            for tb in range(2):
                for bl, lo, hi in ((0, 0, 8), (1, 8, 24)):
                    last = vts1(ang[:, tr, tb, lo:hi], D("invf")[:, lo:hi], posf[:, 2 * bl + tb:2 * bl + tb + 1],
                                ALU.mult, v, t_d)
        v = last
        two_pi = 2 * math.pi
        C1 = 6.28125
        C2 = float(np.float32(round((two_pi - C1) * 2 ** 20) / 2 ** 20))
        C3 = float(np.float32(two_pi - C1 - C2))
        MAGIC = 12582912.0
        vs_ = []
        for tr in range(2):
            vs_.append(vts(kq[:, tr, :, :], ang[:, tr, :, :], 1.0 / two_pi, 0.25 * tr, ALU.mult, ALU.add, v))
        v = vts1(kq[:, :, :, :], kq[:, :, :, :], MAGIC, ALU.add, vs_)
        v = vts1(kq[:, :, :, :], kq[:, :, :, :], MAGIC, ALU.subtract, v)
        fl = lambda t: t[:, :, :, :].rearrange("p a b c -> p (a b c)")
        for cc in (C1, C2, C3):
            v = vstt(fl(ang), fl(kq), -cc, fl(ang), ALU.mult, ALU.add, v)
        v = vts1(ang[:, 1, :, :], ang[:, 1, :, :], math.pi / 2, ALU.add, v)
        v = vts(fl(ang), fl(ang), 3.1415925, -3.1415925, ALU.min, ALU.max, v)
        t_trig = act(fl(trig), fl(ang), ACT.Sin, v)

        def rope(x1, x2, cos, sin, tmp, w):
            n = x1.shape[1]
            c, s = bc(cos, 1, n), bc(sin, 1, n)
            a = vtt(tmp[0], x1, c, ALU.mult, w, t_trig)
            a = vtt(tmp[1], x2, s, ALU.mult, w)
            b = vtt(tmp[2], x2, c, ALU.mult, w)
            b = vtt(tmp[3], x1, s, ALU.mult, w)
            a = vtt(x1, tmp[0], tmp[1], ALU.subtract, a, b)
            return vtt(x2, tmp[2], tmp[3], ALU.add, b)

        lam = sbuf(S_AD, "lam", [128, 8])
        lj = sbuf(S_AD, "lj", [128, 128])
        rl = lambda i: rows[:, 2240 + 64 * i:2304 + 64 * i]
        v1 = vtt(lj[:, 0:64], rl(0), rl(1), ALU.mult, t_rows)
        v2 = vtt(lj[:, 64:128], rl(2), rl(3), ALU.mult, t_rows)
        v = vred(lam[:, 0:2], lj[:, :].rearrange("p (a b) -> p a b", a=2), ALU.add, v1, v2)
        a = act(lam[:, 2:4], lam[:, 0:2], ACT.Exp, v)
        v = vtt(lam[:, 4:5], lam[:, 3:4], lam[:, 2:3], ALU.subtract, a)
        t_lam = vts1(lam[:, 5:6], lam[:, 4:5], -(0.8 - 0.6 * math.exp(0.0)), ALU.add, v)
        nlam = lam[:, 5:6]

        tbs = lambda t: [t[:, tb, :] for tb in range(2)]
        S = ctx.enter_context(ExitStack())
        qk = sbuf(S, "qk", [128, 2, 1024])
        qkT = sbuf(S, "qkT", [128, 8, 256])
        va = sbuf(S, "va", [128, 2, 512])
        vs = sbuf(S, "vs", [128, 2, 512])
        sT = sbuf(S, "sT", [128, 8, 256])
        rt = sbuf(S, "rt", [128, 4, 16, 16])
        yT = sbuf(S, "yT", [128, 8, 256])
        S2 = ctx.enter_context(ExitStack())
        P1 = sbuf(S2, "P1", [128, 8, 256])
        P0 = sbuf(S2, "P0", [128, 8, 128])
        W1T = sbuf(S2, "W1T", [128, 8, 128])
        W0T = sbuf(S2, "W0T", [128, 4, 128])
        zs = sbuf(S2, "zs", [128, 3072])
        ez = sbuf(S2, "ez", [128, 3072])
        mlr = sbuf(S2, "mlr", [128, 2, 3, 8])
        od = sbuf(S2, "od", [128, 2, 512])
        osq = sbuf(S2, "osq", [128, 2, 512])
        ost = sbuf(S2, "ost", [128, 2, 8])

        n_x = norm(tbs(hA), tbs(xn), [t_x, t_x])
        w_xT = to_T(tbs(xn), xT, 8, gcols("g_mix"), n_x)
        t_qk = [[], []]
        for g in range(2):
            b, last = proj512(xT, w_xT, T["w_in_a"], g)
            for tb in range(2):
                op = copy(qk[:, tb, g * 512:g * 512 + 512], b[tb].t[:, :], last)
                free(b[tb], op)
                t_qk[tb].append(op)
        t_v = {}
        for g, dstt, nm in ((2, va, "va"), (3, vs, "vs")):
            b, last = proj512(xT, w_xT, T["w_in_a"], g)
            t_v[nm] = []
            for tb in range(2):
                op = copy(dstt[:, tb, :], b[tb].t[:, :], last)
                free(b[tb], op)
                t_v[nm].append(op)
        t_sT = [None] * 8

        def ev_sT(b, j, c, last):
            op = copy(sT[:, j:j + c, :], b.t[:, 0:c * 256].rearrange("p (a b) -> p a b", a=c), last)
            for q in range(c):
                t_sT[j + q] = op
            return op
        projT(xT, w_xT, T["w_in_t"], 8, ev_sT)
        t_rope = []
        for tb in range(2):
            xv = qk[:, tb, :].rearrange("p (n d) -> p n d", d=64)
            t_rope.append(rope(xv[:, :, 0:8], xv[:, :, 8:16], trig[:, 1, tb, 0:8], trig[:, 0, tb, 0:8],
                               [rt[:, i, :, 0:8] for i in range(4)], t_qk[tb]))
        t_qkT = to_T(tbs(qk), qkT, 8, None, t_rope)

        def seg(kb, r):
            return slice(r * 1024, r * 1024 + 1024) if kb == 0 else slice(2048 + r * 512, 2560 + r * 512)
        t_z = []
        for r in range(2):
            for hp in range(2):
                b = bank()
                for q in range(2):
                    i = hp * 2 + q
                    last = mm(b.t[:, q * 256:q * 256 + 256], sT[64 * r:64 * r + 64, 4 + i, 0:128],
                              sT[64 * r:64 * r + 64, i, :], True, True, b.rel, t_sT[i], t_sT[4 + i])
                op = vts1(zs[:, r * 1024 + hp * 512:r * 1024 + hp * 512 + 512], b.t[:, :], 0.125, ALU.mult, last)
                free(b, op)
                t_z.append(op)
            b = bank()
            for i in range(4):
                last = mm(b.t[:, i * 128:i * 128 + 128], sT[64 * r:64 * r + 64, 4 + i, 128:256],
                          sT[64 * r:64 * r + 64, i, 128:256], True, True, b.rel)
            op = vts1(zs[:, seg(1, r)], b.t[:, :], 0.125, ALU.mult, last)
            free(b, op)
            t_z.append(op)
        a = act(ez[:, :], zs[:, :], ACT.Abs, t_z)
        a = act(ez[:, :], ez[:, :], ACT.Exp, a, scale=-1.0)
        a = act(ez[:, :], ez[:, :], ACT.Ln, a, bias=1.0)
        v = vstt(ez[:, :], zs[:, :], 0.0, ez[:, :], ALU.max, ALU.add, a)

        def diag(t, kb):
            if kb == 0:
                return t[:, 0:2048].rearrange("p (h q) -> p h q", q=256)[:, :, 0:128]
            return t[:, 2048:3072].rearrange("p (h q) -> p h q", q=128)
        t_sp = [vtt(diag(ez, kb), diag(ez, kb), bc(D("maskS"), 1, 8), ALU.mult, v, t_d) for kb in range(2)]
        t_e = []
        for r in range(2):
            for hp in range(2):
                b = bank()
                o = r * 1024 + hp * 512
                mm(b.t[:, :], D("negtri"), ez[:, o:o + 512], True, False, b.rel, t_sp)
                o1 = 2048 + r * 512 + hp * 256
                last = mm(b.t[:, :].rearrange("p (h q) -> p h q", q=256)[:, :, 128:256], D("negones"),
                          ez[:, o1:o1 + 256].rearrange("p (h q) -> p h q", q=128), False, True)
                op = vtt(zs[:, o:o + 512], b.t[:, :], zs[:, o:o + 512], ALU.add, last)
                free(b, op)
                t_e.append(op)
            b = bank()
            last = mm(b.t[:, :], D("negtri"), ez[:, seg(1, r)], True, True, b.rel)
            op = vtt(zs[:, seg(1, r)], b.t[:, :], zs[:, seg(1, r)], ALU.add, last)
            free(b, op)
            t_e.append(op)
        a = act(zs[:, :], zs[:, :], ACT.Exp, t_e)
        t_a = [vtt(diag(zs, kb), diag(zs, kb), bc(D("maskS"), 1, 8), ALU.mult, a) for kb in range(2)]
        t_yT = [None] * 8
        for hp in range(2):
            b = bank()
            for q in range(2):
                i = hp * 2 + q
                for r in range(2):
                    h = 2 * i + r
                    o = b.t[64 * r:64 * r + 64, q * 256:q * 256 + 256]
                    mm(o, vs[:, 0, h * 64:h * 64 + 64], zs[:, r * 1024 + i * 256:r * 1024 + i * 256 + 256],
                       True, False, b.rel, t_a, t_v["vs"])
                    o1 = 2048 + r * 512 + i * 128
                    last = mm(o[:, 128:256], vs[:, 1, h * 64:h * 64 + 64], zs[:, o1:o1 + 128], False, True)
            op = copy(yT[:, 4 + hp * 2:6 + hp * 2, :], b.t[:, :].rearrange("p (a b) -> p a b", a=2), last)
            free(b, op)
            t_yT[4 + hp * 2] = t_yT[5 + hp * 2] = op

        t_s1, t_s0 = [], []
        for c in range(2):
            rs = slice(64 * c, 64 * c + 64)
            for hp in range(2):
                b = bank()
                for q in range(2):
                    h = hp * 2 + q
                    last = mm(b.t[:, q * 256:q * 256 + 256], qkT[rs, h, 128:256], qkT[rs, 4 + h, :], True, True,
                              b.rel, t_qkT[h], t_qkT[4 + h])
                op = vstt(P1[:, c * 4 + hp * 2:c * 4 + hp * 2 + 2, :], b.t[:, :].rearrange("p (a b) -> p a b", a=2),
                          0.125, bc(D("maskA"), 1, 2), ALU.mult, ALU.add, last, t_d)
                free(b, op)
                t_s1.append(op)
            b = bank()
            for h in range(4):
                last = mm(b.t[:, h * 128:h * 128 + 128], qkT[rs, h, 0:128], qkT[rs, 4 + h, 0:128], True, True, b.rel)
            op = vstt(P0[:, c * 4:c * 4 + 4, :], b.t[:, :].rearrange("p (a b) -> p a b", a=4),
                      0.125, bc(D("maskA")[:, 128:256], 1, 4), ALU.mult, ALU.add, last)
            free(b, op)
            t_s0.append(op)
        t_w = []
        for qb, Pq, w in ((0, P0, t_s0), (1, P1, t_s1)):
            k = Pq.shape[2]
            a, v = softmax(Pq[:, :, :], 8, w, mlr[:, qb, 0, :], mlr[:, qb, 1, :])
            v = V(lambda e, qb=qb: e.reciprocal(mlr[:, qb, 2, :], mlr[:, qb, 1, :]), v)
            v = vts1(mlr[:, qb, 2, 4:8], mlr[:, qb, 2, 4:8], nlam, ALU.mult, v, t_lam)
            v = vtt(Pq[:, :, :], Pq[:, :, :], bc(mlr[:, qb, 2, :], 2, k), ALU.mult, v)
            t_w.append(vtt(Pq[:, 0:4, :], Pq[:, 0:4, :], Pq[:, 4:8, :], ALU.add, v))
        t_wT = []
        for j in range(2):
            b = bank()
            for q in range(4):
                i = j * 4 + q
                last = tp(b.t[:, q * 128:q * 128 + 128], P1[:, i // 2, (i % 2) * 128:(i % 2) * 128 + 128], b.rel, t_w[1])
            op = copy(W1T[:, j * 4:j * 4 + 4, :], b.t[:, :].rearrange("p (a b) -> p a b", a=4), last)
            free(b, op)
            t_wT.append(op)
        b = bank()
        for h in range(4):
            last = tp(b.t[:, h * 128:h * 128 + 128], P0[:, h, :], b.rel, t_w[0])
        op = copy(W0T[:, :, :], b.t[:, :].rearrange("p (a b) -> p a b", a=4), last)
        free(b, op)
        t_w0 = op
        t_on = []
        for qb in range(2):
            b = bank()
            for h in range(4):
                hs = slice(h * 128, h * 128 + 128)
                if qb == 0:
                    last = mm(b.t[:, hs], W0T[:, h, :], va[:, 0, hs], True, True, b.rel, t_w0, t_v["va"])
                else:
                    mm(b.t[:, hs], W1T[:, h * 2, :], va[:, 0, hs], True, False, b.rel, t_wT, t_v["va"])
                    last = mm(b.t[:, hs], W1T[:, h * 2 + 1, :], va[:, 1, hs], False, True)
            v = vcopy(od[:, qb, :], b.t[:, :], last)
            free(b, v)
            v4 = lambda t: t[:, qb, :].rearrange("p (a b) -> p a b", a=4)
            q = vtt(osq[:, qb, :], od[:, qb, :], od[:, qb, :], ALU.mult, v)
            q = vred(ost[:, qb, 0:4], v4(osq), ALU.add, q)
            q = vts(ost[:, qb, 4:8], ost[:, qb, 0:4], 1.0 / 128, 1e-6, ALU.mult, ALU.add, q)
            q = rsqrt(ost[:, qb, 4:8], ost[:, qb, 4:8], q)
            q = vts1(ost[:, qb, 4:8], ost[:, qb, 4:8], 1.0 - (0.8 - 0.6 * math.exp(0.0)), ALU.mult, q)
            t_on.append(vtt(v4(od), v4(od), bc(ost[:, qb, 4:8], 2, 128), ALU.mult, q))
        t_yT[0:4] = to_T(tbs(od), yT, 4, gcols("g_subln") * 4, t_on)
        t_h1 = residual(hB, hA, yT, t_yT, T["w_out"], t_x)
        S2.close()
        if stop == 1:
            return finish(nc, Q, sems, ctx, outs, hB, t_h1, load)

        SB = ctx.enter_context(ExitStack())
        kmT = sbuf(SB, "kmT", [128, 8, 256])
        vm = sbuf(SB, "vm", [128, 2, 1024])
        mem = sbuf(SB, "mem", [128, 2, 1024])
        memn = sbuf(SB, "memn", [128, 2, 1024])
        memT = sbuf(SB, "memT", [128, 8, 256])
        PX = sbuf(SB, "PX", [128, 2, 4, 256])
        PXT = sbuf(SB, "PXT", [128, 2, 4, 256])
        mx = sbuf(SB, "mx", [128, 2, 3, 4])
        t_mem = load("act", mem[:, :, :], T["mem"].rearrange("(t p) d -> p t d", p=128), t_h1)
        n_m = norm(tbs(mem), tbs(memn), [t_mem, t_mem])
        w_mT = to_T(tbs(memn), memT, 8, gcols("g_mem"), n_m)
        t_kmT = [None] * 8

        def ev_km(b, j, c, last):
            op = copy(kmT[:, j:j + c, :], b.t[:, :].rearrange("p (a b) -> p a b", a=2), last)
            t_kmT[j] = t_kmT[j + 1] = op
            return op
        projT(memT, w_mT, T["w_xk"], 8, ev_km)
        t_vm = []
        for g in range(2):
            b, last = proj512(memT, w_mT, T["w_xv"], g)
            for tb in range(2):
                op = copy(vm[:, tb, g * 512:g * 512 + 512], b[tb].t[:, :], last)
                free(b[tb], op)
                t_vm.append(op)
        n_h = norm(tbs(hB), tbs(xn), t_h1)
        w_xT = to_T(tbs(xn), xT, 8, gcols("g_cross"), n_h)
        t_sT = [None] * 8
        projT(xT, w_xT, T["w_xq"], 8, ev_sT)
        t_pT = []
        t_p = []
        for tb in range(2):
            ts = slice(tb * 128, tb * 128 + 128)
            sc = []
            for hp in range(2):
                b = bank()
                for q in range(2):
                    h = hp * 2 + q
                    for k in range(2):
                        last = mm(b.t[:, q * 256:q * 256 + 256], sT[:, 2 * h + k, ts], kmT[:, 2 * h + k, :], k == 0, k == 1,
                                  b.rel, t_sT, t_kmT)
                op = vts1(PX[:, tb, hp * 2:hp * 2 + 2, :], b.t[:, :].rearrange("p (a b) -> p a b", a=2), 1.0 / 16, ALU.mult, last)
                free(b, op)
                sc.append(op)
            a, v = softmax(PX[:, tb, :, :], 4, sc, mx[:, tb, 0, :], mx[:, tb, 1, :])
            v = V(lambda e, tb=tb: e.reciprocal(mx[:, tb, 2, :], mx[:, tb, 1, :]), v)
            t_p.append(vtt(PX[:, tb, :, :], PX[:, tb, :, :], bc(mx[:, tb, 2, :], 2, 256), ALU.mult, v))
        for tb in range(2):
            for kb in range(2):
                b = bank()
                for h in range(4):
                    last = tp(b.t[:, h * 128:h * 128 + 128], PX[:, tb, h, kb * 128:kb * 128 + 128], b.rel, t_p[tb])
                op = copy(PXT[:, kb, :, tb * 128:tb * 128 + 128], b.t[:, :].rearrange("p (a b) -> p a b", a=4), last)
                free(b, op)
                t_pT.append(op)
        t_oT = []
        for j in range(4):
            b = bank()
            for q in range(2):
                n = 2 * j + q
                for kb in range(2):
                    last = mm(b.t[:, q * 256:q * 256 + 256], vm[:, kb, n * 128:n * 128 + 128], PXT[:, kb, j, :], kb == 0, kb == 1,
                              b.rel, t_vm, t_pT)
            op = copy(yT[:, 2 * j:2 * j + 2, :], b.t[:, :].rearrange("p (a b) -> p a b", a=2), last)
            free(b, op)
            t_oT += [op, op]
        t_h2 = residual(hA, hB, yT, t_oT, T["w_xo"], t_h1)
        SB.close()
        S.close()
        if stop == 2:
            return finish(nc, Q, sems, ctx, outs, hA, t_h2, load)

        SC = ctx.enter_context(ExitStack())
        aT = sbuf(SC, "aT", [128, 32, 256])
        n_h = norm(tbs(hA), tbs(xn), t_h2)
        w_xT = to_T(tbs(xn), xT, 8, gcols("g_mlp"), n_h)
        t_aT = [None] * 32

        def ev_up(b, j, c, last):
            o = aT[:, j:j + 2, :]
            a = act(o, b.t[:, :].rearrange("p (a b) -> p a b", a=2), ACT.Relu, last)
            t_aT[j] = t_aT[j + 1] = vtt(o, o, o, ALU.mult, a)
            return a
        projT(xT, w_xT, T["w_up"], 32, ev_up)
        bb = [bank() for _ in range(4)]
        for k in range(32):
            wt, tk, i = wnext(T["w_down"][k])
            for tb in range(2):
                for g in range(2):
                    b = bb[tb * 2 + g]
                    last = mm(b.t[:, :], aT[:, k, tb * 128:tb * 128 + 128], wt[:, g * 512:g * 512 + 512], k == 0, k == 31,
                              b.rel, tk, t_aT[k])
            rdone[i] = last
        t_h3 = [[], []]
        for tb in range(2):
            for g in range(2):
                gs = slice(g * 512, g * 512 + 512)
                op = vtt(hB[:, tb, gs], bb[tb * 2 + g].t[:, :], hA[:, tb, gs], ALU.add, last)
                free(bb[tb * 2 + g], op)
                t_h3[tb].append(op)
        t_x2 = []
        for tb in range(2):
            s, v = rstd(hB[:, tb, :], 1024, t_h3[tb])
            t_x2.append(vstt(hA[:, tb, :], hB[:, tb, :], s, rows[:, 0:1024], ALU.mult, ALU.mult, v, t_rows))
        SC.close()
        if stop == 3:
            return finish(nc, Q, sems, ctx, outs, hA, t_x2, load)

        SD = ctx.enter_context(ExitStack())
        n_h = norm(tbs(hA), tbs(xn), t_x2)
        w_xT = to_T(tbs(xn), xT, 8, gcols("g_mix_2"), n_h)
        ytok = sbuf(SD, "ytok", [128, 2, 1024])
        yT2 = sbuf(SD, "yT2", [128, 8, 256])
        SM = ctx.enter_context(ExitStack())
        cq = sbuf(SM, "cq", [128, 2, 672])
        cn = sbuf(SM, "cn", [128, 2, 640])
        cT = sbuf(SM, "cT", [128, 5, 256])
        QK = sbuf(SM, "QK", [128, 2, 2, 8, 96])
        QKs = sbuf(SM, "QKs", [128, 2, 2, 8, 96])
        qst = sbuf(SM, "qst", [128, 2, 2, 16])
        vM = sbuf(SM, "vM", [128, 2, 512])
        qT2 = sbuf(SM, "qT2", [96, 2, 8, 256])
        rt2 = sbuf(SM, "rt2", [128, 4, 16, 16])
        M1 = sbuf(SM, "M1", [128, 8, 256])
        M0 = sbuf(SM, "M0", [128, 8, 128])
        MT1 = sbuf(SM, "MT1", [128, 8, 2, 128])
        MT0 = sbuf(SM, "MT0", [128, 8, 128])
        mst = sbuf(SM, "mst", [128, 2, 3, 8])

        bq = [bank() for _ in range(4)]
        for k in range(8):
            wt, tk, i = wnext(T["w_mla"][k], 672)
            for tb in range(2):
                xs = xT[:, k, tb * 128:tb * 128 + 128]
                mm(bq[tb].t[:, 0:384], xs, wt[:, 0:384], k == 0, k == 7, bq[tb].rel, tk, w_xT[k])
                last = mm(bq[2 + tb].t[:, 0:288], xs, wt[:, 384:672], k == 0, k == 7, bq[2 + tb].rel)
            rdone[i] = last
        t_cq = [[], []]
        for tb in range(2):
            for j, lo, hi in ((0, 0, 384), (1, 384, 672)):
                b = bq[2 * j + tb]
                op = copy(cq[:, tb, lo:hi], b.t[:, 0:hi - lo], last)
                free(b, op)
                t_cq[tb].append(op)
        n_q = norm([cq[:, tb, 0:384] for tb in range(2)], [cn[:, tb, 0:384] for tb in range(2)], t_cq)
        n_kv = norm([cq[:, tb, 384:640] for tb in range(2)], [cn[:, tb, 384:640] for tb in range(2)], t_cq)
        w_cT = to_T(tbs(cn), cT, 5, gcols("g_cq") + gcols("g_ckv"), [[n_q[tb], n_kv[tb]] for tb in range(2)])
        bq = [bank() for _ in range(4)]
        for k in range(3):
            wt, tk, i = wnext(T["w_uq"][k], 768)
            for tb in range(2):
                xs = cT[:, k, tb * 128:tb * 128 + 128]
                mm(bq[tb].t[:, 0:480], xs, wt[:, 0:480], k == 0, k == 2, bq[tb].rel, tk, w_cT[k])
                last = mm(bq[2 + tb].t[:, 0:288], xs, wt[:, 480:768], k == 0, k == 2, bq[2 + tb].rel)
            rdone[i] = last
        t_q = [[], []]
        for tb in range(2):
            for j, lo, hi in ((0, 0, 5), (1, 5, 8)):
                b = bq[2 * j + tb]
                op = copy(QK[:, tb, 0, lo:hi, :], b.t[:, 0:(hi - lo) * 96].rearrange("p (a b) -> p a b", b=96), last)
                free(b, op)
                t_q[tb].append(op)
        bq = [bank() for _ in range(4)]
        for k in range(2):
            wt, tk, i = wnext(T["w_ukv"][k])
            for tb in range(2):
                xs = cT[:, 3 + k, tb * 128:tb * 128 + 128]
                mm(bq[tb].t[:, :], xs, wt[:, 0:512], k == 0, k == 1, bq[tb].rel, tk, w_cT[3 + k])
                last = mm(bq[2 + tb].t[:, :], xs, wt[:, 512:1024], k == 0, k == 1, bq[2 + tb].rel)
            rdone[i] = last
        t_vM = []
        for tb in range(2):
            op = copy(QK[:, tb, 1, :, 0:64], bq[tb].t[:, :].rearrange("p (a b) -> p a b", b=64), last)
            free(bq[tb], op)
            t_q[tb].append(op)
            op = copy(vM[:, tb, :], bq[2 + tb].t[:, :], last)
            free(bq[2 + tb], op)
            t_vM.append(op)
            t_q[tb].append(G(lambda e, tb=tb: e.tensor_copy(QK[:, tb, 1, :, 64:96], bc(cq[:, tb, 640:672], 1, 8)), t_cq[tb]))
        t_qT = []
        for tb in range(2):
            h16 = lambda t: t[:, tb, :, :, :].rearrange("p a b c -> p (a b) c")
            v = vtt(h16(QKs), h16(QK), h16(QK), ALU.mult, t_q[tb])
            v = vred(qst[:, tb, 0, :], h16(QKs), ALU.add, v)
            v = vts(qst[:, tb, 1, :], qst[:, tb, 0, :], 1.0 / 96, 1e-6, ALU.mult, ALU.add, v)
            v = rsqrt(qst[:, tb, 1, :], qst[:, tb, 1, :], v)
            v = vtt(h16(QK), h16(QK), bc(qst[:, tb, 1, :], 2, 96), ALU.mult, v)
            v = [vtt(QK[:, tb, j, :, :], QK[:, tb, j, :, :], bc(rows[:, 2048 + 96 * j:2144 + 96 * j], 1, 8), ALU.mult, v, t_rows)
                 for j in range(2)]
            v = rope(h16(QK)[:, :, 64:80], h16(QK)[:, :, 80:96], trig[:, 1, tb, 8:24], trig[:, 0, tb, 8:24],
                     [rt2[:, i, :, :] for i in range(4)], v)
            for j in range(2):
                for hp in range(2):
                    b = bank()
                    for q in range(4):
                        last = tp(b.t[0:96, q * 128:q * 128 + 128], QK[:, tb, j, hp * 4 + q, :], b.rel, v)
                    op = copy(qT2[:, j, hp * 4:hp * 4 + 4, tb * 128:tb * 128 + 128],
                              b.t[0:96, :].rearrange("p (a b) -> p a b", a=4), last)
                    free(b, op)
                    t_qT.append(op)
        isq = 96 ** -0.5
        t_m1, t_m0 = [], []
        for hp in range(4):
            b = bank()
            for q in range(2):
                h = hp * 2 + q
                last = mm(b.t[:, q * 256:q * 256 + 256], qT2[:, 0, h, 128:256], qT2[:, 1, h, :], True, True, b.rel, t_qT)
            op = vstt(M1[:, hp * 2:hp * 2 + 2, :], b.t[:, :].rearrange("p (a b) -> p a b", a=2), isq,
                      bc(D("maskM"), 1, 2), ALU.mult, ALU.add, last)
            free(b, op)
            t_m1.append(op)
        for hp in range(2):
            b = bank()
            for q in range(4):
                h = hp * 4 + q
                last = mm(b.t[:, q * 128:q * 128 + 128], qT2[:, 0, h, 0:128], qT2[:, 1, h, 0:128], True, True, b.rel, t_qT)
            op = vstt(M0[:, hp * 4:hp * 4 + 4, :], b.t[:, :].rearrange("p (a b) -> p a b", a=4), isq,
                      bc(D("maskM")[:, 128:256], 1, 4), ALU.mult, ALU.add, last)
            free(b, op)
            t_m0.append(op)
        t_sm, t_l = [], []
        for qb, Mq, w in ((0, M0, t_m0), (1, M1, t_m1)):
            a, v = softmax(Mq[:, :, :], 8, w, mst[:, qb, 0, :], mst[:, qb, 1, :])
            t_sm.append(a)
            t_l.append(V(lambda e, qb=qb: e.reciprocal(mst[:, qb, 2, :], mst[:, qb, 1, :]), v))
        t_mT = [[], []]
        for j in range(2):
            b = bank()
            for q in range(4):
                last = tp(b.t[:, q * 128:q * 128 + 128], M0[:, j * 4 + q, :], b.rel, t_sm[0])
            op = copy(MT0[:, j * 4:j * 4 + 4, :], b.t[:, :].rearrange("p (a b) -> p a b", a=4), last)
            free(b, op)
            t_mT[0].append(op)
        for j in range(4):
            b = bank()
            for q in range(4):
                h, kb = j * 2 + q // 2, q % 2
                last = tp(b.t[:, q * 128:q * 128 + 128], M1[:, h, kb * 128:kb * 128 + 128], b.rel, t_sm[1])
            op = copy(MT1[:, j * 2:j * 2 + 2, :, :], b.t[:, :].rearrange("p (a k b) -> p a k b", a=2, k=2), last)
            free(b, op)
            t_mT[1].append(op)
        t_ya = []
        for qb in range(2):
            b = bank()
            for h in range(8):
                hs = slice(h * 64, h * 64 + 64)
                if qb == 0:
                    last = mm(b.t[:, hs], MT0[:, h, :], vM[:, 0, hs], True, True, b.rel, t_mT[0], t_vM)
                else:
                    mm(b.t[:, hs], MT1[:, h, 0, :], vM[:, 0, hs], True, False, b.rel, t_mT[1], t_vM)
                    last = mm(b.t[:, hs], MT1[:, h, 1, :], vM[:, 1, hs], False, True)
            o = ytok[:, qb, 0:512].rearrange("p (a b) -> p a b", a=8)
            v = vtt(o, b.t[:, :].rearrange("p (a b) -> p a b", a=8), bc(mst[:, qb, 2, :], 2, 64), ALU.mult, last, t_l)
            free(b, v)
            js = junk[:, qb * 512:qb * 512 + 512].rearrange("p (a b) -> p a b", a=8)
            q = vtt(js, o, o, ALU.mult, v, n_kv)
            q = vred(mst[:, qb, 0, :], js, ALU.add, q)
            q = vts(mst[:, qb, 1, :], mst[:, qb, 0, :], 1.0 / 64, 1e-6, ALU.mult, ALU.add, q)
            q = rsqrt(mst[:, qb, 1, :], mst[:, qb, 1, :], q)
            t_ya.append(vtt(o, o, bc(mst[:, qb, 1, :], 2, 64), ALU.mult, q))
        t_yT = [None] * 8
        t_yT[0:4] = to_T([ytok[:, tb, 0:512] for tb in range(2)], yT2, 4, gcols("g_attn_out"), t_ya)
        SM.close()
        if stop == 4:
            return finish(nc, Q, sems, ctx, outs, ytok, [t_ya, t_yT], load)

        SR = ctx.enter_context(ExitStack())
        pR = sbuf(SR, "pR", [128, 14, 257])
        pm = sbuf(SR, "pm", [128, 14, 256])
        sg = sbuf(SR, "sg", [128, 256])
        prep = sbuf(SR, "prep", [128, 5, 4, 256])
        ld, aa, cum, t0, t1 = (prep[:, i, :, :] for i in range(5))
        Pc = sbuf(SR, "Pc", [128, 4, 256])
        ARt = sbuf(SR, "ARt", [128, 4, 2, 256])
        be = sbuf(SR, "be", [128, 4, 256])
        ka = sbuf(SR, "ka", [128, 4, 256])
        atok = sbuf(SR, "atok", [128, 2, 512])
        btok = sbuf(SR, "btok", [128, 2, 512])
        ktok = sbuf(SR, "ktok", [128, 2, 512])
        vtok = ytok[:, :, 0:512]
        gtok = rows[:, 0:1024].rearrange("p (t n) -> p t n", t=2)
        bon = sbuf(SR, "bon", [128, 16])
        t_mz = V(lambda e: e.memset(pR[:, :, 0:1], 0.0), t_yT[0:4], t_ya)
        t_pR = []

        def ev_p(b, j, c, last):
            op = copy(pR[:, j:j + c, 1:257], b.t[:, :].rearrange("p (a b) -> p a b", a=2), last, t_yT[0:4], t_ya)
            t_pR.append(op)
            return op
        projT(xT, w_xT, T["w_rwkv"], 14, ev_p)
        mu = gcols("rwkv_mu")
        v = vtt(pm[:, :, :], pR[:, :, 0:256], pR[:, :, 1:257], ALU.subtract, t_pR, t_mz)
        t_pm = [vstt(pm[:, i, :], pm[:, i, :], mu[i], pR[:, i, 1:257], ALU.mult, ALU.add, v) for i in range(14)]
        wt, t_lw, i_lw = wnext(T["w_lora"])
        w2s, a2s, g2s = wt[0:64, 0:512], wt[64:128, 0:512], wt[:, 512:1024]
        t_tw = act(t0[0:64, 0, :], pm[0:64, 12, :], ACT.Tanh, t_pm)
        t_sg = act(sg[:, :], pm[:, 13, :], ACT.Sigmoid, t_pm)
        t_ld, t_aa = [], []
        for j in range(2):
            b = bank()
            for q in range(2):
                i = 2 * j + q
                last = mm(b.t[:, q * 256:q * 256 + 256], w2s[:, i * 128:i * 128 + 128], t0[0:64, 0, :], True, True,
                          b.rel, t_lw, t_tw)
            for q in range(2):
                i = 2 * j + q
                op = act(ld[:, i, :], b.t[:, q * 256:q * 256 + 256], ACT.Sigmoid, last, bias=gcols("w0")[i])
                t_ld.append(op)
            free(b, op)
        for j in range(2):
            b = bank()
            for q in range(2):
                i = 2 * j + q
                last = mm(b.t[:, q * 256:q * 256 + 256], a2s[:, i * 128:i * 128 + 128], pm[64:128, 12, :], True, True,
                          b.rel, t_lw, t_pm)
            for q in range(2):
                i = 2 * j + q
                op = act(aa[:, i, :], b.t[:, q * 256:q * 256 + 256], ACT.Sigmoid, last, bias=gcols("a0")[i])
                t_aa.append(op)
            free(b, op)
        t_g = []
        for tb in range(2):
            b = bank()
            last = mm(b.t[:, :], sg[:, tb * 128:tb * 128 + 128], g2s, True, True, b.rel, t_sg)
            op = acopy(gtok[:, tb, :], b.t[:, :], last)
            free(b, op)
            t_g.append(op)
        rdone[i_lw] = last
        v = vts1(ld[:, :, :], ld[:, :, :], -math.exp(-0.5), ALU.mult, t_ld)
        f2 = lambda t: t[:, :, :].rearrange("p a b -> p (a b)")
        t_cum = []
        for i in range(4):
            t_cum.append(V(lambda e, i=i: e.tensor_tensor_scan(cum[:, i, :], D("rst"), ld[:, i, :], 0.0, ALU.mult, ALU.add), v))
        kkc, kac, rkc = gcols("k_k"), gcols("k_a"), gcols("r_k")
        vk = [vts1(t1[:, i, :], pm[:, 4 + i, :], kkc[i], ALU.mult, t_pm) for i in range(4)]
        v = vtt(f2(be), f2(t1), f2(t1), ALU.mult, vk)
        t_rn = []
        for j in range(2):
            b = bank()
            last = mm(b.t[:, :], D("blk"), be[:, 2 * j:2 * j + 2, :], True, True, b.rel, v)
            op = vts1(ka[:, 2 * j:2 * j + 2, :], b.t[:, :].rearrange("p (a b) -> p a b", a=2), 1e-24, ALU.max, last)
            free(b, op)
            t_rn.append(rsqrt(ka[:, 2 * j:2 * j + 2, :], ka[:, 2 * j:2 * j + 2, :], op))
        t_kk = vtt(f2(t1), f2(t1), f2(ka), ALU.mult, t_rn)
        t_P = act(Pc[:, :, :], cum[:, :, :], ACT.Exp, t_cum)
        v = vtt(ld[:, :, :], cum[:, :, :], ld[:, :, :], ALU.subtract, t_cum)
        t_Pp = act(ld[:, :, :], ld[:, :, :], ACT.Exp, v)
        t_Pi = act(cum[:, :, :], cum[:, :, :], ACT.Exp, t_P, v, scale=-1.0)
        t_al = vtt(ARt[:, :, 0, :], t1[:, :, :], ld[:, :, :], ALU.mult, t_kk, t_Pp)
        t_rho = vtt(ARt[:, :, 1, :], pm[:, 0:4, :], Pc[:, :, :], ALU.mult, t_P)
        v = vtt(f2(be), f2(t1), f2(aa), ALU.mult, t_kk, t_aa, last)
        t_be = vtt(f2(be), f2(be), f2(cum), ALU.mult, v, t_Pi)
        vk = [vts(t1[:, i, :], aa[:, i, :], 1.0, kac[i], ALU.subtract, ALU.mult, t_be, t_al) for i in range(4)]
        t_kp = vstt(f2(t1), f2(t1), 1.0, pm[:, 4:8, :].rearrange("p a b -> p (a b)"), ALU.add, ALU.mult, vk)
        t_ka = vtt(f2(ka), f2(t1), f2(cum), ALU.mult, t_kp, t_Pi)
        vk = [vstt(t0[:, i, :], pm[:, i, :], rkc[i], t1[:, i, :], ALU.mult, ALU.mult, t_kp, t_ld) for i in range(4)]
        b = bank()
        for tb in range(2):
            for i in range(4):
                last = mm(b.t[:, tb * 8 + 2 * i:tb * 8 + 2 * i + 2], t0[:, i, tb * 128:tb * 128 + 128], D("hsel"), True, True, b.rel, vk)
        t_bon = vcopy(bon[:, :], b.t[:, 0:16], last)
        free(b, t_bon)
        t_tok = {}
        for nm, src, dt_, w in (("v", pm[:, 8:12, :], vtok, t_pm), ("a", ARt[:, :, 0, :], atok, t_al),
                                ("b", be[:, :, :], btok, t_be), ("k", ka[:, :, :], ktok, t_ka)):
            t_tok[nm] = []
            for tb in range(2):
                b = bank()
                for i in range(4):
                    last = tp(b.t[:, i * 128:i * 128 + 128], src[:, i, tb * 128:tb * 128 + 128], b.rel, w)
                op = copy(dt_[:, tb, :], b.t[:, :], last)
                free(b, op)
                t_tok[nm].append(op)

        SI = ctx.enter_context(ExitStack())
        GB = sbuf(SI, "GB", [128, 16, 256])
        GK = prep[:, 0:4, :, :].rearrange("p a b c -> p (a b) c")
        t128 = lambda t: t.rearrange("p a b -> p (a b)")[:, 0:2048].rearrange("p (n d) -> p n d", d=128)
        N_, X, Y, QX = t128(xT[:, :, :]), t128(hB[:, :, :]), t128(xn[:, :, :]), t128(pR[:, :, :])
        QY = pm[:, 0:8, :].rearrange("p a (c b) -> p (a c) b", b=128)
        prob = lambda b_, r, i: (b_ * 2 + r) * 4 + i
        t_GB, t_GK, t_N = [], [], []
        for kind in range(3):
            for b_ in range(2):
                ts = slice(b_ * 128, b_ * 128 + 128)
                for r in range(2):
                    rs = slice(64 * r, 64 * r + 64)
                    if kind < 2:
                        for hp in range(2):
                            b = bank()
                            for q in range(2):
                                i = hp * 2 + q
                                src, w = ((be, t_be), (ka, t_ka))[kind]
                                last = mm(b.t[:, q * 256:q * 256 + 256].rearrange("p (a b) -> p a b", a=2), src[rs, i, ts],
                                          ARt[rs, i, :, ts], True, True, b.rel, w, t_al, t_rho)
                            p0 = prob(b_, r, hp * 2)
                            op = vtt((GB, GK)[kind][:, p0:p0 + 2, :], b.t[:, :].rearrange("p (a b) -> p a b", a=2),
                                     bc(D("m2"), 1, 2), ALU.mult, last)
                            free(b, op)
                            (t_GB, t_GK)[kind].append(op)
                    else:
                        b = bank()
                        for i in range(4):
                            last = mm(b.t[:, i * 128:i * 128 + 128], ARt[rs, i, 0, ts], be[rs, i, ts], True, True, b.rel)
                        p0 = prob(b_, r, 0)
                        op = vtt(N_[:, p0:p0 + 4, :], b.t[:, :].rearrange("p (a b) -> p a b", a=4), bc(D("mt"), 1, 4), ALU.mult, last)
                        free(b, op)
                        t_N.append(op)
        NT = GB[:, :, 0:128]
        v = vstt(X[:, :, :], N_[:, :, :], -1.0, bc(D("lx0"), 1, 16), ALU.mult, ALU.mult, t_N)
        t_X = [vtt(X[:, :, :], X[:, :, :], bc(ident, 1, 16), ALU.add, v)]
        v = vstt(Y[:, :, :], NT, -1.0, bc(D("ly0"), 1, 16), ALU.mult, ALU.mult, t_GB)
        t_Y = [vtt(Y[:, :, :], Y[:, :, :], bc(ident, 1, 16), ALU.add, v)]
        t_prev = []
        for l in range(1, 6):
            both = l < 5
            t_QX, t_QY = [], []
            for side in ((0, 1) if both else (1,)):
                for j in range(4):
                    b = bank()
                    for q in range(4):
                        p = 4 * j + q
                        lt, rh, w = ((NT, X, t_X), (N_, Y, t_Y))[side]
                        last = mm(b.t[:, q * 128:q * 128 + 128], lt[:, p, :], rh[:, p, :], True, True, b.rel, w, t_N, t_GB)
                    op = copy((QX, QY)[side][:, 4 * j:4 * j + 4, :], b.t[:, :].rearrange("p (a b) -> p a b", a=4), last,
                              t_prev, t_bon, t_rho)
                    free(b, op)
                    (t_QX, t_QY)[side].append(op)
            t_t = []
            t_rd = []
            for side in ((0, 1) if both else (1,)):
                for j in range(4):
                    b = bank()
                    for q in range(4):
                        p = 4 * j + q
                        lt, rh = ((Y, QX), (X, QY))[side]
                        last = mm(b.t[:, q * 128:q * 128 + 128], lt[:, p, :], rh[:, p, :], True, True, b.rel, t_QX, t_QY, t_X, t_Y)
                    op = vtt((QX, QY)[side][:, 4 * j:4 * j + 4, :], b.t[:, :].rearrange("p (a b) -> p a b", a=4),
                             bc(D(("lx%d", "ly%d")[side] % l), 1, 4), ALU.mult, last)
                    free(b, op)
                    t_t.append((side, j, op))
                    t_rd = [last]
            t_prev = []
            nX, nY = [], []
            for side, j, op in t_t:
                M_ = (X, Y)[side][:, 4 * j:4 * j + 4, :]
                Z = (QX, QY)[side][:, 4 * j:4 * j + 4, :]
                o = G(lambda e, M_=M_, Z=Z: e.tensor_tensor(M_, M_, Z, ALU.subtract), op, t_rd)
                (nX, nY)[side].append(o)
                t_prev.append(o)
            t_X, t_Y = nX or t_X, nY
        MV = QX[:, 0:8, :].rearrange("p a b -> p (a b)").rearrange("p (t n) -> p t n", t=2)
        Ut = QX[:, 8:16, :].rearrange("p a b -> p (a b)").rearrange("p (t n) -> p t n", t=2)
        TAT = X[:, 0:8, :].rearrange("p (i c) t -> p i (c t)", c=2)
        nU = X[:, 8:16, :].rearrange("p a b -> p (a b)").rearrange("p (t n) -> p t n", t=2)
        t_MV, t_Ut, t_TA = [], [], []
        for b_ in range(2):
            b = bank()
            for h in range(8):
                p = prob(b_, h % 2, h // 2)
                last = mm(b.t[:, h * 64:h * 64 + 64], GK[:, p, 0:128], vtok[:, b_, h * 64:h * 64 + 64], True, True,
                          b.rel, t_GK, t_tok["v"])
            op = vcopy(MV[:, b_, :], b.t[:, :], last, t_prev)
            free(b, op)
            t_MV.append(op)
        for b_ in range(2):
            b = bank()
            for h in range(8):
                p = prob(b_, h % 2, h // 2)
                last = mm(b.t[:, h * 64:h * 64 + 64], Y[:, p, :], MV[:, b_, h * 64:h * 64 + 64], True, True, b.rel, t_Y, t_MV)
            op = vts1(Ut[:, b_, :], b.t[:, :], -1.0, ALU.mult, last)
            free(b, op)
            t_Ut.append(op)
        for j in range(2):
            b = bank()
            for q in range(2):
                i = 2 * j + q
                for b_ in range(2):
                    for r in range(2):
                        h = 2 * i + r
                        last = mm(b.t[64 * r:64 * r + 64, q * 256 + b_ * 128:q * 256 + b_ * 128 + 128],
                                  atok[:, b_, h * 64:h * 64 + 64], Y[:, prob(b_, r, i), :], True, True, b.rel, t_Y, t_tok["a"])
            op = vcopy(TAT[:, 2 * j:2 * j + 2, :], b.t[:, :].rearrange("p (a b) -> p a b", a=2), last, t_prev)
            free(b, op)
            t_TA.append(op)
        ST = pR[:, :, :].rearrange("p a b -> p (a b)")[:, 2048:3328].rearrange("p (c i d) -> p c i d", c=5, i=4)
        yr = junk[:, :].rearrange("p (t n) -> p t n", t=2)
        ysq = N_[:, 0:8, :].rearrange("p a b -> p (a b)").rearrange("p (n d) -> p n d", d=64)
        yst = sbuf(SI, "yst", [128, 3, 16])
        t_S = V(lambda e: e.memset(ST[:, 0, :, :], 0.0))
        t_nU = []
        t_yr = [[], []]
        for b_ in range(2):
            by = [bank(), bank()]
            for hf in range(2):
                c = 2 * b_ + hf
                ps = slice(64 * hf, 64 * hf + 64)
                cs = slice(64 * c, 64 * c + 64)
                bu = [bank(), bank()]
                for r in range(2):
                    rs = slice(64 * r, 64 * r + 64)
                    for i in range(4):
                        last = mm(bu[r].t[ps, i * 64:i * 64 + 64], TAT[rs, i, cs], ST[rs, c, i, :], True, True,
                                  bu[r].rel, t_TA, t_S)
                    hv = lambda t: t[ps, b_, :].rearrange("p (i r d) -> p i r d", r=2, d=64)[:, :, r, :]
                    op = vtt(hv(nU), hv(Ut), bu[r].t[ps, 0:256].rearrange("p (i d) -> p i d", d=64), ALU.subtract, last, t_Ut, t_prev)
                    free(bu[r], op)
                    t_nU.append(op)
                    for i in range(4):
                        ly = mm(by[r].t[ps, i * 64:i * 64 + 64], ARt[rs, i, 1, cs], ST[rs, c, i, :], True, True, by[r].rel, t_S)
                b = bank()
                for r in range(2):
                    rs = slice(64 * r, 64 * r + 64)
                    for i in range(4):
                        hs = slice((2 * i + r) * 64, (2 * i + r) * 64 + 64)
                        o = b.t[rs, i * 64:i * 64 + 64]
                        mm(o, ktok[ps, b_, hs], vtok[ps, b_, hs], True, False, b.rel, t_tok["k"], t_tok["v"])
                        last = mm(o, btok[ps, b_, hs], nU[ps, b_, hs], False, True, t_tok["b"], t_nU)
                v = vtt(ST[:, c + 1, :, :], b.t[:, 0:256].rearrange("p (i d) -> p i d", d=64), ST[:, c, :, :], ALU.add, last, t_S)
                free(b, v)
                t_S = vtt(ST[:, c + 1, :, :], ST[:, c + 1, :, :], bc(Pc[:, :, 64 * c + 63], 2, 64), ALU.mult, v)
            for r in range(2):
                hv = lambda t: t[:, b_, :].rearrange("p (i r d) -> p i r d", r=2, d=64)[:, :, r, :]
                op = vcopy(hv(yr), by[r].t[:, 0:256].rearrange("p (i d) -> p i d", d=64), ly)
                free(by[r], op)
            b = bank()
            for h in range(8):
                hs = slice(h * 64, h * 64 + 64)
                p = prob(b_, h % 2, h // 2)
                mm(b.t[:, hs], GB[:, p, 128:256], nU[:, b_, hs], True, False, b.rel, t_nU)
                last = mm(b.t[:, hs], GK[:, p, 128:256], vtok[:, b_, hs], False, True)
            v = vtt(yr[:, b_, :], b.t[:, :], yr[:, b_, :], ALU.add, last, op)
            free(b, v)
            t_yr[b_] = v
        y16 = yr[:, :, :].rearrange("p t (n d) -> p (t n) d", d=64)
        yf = yr[:, :, :]
        v = vred(yst[:, 0, :], y16, ALU.add, t_yr)
        v = vts1(yst[:, 0, :], yst[:, 0, :], 1.0 / 64, ALU.mult, v)
        v = vtt(y16, y16, bc(yst[:, 0, :], 2, 64), ALU.subtract, v)
        q = vtt(ysq, y16, y16, ALU.mult, v, t_Y)
        q = vred(yst[:, 1, :], ysq, ALU.add, q)
        q = vts(yst[:, 1, :], yst[:, 1, :], 1.0 / 64, 64e-5, ALU.mult, ALU.add, q)
        q = rsqrt(yst[:, 1, :], yst[:, 1, :], q)
        v = vtt(y16, y16, bc(yst[:, 1, :], 2, 64), ALU.mult, q)
        v = vtt(yf, yf, bc(rows[:, 1024:1536], 1, 2), ALU.mult, v, t_rows)
        v = vtt(yf, yf, bc(rows[:, 1536:2048], 1, 2), ALU.add, v)
        q = [vtt(ysq[:, tb * 8:tb * 8 + 8, :], vtok[:, tb, :].rearrange("p (n d) -> p n d", d=64),
                 bc(bon[:, tb * 8:tb * 8 + 8], 2, 64), ALU.mult, t_bon, t_tok["v"]) for tb in range(2)]
        v = vtt(y16, y16, ysq, ALU.add, v, q)
        t_yb = vtt(ytok[:, :, 512:1024], yf, gtok[:, :, :], ALU.mult, v, t_g)
        t_yT[4:8] = to_T([ytok[:, tb, 512:1024] for tb in range(2)], yT2[:, 4:8, :], 4, None, [t_yb, t_yb])
        t_x3 = residual(hB, hA, yT2, t_yT, T["w_o"], t_x2)
        if stop == 5:
            return finish(nc, Q, sems, ctx, outs, hB, t_x3, load)
        n_h = []
        for tb in range(2):
            n_h.append(acopy(hA[:, tb, :], hB[:, tb, :], t_x3))
        n_n = norm(tbs(hB), tbs(xn), t_x3)
        w_xT = to_T(tbs(xn), xT, 8, gcols("g_ffn"), n_n)
        t_x3 = [n_h, w_xT]
        SI.close()
        SR.close()
        SD.close()
        S_AD.close()

        SE = ctx.enter_context(ExitStack())
        slT = sbuf(SE, "slT", [128, 3, 256])
        A4 = sbuf(SE, "A4", [128, 2, 4, 128])
        B4 = sbuf(SE, "B4", [128, 2, 4, 128])
        ST_ = ctx.enter_context(ExitStack())
        qP = sbuf(ST_, "qP", [128, 16, 256])
        sS = sbuf(ST_, "sS", [128, 16, 128])
        sS2 = sbuf(ST_, "sS2", [128, 16, 128])
        m16 = sbuf(ST_, "m16", [128, 16, 16])
        ix = sbuf(ST_, "ix", [128, 16, 16], U32)
        ixf = sbuf(ST_, "ixf", [128, 16, 16])
        cand = sbuf(ST_, "cand", [128, 8, 16, 16])
        cand2 = sbuf(ST_, "cand2", [128, 8, 256])
        top = sbuf(ST_, "top", [128, 8, 16])
        pst = sbuf(ST_, "pst", [128, 8, 16], U32)
        psi = sbuf(ST_, "psi", [128, 2, 128], U32)
        psf = sbuf(ST_, "psf", [128, 2, 128])
        sel = sbuf(ST_, "sel", [128, 3, 128])
        gs = sbuf(ST_, "gs", [128, 2, 8])
        t_qP = []

        def ev_q(b, j, c, last):
            op = copy(qP[:, j:j + 2, :], b.t[:, :].rearrange("p (a b) -> p a b", a=2), last, t_x3)
            t_qP.append(op)
            return op
        projT(xT, w_xT, T["w_pq"], 16, ev_q)
        sk = [wnext(T["sub_keys"][j]) for j in range(2)]
        t_sl = []
        t_done = []
        for tb in range(2):
            t_s = []
            for j in range(4):
                b = bank()
                for q in range(4):
                    hp = 4 * j + q
                    wt, tk, i = sk[hp // 8]
                    last = mm(b.t[:, q * 128:q * 128 + 128], qP[:, hp, tb * 128:tb * 128 + 128],
                              wt[:, (hp % 8) * 128:(hp % 8) * 128 + 128], True, True, b.rel, tk, t_qP)
                    rdone[i] = last
                op = acopy(sS[:, 4 * j:4 * j + 4, :], b.t[:, :].rearrange("p (a b) -> p a b", a=4), last, t_done)
                free(b, op)
                t_s.append(op)

            def top16(n, src, src2, m, xi, w):
                a = [V(lambda e, i=i: e.max(m[:, i, 0:8], src(i)), w) for i in range(n)]
                b1 = [V(lambda e, i=i: e.max_index(xi[:, i, 0:8], m[:, i, 0:8], src(i)), a[i]) for i in range(n)]
                c1 = [V(lambda e, i=i: e.match_replace(src2(i), m[:, i, 0:8], src(i), -3.0e38), a[i]) for i in range(n)]
                d1 = [V(lambda e, i=i: e.max(m[:, i, 8:16], src2(i)), c1[i]) for i in range(n)]
                e1 = [V(lambda e, i=i: e.max_index(xi[:, i, 8:16], m[:, i, 8:16], src2(i)), d1[i]) for i in range(n)]
                return [e1[-1], b1[-1], d1[-1]]
            v = top16(16, lambda i: sS[:, i, :], lambda i: sS2[:, i, :], m16, ix, t_s)
            v1 = vcopy(ixf[:, :, :], ix[:, :, :], v)
            mv = m16[:, :, :].rearrange("p (h c) k -> p h c k", c=2)
            xv = ixf[:, :, :].rearrange("p (h c) k -> p h c k", c=2)
            v = vtt(cand[:, :, :, :], bc(mv[:, :, 0, :], 3, 16), bc(mv[:, :, 1, :], 2, 16), ALU.add, v)
            cv = lambda i: cand[:, i, :, :].rearrange("p a b -> p (a b)")
            v = top16(8, cv, lambda i: cand2[:, i, :], top, pst, v)
            g = vtt(top[:, :, :], top[:, :, :], bc(top[:, :, 0], 2, 16), ALU.subtract, v) if False else None
            sg_ = sel[:, 2, :].rearrange("p (h k) -> p h k", k=16)
            g = vtt(sg_, top[:, :, :], bc(top[:, :, 0], 2, 16), ALU.subtract, v)
            g = act(sg_, sg_, ACT.Exp, g)
            g = vred(gs[:, 0, :], sg_, ALU.add, g)
            g = V(lambda e: e.reciprocal(gs[:, 1, :], gs[:, 0, :]), g)
            g = vtt(sg_, sg_, bc(gs[:, 1, :], 2, 16), ALU.mult, g)
            pf = pst[:, :, :].rearrange("p h k -> p (h k)")
            s0 = vts1(psi[:, 0, :], pf, 4, ALU.logical_shift_right, v)
            s1 = vts1(psi[:, 1, :], pf, 15, ALU.bitwise_and, v)
            s0 = vcopy(psf[:, :, :], psi[:, :, :], s0, s1)
            eq = cand[:, :, :, :]
            eqf = eq.rearrange("p h a b -> p (h a) b")
            for j in range(2):
                q = vtt(eqf, bc(psf[:, j, :], 2, 16), bc(C("iota16"), 1, 128), ALU.is_equal, s0, v)
                q = vtt(eq, eq, bc(xv[:, :, j, :], 2, 16), ALU.mult, q, v1)
                s0 = vred(sel[:, j, :], eqf, ALU.add, q)
            b = bank()
            for j in range(3):
                last = tp(b.t[:, j * 128:j * 128 + 128], sel[:, j, :], b.rel, s0, g)
            op = vcopy(slT[:, :, tb * 128:tb * 128 + 128], b.t[:, 0:384].rearrange("p (a b) -> p a b", a=3), last)
            free(b, op)
            t_sl.append(op)
            t_done = [op, s0, g]
        ST_.close()
        Gt = sbuf(SE, "Gt", [128, 128, 256])
        t_G = []
        used = [[], []]
        for t4 in range(64):
            u = t4 % 2
            va_, vb_ = [], []
            for q in range(4):
                t = t4 * 4 + q
                vb_.append(vts1(B4[:, u, q, :], C("iota"), slT[:, 1, t:t + 1], ALU.is_equal, t_sl, used[u]))
                va_.append(vts(A4[:, u, q, :], C("iota"), slT[:, 0, t:t + 1], slT[:, 2, t:t + 1], ALU.is_equal, ALU.mult))
            b = bank()
            for q in range(4):
                last = mm(b.t[:, q * 128:q * 128 + 128], B4[:, u, q, :], A4[:, u, q, :], True, True, b.rel, va_, vb_)
            used[u] = [last]
            op = acopy(Gt[:, :, t4 * 4:t4 * 4 + 4], b.t[:, :].rearrange("p (t i) -> p i t", t=4), last)
            free(b, op)
            t_G.append(op)
        NW = 3
        ge = sbuf(SE, "ge", [128, NW, 256])
        Wt = sbuf(SE, "Wt", [128, NW, 256])
        bo = [bank() for _ in range(4)]
        t_W = {}
        vslot = {}
        t_O = {}

        def scores(c):
            wt, tk, i = wnext(T["eu"][c])
            vslot[c] = wnext(T["ev"][c])
            b = bank()
            for k in range(8):
                last = mm(b.t[:, 0:256], wt[:, k * 128:k * 128 + 128], xT[:, k, :], k == 0, k == 7, tk, b.rel, w_xT)
            rdone[i] = last
            a = act(ge[:, c % NW, :], b.t[:, 0:256], ACT.Gelu, last, t_W.get(c - NW), t_G)
            free(b, a)
            t_W[c] = vtt(Wt[:, c % NW, :], ge[:, c % NW, :], Gt[:, c, :], ALU.mult, a, t_G, t_O.get(c - NW))

        def apply(c):
            wt, tk, i = vslot[c]
            for tb in range(2):
                for g in range(2):
                    b = bo[tb * 2 + g]
                    last = mm(b.t[:, :], Wt[:, c % NW, tb * 128:tb * 128 + 128], wt[:, g * 512:g * 512 + 512], c == 0, c == 127,
                              b.rel, tk, t_W[c])
            rdone[i] = last
            t_O[c] = last
        NE = 128
        for c in range(NE + 2):
            if c < NE:
                scores(c)
            if c >= 2:
                apply(c - 2)
        fin = [[], []]
        for tb in range(2):
            for g in range(2):
                gsl = slice(g * 512, g * 512 + 512)
                fin[tb].append(vtt(hA[:, tb, gsl], bo[tb * 2 + g].t[:, :], hA[:, tb, gsl], ALU.add, t_O[127], n_h))
        return finish(nc, Q, sems, ctx, outs, hA, fin, load)


def finish(nc, Q, sems, ctx, out, src, toks, load):
    o = out.rearrange("b (t p) d -> p (b t) d", p=128)
    d = load("sp", o, src[:, :, :], toks)
    Q.add("sp", lambda e: e.nop(), d)
    Q.number(sems)
    block = ctx.enter_context(nc.Block())

    @block.tensor
    def _(e):
        Q.emit("pe", e)

    @block.vector
    def _(e):
        Q.emit("dve", e)

    @block.scalar
    def _(e):
        Q.emit("act", e)

    @block.gpsimd
    def _(e):
        Q.emit("pool", e)

    @block.sync
    def _(e):
        Q.emit("sp", e)


def layout(inputs):
    I = {k: np.asarray(v) for k, v in inputs.items()}
    c, d = constants()

    def w_t(W):
        K, N = W.shape
        return np.ascontiguousarray(W.reshape(K // 128, 128, N // 128, 128).transpose(2, 1, 0, 3)).reshape(N // 128, 128, K)

    def w_g(W):
        N = W.shape[1]
        return np.ascontiguousarray(W.reshape(4, 2, 128, N // 512, 512).transpose(3, 0, 2, 1, 4)).reshape(-1, 128, 1024)

    def w_k(W):
        return np.ascontiguousarray(W.reshape(-1, 128, W.shape[1]))

    def cols(v):
        return v.reshape(-1, 128).T

    def row(v):
        return np.broadcast_to(v.reshape(1, -1), (128, v.size))

    w_in = I["w_in"][0]
    w2 = I["w_in_2"][0]
    pk = {"g_mix": I["g_mix"], "g_cross": I["g_cross"], "g_mem": I["g_mem"], "g_mlp": I["g_mlp"], "g_subln": I["g_subln"],
          "g_mix_2": I["g_mix_2"], "g_cq": I["g_cq_2"], "g_ckv": I["g_ckv_2"], "g_attn_out": I["g_attn_out_2"],
          "rwkv_mu": I["rwkv_mu_2"], "w0": I["w0_2"], "a0": I["a0_2"], "k_k": I["k_k_2"], "k_a": I["k_a_2"], "r_k": I["r_k_2"],
          "g_ffn": I["g_ffn_2"]}
    pk = {k: cols(v) for k, v in pk.items()}
    poff, _ = offsets(pk)
    rows = np.concatenate([row(I[k]) for k in ("g_final", "ln_x_w_2", "ln_x_b_2", "g_qnorm_2", "g_knorm_2", "lambda_q1",
                                                "lambda_k1", "lambda_q2", "lambda_k2")], 1)
    T = {
        "x": I["x"][0], "mem": I["mem"][0], "cst": np.concatenate(list(c.values()), 1), "dst": np.concatenate(list(d.values()), 1),
        "par": np.concatenate(list(pk.values()), 1), "rows": rows,
        "pos": np.concatenate([I["positions"].reshape(2, 128).T, I["positions_2"].reshape(2, 128).T], 1),
        "w_in_a": w_g(np.concatenate([w_in[:, 0:1536], w_in[:, 2560:3072]], 1)), "w_in_t": w_t(w_in[:, 1536:2560]),
        "w_out": w_g(I["w_out"][0]), "w_xk": w_t(I["w_xkv"][0][:, 0:1024]), "w_xv": w_g(I["w_xkv"][0][:, 1024:2048]),
        "w_xq": w_t(I["w_xq"][0]), "w_xo": w_g(I["w_xo"][0]), "w_up": w_t(I["w_up"][0]), "w_down": w_k(I["w_down"][0]),
        "w_mla": w_k(w2[:, 0:672]), "w_rwkv": w_t(w2[:, 672:2464]), "w_uq": w_k(I["w_uq_2"][0]),
        "w_ukv": w_k(np.concatenate([I["w_uk_2"][0], I["w_uv_2"][0]], 1)),
        "w_lora": np.concatenate([np.concatenate([I["w2_2"][0], I["a2_2"][0]], 0), I["g2_2"][0]], 1)[None],
        "w_o": w_g(I["w_o_2"][0]), "w_pq": w_t(I["w_pq_2"][0]),
        "sub_keys": I["sub_keys_2"][0].transpose(3, 0, 1, 2).reshape(128, 2, 1024).transpose(1, 0, 2),
        "eu": np.ascontiguousarray(I["expert_u_2"][0].reshape(128, 128, 8, 128).transpose(0, 3, 2, 1)).reshape(128, 128, 1024),
        "ev": I["expert_v_2"][0].reshape(128, 128, 1024),
    }
    return {k: np.ascontiguousarray(v) for k, v in T.items()}, poff


def kernel(**inputs):
    import concourse.bacc as _bacc
    from concourse import mybir as _mybir
    from concourse.bass_utils import run_bass_kernel_spmd as _run

    nc = _bacc.Bacc("TRN2", target_bir_lowering=False, num_devices=1)
    T, poff = layout(inputs)
    arrays, args = {}, {}
    for name, a in T.items():
        arrays[f"in_{name}"] = a
        args[name] = nc.dram_tensor(f"in_{name}", a.shape, _mybir.dt.from_np(a.dtype), kind="ExternalInput").ap()
    out = nc.dram_tensor("out_0", (1, 256, 1024), _mybir.dt.from_np(np.dtype("float32")), kind="ExternalOutput").ap()
    build(nc, args, poff, out, STOP)
    r = _run(nc, [arrays], core_ids=[0])
    return r.results[0]["out_0"]


STOP = 99
```

```python
import math
from collections import deque
from contextlib import ExitStack

import numpy as np
import concourse.bass as bass
from concourse import mybir

F32 = mybir.dt.float32
F32R = mybir.dt.float32r
BF16 = mybir.dt.bfloat16
I32 = mybir.dt.int32
U32 = mybir.dt.uint32
ALU = mybir.AluOpType
ACT = mybir.ActivationFunctionType
AX = mybir.AxisListType.X
NRAW, NSP = 4, 3
ORDER = [("w_in_a", 16, 1024, 1), ("w_in_t", 8, 1024, 1), ("w_xk", 8, 1024, 1), ("w_xv", 8, 1024, 1), ("w_out", 8, 1024, 1),
         ("w_xq", 8, 1024, 1), ("w_xo", 8, 1024, 1), ("w_up", 32, 1024, 1), ("w_down", 32, 1024, 1), ("w_mla", 8, 672, 1),
         ("w_rwkv", 14, 1024, 1), ("w_uq", 3, 768, 1), ("w_ukv", 2, 1024, 1), ("w_lora", 1, 1024, 0), ("w_o", 8, 1024, 1),
         ("w_pq", 16, 1024, 1), ("sub_keys", 2, 1024, 0), ("eu", 128, 1024, 1), ("ev", 128, 1024, 1)]
ON_POOL = ("w_xk", "w_xv", "eu", "ev")
NEG = -1e30


class Op:

    def __init__(self, eng):
        self.eng, self.sem, self.val, self.need, self.dma = eng, None, 0, False, False


class Queues:

    def __init__(self):
        self.q = {e: [] for e in ("pe", "dve", "act", "pool", "sp")}

    def add(self, eng, fn, *waits):
        op = Op(eng)
        ws = []
        todo = list(waits)
        while todo:
            w = todo.pop()
            if w is None:
                continue
            if isinstance(w, (list, tuple)):
                todo += w
            else:
                w.need = True
                ws.append(w)
        self.q[eng].append((op, fn, ws))
        return op

    def dma(self, eng, out, in_, sem, val, *waits):
        op = self.add(eng, lambda e: e.dma_start(out, in_), *waits)
        op.sem, op.val, op.dma = sem, val, True
        return op

    def number(self, sems):
        for eng, q in self.q.items():
            n = 0
            for op, _, _ in q:
                if op.need and not op.dma:
                    n += 1
                    op.sem, op.val = sems[eng], n

    def emit(self, eng, e):
        seen = {}
        for op, fn, ws in self.q[eng]:
            want = {}
            for w in ws:
                if eng == "pe" and w.eng == "pe":
                    continue
                k = id(w.sem)
                if want.get(k, (None, 0))[1] < w.val:
                    want[k] = (w.sem, w.val)
            for k, (s, v) in want.items():
                if seen.get(k, 0) < v:
                    e.wait_ge(s, v)
                    seen[k] = v
            ins = fn(e)
            if op.dma:
                ins.then_inc(op.sem, 16)
            elif op.need:
                ins.then_inc(op.sem, 1)


SIZE = {F32: 4, F32R: 4, I32: 4, U32: 4, BF16: 2}


class Mem:

    def __init__(self, nc, at, end):
        self.nc, self.at, self.end = nc, at, end

    def sub(self):
        return Mem(self.nc, self.at, self.end)

    def __call__(self, name, shape, dt=F32):
        t = self.nc.alloc_sbuf_tensor_at(name, shape, dt, offset=self.at)
        self.at += int(np.prod(shape[1:])) * SIZE[dt]
        self.at = (self.at + 31) // 32 * 32
        assert self.at <= self.end, (name, self.at, self.end)
        return t


def bc(ap, axis, n):
    u = ap.unsqueeze(axis)
    shape = list(u.shape)
    shape[axis] = n
    return u.to_broadcast(shape)


def constants():
    p = np.arange(128)[:, None]
    f = np.arange(128)[None, :]
    one = lambda m: m.astype(np.float32)
    add = lambda m: np.where(m, 0.0, NEG).astype(np.float32)
    c = {"ident": one(p == f), "iota": np.broadcast_to(np.arange(128, dtype=np.float32), (128, 128)),
         "iota16": np.broadcast_to(np.arange(16, dtype=np.float32), (128, 16))}
    d = {}
    z = np.zeros((128, 128), np.float32)
    d["maskA"] = np.concatenate([z, add(f <= p)], 1)
    d["maskM"] = np.concatenate([z, add(f // 64 <= p // 64)], 1)
    d["maskS"] = one(p < f)
    d["negtri"] = -one(p >= f)
    d["negones"] = -np.ones((128, 128), np.float32)
    d["blk"] = one(p // 64 == f // 64)
    d["hsel"] = one(p // 64 == np.arange(2)[None, :])
    same = p // 64 == f // 64
    d["m2"] = np.concatenate([one(same & (p < f)), one(same & (p <= f))], 1)
    d["eye2"] = one(p % 64 == np.arange(64)[None, :])
    for l in range(6):
        m = 1 << l
        lev = (p // (2 * m) == f // (2 * m)) & (p // m % 2 == 1) & (f // m % 2 == 0)
        d[f"lx{l}"] = one(lev)[:, 0:64] + one(lev)[:, 64:128]
        d[f"ly{l}"] = one(lev.T)[:, 0:64] + one(lev.T)[:, 64:128]
    d["rst"] = np.broadcast_to(one(np.arange(256)[None, :] % 64 != 0), (128, 256))
    f1 = np.float32(500000.0) ** (-np.arange(0, 16, 2, dtype=np.float32) / np.float32(16))
    f2 = np.float32(10000.0) ** (-np.arange(16, dtype=np.float32) / np.float32(16))
    d["invf"] = np.broadcast_to(np.concatenate([f1, f2]).astype(np.float32), (128, 24))
    return c, d


def offsets(d):
    off, n = {}, 0
    for k, v in d.items():
        off[k] = (n, n + v.shape[1])
        n += v.shape[1]
    return off, n


def build(nc, T, poff, outs, stop=99):
    coff, ncc = offsets(constants()[0])
    doff, ncd = offsets(constants()[1])
    npar = max(b for _, b in poff.values())
    Q = Queues()
    ctx = ExitStack()
    with ctx:
        sems = {e: ctx.enter_context(nc.semaphore("s_" + e)) for e in Q.q}

        base = (nc.sbuf_base + 31) // 32 * 32
        fence = ctx.enter_context(nc.sbuf_tensor("fence", [128, (nc.sbuf_bytes_remaining - 64) // 4], F32))
        P = Mem(nc, base, nc.sbuf_base // 32 * 32)

        def sbuf(m, name, shape, dt=F32):
            return m(name, shape, dt)

        def PE(fn, *w): return Q.add("pe", fn, *w)
        def V(fn, *w): return Q.add("dve", fn, *w)
        def A(fn, *w): return Q.add("act", fn, *w)
        def G(fn, *w): return Q.add("pool", fn, *w)

        nload = [0]

        def load(eng, out, in_, *w):
            nload[0] += 1
            return Q.dma(eng, out, in_, ctx.enter_context(nc.semaphore(f"ld{nload[0]}")), 16, *w)

        class Bank:
            pass
        banks = deque()
        for i in range(8):
            b = Bank()
            b.t = ctx.enter_context(nc.psum_tensor(f"ps{i}", [128, 512], F32))
            b.rel = []
            banks.append(b)

        def bank(): return banks.popleft()

        def free(b, *ops):
            b.rel = list(ops)
            banks.append(b)

        raw = sbuf(P, "raw", [128, NRAW, 1024])
        spl = sbuf(P, "spl", [128, NSP, 2, 1024], F32R)
        rsem = [ctx.enter_context(nc.semaphore(f"raw{i}")) for i in range(NRAW)]
        pieces = [(nm, j, n, sp) for nm, cnt, n, sp in ORDER for j in range(cnt)]
        nsplit = [0]
        state = {"dma": 0, "split": 0, "use": 0}
        t_dma, t_hl, slot_of, wfree, rawfree = {}, {}, {}, {}, {}
        last_in_slot = {}

        def issue(i):
            nm, j, n, _ = pieces[i]
            t_dma[i] = Q.dma("sp", raw[:, i % NRAW, 0:n], T[nm][j], rsem[i % NRAW], 16 * (i // NRAW + 1), rawfree.get(i - NRAW))

        def raw_done(i, op):
            rawfree[i] = op
            if i + NRAW < len(pieces):
                issue(i + NRAW)

        def split(i):
            nm, j, n, sp = pieces[i]
            if not sp:
                return
            k = nsplit[0]
            nsplit[0] += 1
            s_ = k % NSP
            slot_of[i] = s_
            before = last_in_slot.get(s_)
            r, h, l = raw[:, i % NRAW, 0:n], spl[:, s_, 0, 0:n], spl[:, s_, 1, 0:n]
            w = wfree[before] if before is not None else None
            a = A(lambda e: e.activation(h, r, ACT.Copy), t_dma[i], w)
            f = G if nm in ON_POOL else V
            b = f(lambda e: e.tensor_tensor(l, r, h.bitcast(F32), ALU.subtract), a, w)
            last_in_slot[s_] = i
            t_hl[i] = (a, b)
            raw_done(i, b)

        def ahead():
            while state["split"] < len(pieces) and state["split"] <= state["use"] + NSP - 1:
                i = state["split"]
                if i not in t_dma:
                    break
                if pieces[i][3]:
                    before = last_in_slot.get(nsplit[0] % NSP)
                    if before is not None and before not in wfree:
                        break
                split(i)
                state["split"] += 1

        def wnext(nm, j):
            i = state["use"]
            assert pieces[i][:2] == (nm, j), (pieces[i], nm, j)
            ahead()
            assert state["split"] > i
            state["use"] += 1
            n = pieces[i][2]
            if not pieces[i][3]:
                return raw[:, i % NRAW, 0:n], None, t_dma[i], i
            return spl[:, slot_of[i], 0, 0:n], spl[:, slot_of[i], 1, 0:n], t_hl[i], i

        def wdone(i, op):
            wfree[i] = op
            if not pieces[i][3]:
                raw_done(i, op)
            ahead()

        cst = sbuf(P, "cst", [128, ncc])
        par = sbuf(P, "par", [128, npar])
        hA_at = P.at
        hA = sbuf(P, "hA", [128, 2, 1024])
        x_at = P.at
        xhl = sbuf(P, "xhl", [128, 2, 8, 256], F32R)
        xT = (xhl[:, 0, :, :], xhl[:, 1, :, :])
        stats = sbuf(P, "stats", [128, 96])
        neghalf = sbuf(P, "neghalf", [128, 1])
        S_AD = P.sub()
        dst = sbuf(S_AD, "dst", [128, ncd])
        rows = sbuf(S_AD, "rows", [128, 2496])
        hx = sbuf(S_AD, "hx", [128, 2, 2, 1024])
        hB, xn = hx[:, 0, :, :], hx[:, 1, :, :]
        junk = sbuf(S_AD, "junk", [128, 1024])
        pos = sbuf(S_AD, "pos", [128, 4], I32)

        def C(k): return cst[:, coff[k][0]:coff[k][1]]
        def D(k): return dst[:, doff[k][0]:doff[k][1]]
        def par_(k): return par[:, poff[k][0]:poff[k][1]]

        ident = C("ident")
        t_half = G(lambda e: e.memset(neghalf[:, :], -0.5))
        x_r = T["x"].rearrange("(t p) d -> p t d", p=128)
        t_x = load("act", hA[:, :, :], x_r)
        t_c = load("act", cst[:, :], T["cst"])
        t_par = load("act", par[:, :], T["par"])
        t_pos = load("act", pos[:, :], T["pos"])
        t_d = load("act", dst[:, :], T["dst"])
        t_rows = load("act", rows[:, :], T["rows"])
        for i in range(NRAW):
            issue(i)
        nstat = [0]

        def stat():
            nstat[0] += 1
            return stats[:, nstat[0] - 1:nstat[0]]

        def mm(out, l, r, st, sp, *w):
            return PE(lambda e: e.matmul(out, l, r, start=st, stop=sp), *w)

        def tp(out, in_, *w):
            n = in_.shape[0]
            return PE(lambda e: e.transpose(out, in_, ident[0:n, 0:n]), t_c, *w)

        def vts(out, a, s1, s2, o0, o1, *w):
            return V(lambda e: e.tensor_scalar(out, a, s1, s2, o0, o1), *w)

        def vts1(out, a, s1, o0, *w):
            return V(lambda e: e.tensor_scalar(out, a, s1, None, o0), *w)

        def rsqrt(out, a, *w):
            h = neghalf[:, 0:1].to_broadcast(list(a.shape)) if len(a.shape) == 2 else bc(neghalf[:, 0:1], 1, a.shape[1]).to_broadcast(list(a.shape))
            return G(lambda e: e.tensor_tensor(out, a, h, ALU.pow), t_half, *w)

        def vtt(out, a, b, op, *w):
            return V(lambda e: e.tensor_tensor(out, a, b, op), *w)

        def vstt(out, a, s, b, o0, o1, *w):
            return V(lambda e: e.scalar_tensor_tensor(out, a, s, b, o0, o1), *w)

        def vcopy(out, a, *w):
            return V(lambda e: e.tensor_copy(out, a), *w)

        def vred(out, a, op, *w):
            return V(lambda e: e.tensor_reduce(out, a, AX, op), *w)

        def act(out, a, f, *w, scale=1.0, bias=0.0, acc=None):
            return A(lambda e: e.activation(out, a, f, bias=bias, scale=scale, accum_out=acc), *w)

        def acopy(out, a, *w):
            return A(lambda e: e.activation(out, a, ACT.Copy), *w)

        flip = [0]

        def copy(out, a, *w):
            flip[0] ^= 1
            return (vcopy if flip[0] else acopy)(out, a, *w)

        t_junk = [None]

        def rstd(src, n, w):
            s, s2 = stat(), stat()
            a = act(junk[:, 0:src.shape[1]], src, ACT.Square, w, t_junk[0], acc=s)
            t_junk[0] = a
            v = vts(s2, s, 1.0 / n, 1e-6, ALU.mult, ALU.add, a)
            return s2, rsqrt(s2, s2, v)

        def norm(src, out, w):
            r = []
            for tb in range(2):
                s, v = rstd(src[tb], src[tb].shape[1], w[tb])
                r.append(vts1(out[tb], src[tb], s, ALU.mult, v, w[tb]))
            return r

        def to_T(src, out, nk, g, w, w2=None):
            toks = []
            for j in range(0, nk, 2):
                b = bank()
                n = min(2, nk - j)
                for k in range(n):
                    for tb in range(2):
                        last = tp(b.t[:, k * 256 + tb * 128:k * 256 + tb * 128 + 128],
                                  src[tb][:, (j + k) * 128:(j + k + 1) * 128], b.rel, w[tb])
                hl = []
                for k in range(n):
                    o = tuple(t[:, j + k, :] for t in out)
                    i = b.t[:, k * 256:(k + 1) * 256]
                    s = g[j + k] if g is not None else None
                    h, l = o
                    if s is None:
                        hl.append((acopy(h, i, last, w2), lambda a_, h=h, l=l, i=i: vtt(l, i, h.bitcast(F32), ALU.subtract, a_, w2)))
                    else:
                        hl.append((act(h, i, ACT.Copy, last, t_par, w2, scale=s),
                                   lambda a_, h=h, l=l, i=i, s=s: vstt(l, i, s, h.bitcast(F32), ALU.mult, ALU.subtract, a_, w2)))
                fin_ = hl[-1][0]
                for a_, f in hl:
                    op = f([a_, fin_])
                    toks.append([a_, op])
                free(b, op)
            return toks

        def to_T32(src, out, nk, w):
            toks = []
            for j in range(0, nk, 2):
                b = bank()
                for k in range(2):
                    for tb in range(2):
                        last = tp(b.t[:, k * 256 + tb * 128:k * 256 + tb * 128 + 128],
                                  src[tb][:, (j + k) * 128:(j + k + 1) * 128], b.rel, w[tb])
                op = copy(out[:, j:j + 2, :], b.t[:, :].rearrange("p (a b) -> p a b", a=2), last)
                free(b, op)
                toks += [op, op]
            return toks

        def gcols(k):
            return [par[:, c:c + 1] for c in range(*poff[k])]

        def evac_hl(out, a, last, *w):
            h, l = out
            x = acopy(h, a, last, *w)
            return [x, vtt(l, a, h.bitcast(F32), ALU.subtract, x, last, *w)]

        def mm3(out, l, r, st, sp, *w):
            mm(out, l[0], r[0], st, False, *w)
            mm(out, l[0], r[1], False, False, *w)
            return mm(out, l[1], r[0], False, sp, *w)

        def proj512(inT, w, W, g):
            b = [bank(), bank()]
            for j in range(4):
                wh, wl, tk, i = wnext(W, g * 4 + j)
                for k in range(2):
                    for tb in range(2):
                        cs = slice(k * 512, k * 512 + 512)
                        x = tuple(t[:, 2 * j + k, tb * 128:tb * 128 + 128] for t in inT)
                        last = mm3(b[tb].t[:, :], x, (wh[:, cs], wl[:, cs]), j + k == 0, 2 * j + k == 7,
                                   tk, w[2 * j + k], b[tb].rel if j + k == 0 else None)
                wdone(i, last)
            return b, last

        def projT(inT, w, W, n, evac):
            for j in range(0, n, 2):
                b = bank()
                c = min(2, n - j)
                for q in range(c):
                    wh, wl, tk, i = wnext(W, j + q)
                    for k in range(8):
                        cs = slice(k * 128, k * 128 + 128)
                        last = mm3(b.t[:, q * 256:q * 256 + 256], (wh[:, cs], wl[:, cs]), tuple(t[:, k, :] for t in inT),
                                   k == 0, k == 7, tk, w[k], b.rel)
                    wdone(i, last)
                free(b, evac(b, j, c, last))

        def residual(out, base, inT, w, W, wb):
            r = [[], []]
            for g in range(2):
                b, last = proj512(inT, w, W, g)
                for tb in range(2):
                    op = vtt(out[:, tb, g * 512:g * 512 + 512], b[tb].t[:, :],
                             base[:, tb, g * 512:g * 512 + 512], ALU.add, last, wb)
                    free(b[tb], op)
                    r[tb].append(op)
            return r

        def softmax(S, n, w, M, L):
            k = S.shape[2]
            v = vred(M, S, ALU.max, w)
            yield
            v = vtt(S, S, bc(M, 2, k), ALU.subtract, v)
            yield
            a = act(S, S, ACT.Exp, v)
            yield
            return a, vred(L, S, ALU.add, a)

        def run(g):
            while True:
                try:
                    next(g)
                except StopIteration as e:
                    return e.value

        trig = sbuf(S_AD, "trig", [128, 2, 2, 24])
        ang = sbuf(S_AD, "ang", [128, 2, 2, 24])
        kq = sbuf(S_AD, "kq", [128, 2, 2, 24])
        posf = sbuf(S_AD, "posf", [128, 4])
        v = vcopy(posf[:, :], pos[:, :], t_pos)
        last = None
        for tr in range(2):
            for tb in range(2):
                for bl, lo, hi in ((0, 0, 8), (1, 8, 24)):
                    last = vts1(ang[:, tr, tb, lo:hi], D("invf")[:, lo:hi], posf[:, 2 * bl + tb:2 * bl + tb + 1],
                                ALU.mult, v, t_d)
        v = last
        two_pi = 2 * math.pi
        C1 = 6.28125
        C2 = float(np.float32(round((two_pi - C1) * 2 ** 20) / 2 ** 20))
        C3 = float(np.float32(two_pi - C1 - C2))
        MAGIC = 12582912.0
        vs_ = []
        for tr in range(2):
            vs_.append(vts(kq[:, tr, :, :], ang[:, tr, :, :], 1.0 / two_pi, 0.25 * tr, ALU.mult, ALU.add, v))
        v = vts1(kq[:, :, :, :], kq[:, :, :, :], MAGIC, ALU.add, vs_)
        v = vts1(kq[:, :, :, :], kq[:, :, :, :], MAGIC, ALU.subtract, v)
        fl = lambda t: t[:, :, :, :].rearrange("p a b c -> p (a b c)")
        for cc in (C1, C2, C3):
            v = vstt(fl(ang), fl(kq), -cc, fl(ang), ALU.mult, ALU.add, v)
        v = vts1(ang[:, 1, :, :], ang[:, 1, :, :], math.pi / 2, ALU.add, v)
        v = vts(fl(ang), fl(ang), 3.1415925, -3.1415925, ALU.min, ALU.max, v)
        t_trig = act(fl(trig), fl(ang), ACT.Sin, v)

        t_tmp = [None]

        def rope(x1, x2, cos, sin, tmp, w):
            n = x1.shape[1]
            c, s = bc(cos, 1, n), bc(sin, 1, n)
            a = vtt(tmp[0], x1, c, ALU.mult, w, t_trig, t_tmp[0])
            a = vtt(tmp[1], x2, s, ALU.mult, w)
            b = vtt(tmp[2], x2, c, ALU.mult, w)
            b = vtt(tmp[3], x1, s, ALU.mult, w)
            a = vtt(x1, tmp[0], tmp[1], ALU.subtract, a, b)
            t_tmp[0] = vtt(x2, tmp[2], tmp[3], ALU.add, b)
            return [a, t_tmp[0]]

        lam = sbuf(S_AD, "lam", [128, 8])
        lj = sbuf(S_AD, "lj", [128, 128])
        rl = lambda i: rows[:, 2240 + 64 * i:2304 + 64 * i]
        v1 = vtt(lj[:, 0:64], rl(0), rl(1), ALU.mult, t_rows)
        v2 = vtt(lj[:, 64:128], rl(2), rl(3), ALU.mult, t_rows)
        v = vred(lam[:, 0:2], lj[:, :].rearrange("p (a b) -> p a b", a=2), ALU.add, v1, v2)
        a = act(lam[:, 2:4], lam[:, 0:2], ACT.Exp, v)
        v = vtt(lam[:, 4:5], lam[:, 3:4], lam[:, 2:3], ALU.subtract, a)
        t_lam = vts1(lam[:, 5:6], lam[:, 4:5], -(0.8 - 0.6 * math.exp(0.0)), ALU.add, v)
        nlam = lam[:, 5:6]

        tbs = lambda t: [t[:, tb, :] for tb in range(2)]
        S = S_AD.sub()
        qk = sbuf(S, "qk", [128, 2, 1024])
        qkT = sbuf(S, "qkT", [128, 8, 256])
        va = sbuf(S, "va", [128, 2, 512])
        vs = sbuf(S, "vs", [128, 2, 512])
        sT = sbuf(S, "sT", [128, 8, 256])
        yhl = sbuf(S, "yhl", [128, 2, 8, 256], F32R)
        yT = (yhl[:, 0, :, :], yhl[:, 1, :, :])
        kmT = sbuf(S, "kmT", [128, 8, 256])
        vm = sbuf(S, "vm", [128, 2, 1024])
        S2 = S.sub()
        P0 = sbuf(S2, "P0", [128, 8, 128])
        P1 = qk[:, :, :].rearrange("p t n -> p (t n)").rearrange("p (a b) -> p a b", b=256)
        rt = P0[:, :, :].rearrange("p a b -> p (a b)").rearrange("p (i n d) -> p i n d", i=4, n=16)
        qkf = qkT[:, :, :].rearrange("p a b -> p (a b)").rearrange("p (a b) -> p a b", b=128)
        W1T, W0T = qkf[:, 0:8, :], qkf[:, 8:12, :]
        zs = sbuf(S2, "zs", [128, 3072])
        ez = sbuf(S2, "ez", [128, 3072])
        mlr = sbuf(S2, "mlr", [128, 2, 3, 8])
        xn4 = xn.rearrange("p t n -> p (t n)").rearrange("p (i t n) -> p i t n", i=2, t=2)
        od, osq = xn4[:, 0, :, :], xn4[:, 1, :, :]
        ost = sbuf(S2, "ost", [128, 2, 8])

        R = {}
        t_mem = load("act", hB[:, :, :], T["mem"].rearrange("(t p) d -> p t d", p=128))
        n_x = norm(tbs(hA), tbs(xn), [t_x, t_x])
        w_xT = to_T(tbs(xn), xT, 8, gcols("g_mix"), n_x)
        n_m = norm(tbs(hB), tbs(xn), [[t_mem, w_xT[-1]], [t_mem, w_xT[-1]]])
        t_qk = [[], []]
        for g in range(2):
            b, last = proj512(xT, w_xT, "w_in_a", g)
            for tb in range(2):
                op = copy(qk[:, tb, g * 512:g * 512 + 512], b[tb].t[:, :], last)
                free(b[tb], op)
                t_qk[tb].append(op)
        t_rope = []
        for tb in range(2):
            xv = qk[:, tb, :].rearrange("p (n d) -> p n d", d=64)
            t_rope.append(rope(xv[:, :, 0:8], xv[:, :, 8:16], trig[:, 1, tb, 0:8], trig[:, 0, tb, 0:8],
                               [rt[:, i, :, 0:8] for i in range(4)], t_qk[tb]))
        t_v = {}
        for g, dstt, nm in ((2, va, "va"), (3, vs, "vs")):
            b, last = proj512(xT, w_xT, "w_in_a", g)
            t_v[nm] = []
            for tb in range(2):
                op = copy(dstt[:, tb, :], b[tb].t[:, :], last)
                free(b[tb], op)
                t_v[nm].append(op)
        t_sT = [None] * 8

        def ev_sT(b, j, c, last):
            op = copy(sT[:, j:j + c, :], b.t[:, 0:c * 256].rearrange("p (a b) -> p a b", a=c), last)
            for q in range(c):
                t_sT[j + q] = op
            return op
        projT(xT, w_xT, "w_in_t", 8, ev_sT)

        def memory():
            w_mT = to_T(tbs(xn), yT, 8, gcols("g_mem"), n_m)
            R["nm"] = w_mT[-1]
            yield
            t_kmT = [None] * 8
            for j in range(0, 8, 2):
                b = bank()
                for q in range(2):
                    wh, wl, tk, i = wnext("w_xk", j + q)
                    for k in range(8):
                        cs = slice(k * 128, k * 128 + 128)
                        last = mm3(b.t[:, q * 256:q * 256 + 256], (wh[:, cs], wl[:, cs]), tuple(t[:, k, :] for t in yT),
                                   k == 0, k == 7, tk, w_mT[k], b.rel)
                    wdone(i, last)
                    if q == 0:
                        yield
                op = acopy(kmT[:, j:j + 2, :], b.t[:, :].rearrange("p (a b) -> p a b", a=2), last)
                free(b, op)
                t_kmT[j] = t_kmT[j + 1] = op
                yield
            t_vm = []
            for g in range(2):
                b = [bank(), bank()]
                for j in range(4):
                    wh, wl, tk, i = wnext("w_xv", g * 4 + j)
                    for k in range(2):
                        for tb in range(2):
                            cs = slice(k * 512, k * 512 + 512)
                            x = tuple(t[:, 2 * j + k, tb * 128:tb * 128 + 128] for t in yT)
                            last = mm3(b[tb].t[:, :], x, (wh[:, cs], wl[:, cs]), j + k == 0, 2 * j + k == 7,
                                       tk, w_mT[2 * j + k], b[tb].rel)
                    wdone(i, last)
                    if j < 3:
                        yield
                for tb in range(2):
                    op = acopy(vm[:, tb, g * 512:g * 512 + 512], b[tb].t[:, :], last)
                    free(b[tb], op)
                    t_vm.append(op)
                yield
            R["kmT"], R["vm"], R["km"] = t_kmT, t_vm, last

        t_yT = [None] * 8

        def seg(kb, r):
            return slice(r * 1024, r * 1024 + 1024) if kb == 0 else slice(2048 + r * 512, 2560 + r * 512)
        t_z = []
        for r in range(2):
            for hp in range(2):
                b = bank()
                for q in range(2):
                    i = hp * 2 + q
                    last = mm(b.t[:, q * 256:q * 256 + 256], sT[64 * r:64 * r + 64, 4 + i, 0:128],
                              sT[64 * r:64 * r + 64, i, :], True, True, b.rel, t_sT[i], t_sT[4 + i])
                op = vts1(zs[:, r * 1024 + hp * 512:r * 1024 + hp * 512 + 512], b.t[:, :], 0.125, ALU.mult, last)
                free(b, op)
                t_z.append(op)
            b = bank()
            for i in range(4):
                last = mm(b.t[:, i * 128:i * 128 + 128], sT[64 * r:64 * r + 64, 4 + i, 128:256],
                          sT[64 * r:64 * r + 64, i, 128:256], True, True, b.rel)
            op = vts1(zs[:, seg(1, r)], b.t[:, :], 0.125, ALU.mult, last)
            free(b, op)
            t_z.append(op)
        t_qkT = to_T32(tbs(qk), qkT, 8, t_rope)

        t_s1, t_s0 = [], []
        for c in range(2):
            rs = slice(64 * c, 64 * c + 64)
            for hp in range(2):
                b = bank()
                for q in range(2):
                    h = hp * 2 + q
                    last = mm(b.t[:, q * 256:q * 256 + 256], qkT[rs, h, 128:256], qkT[rs, 4 + h, :], True, True,
                              b.rel, t_qkT[h], t_qkT[4 + h])
                op = vstt(P1[:, c * 4 + hp * 2:c * 4 + hp * 2 + 2, :], b.t[:, :].rearrange("p (a b) -> p a b", a=2),
                          0.125, bc(D("maskA"), 1, 2), ALU.mult, ALU.add, last, t_d)
                free(b, op)
                t_s1.append(op)
            b = bank()
            for h in range(4):
                last = mm(b.t[:, h * 128:h * 128 + 128], qkT[rs, h, 0:128], qkT[rs, 4 + h, 0:128], True, True, b.rel)
            op = vstt(P0[:, c * 4:c * 4 + 4, :], b.t[:, :].rearrange("p (a b) -> p a b", a=4),
                      0.125, bc(D("maskA")[:, 128:256], 1, 4), ALU.mult, ALU.add, last)
            free(b, op)
            t_s0.append(op)
        def stick():
            a = act(ez[:, :], zs[:, :], ACT.Abs, t_z)
            yield
            a = act(ez[:, :], ez[:, :], ACT.Exp, a, scale=-1.0)
            yield
            a = act(ez[:, :], ez[:, :], ACT.Ln, a, bias=1.0)
            yield
            v = vstt(ez[:, :], zs[:, :], 0.0, ez[:, :], ALU.max, ALU.add, a)

            def diag(t, kb):
                if kb == 0:
                    return t[:, 0:2048].rearrange("p (h q) -> p h q", q=256)[:, :, 0:128]
                return t[:, 2048:3072].rearrange("p (h q) -> p h q", q=128)
            yield
            t_sp = [vtt(diag(ez, kb), diag(ez, kb), bc(D("maskS"), 1, 8), ALU.mult, v, t_d) for kb in range(2)]
            yield
            t_e = []
            for r in range(2):
                for hp in range(2):
                    b = bank()
                    o = r * 1024 + hp * 512
                    mm(b.t[:, :], D("negtri"), ez[:, o:o + 512], True, False, b.rel, t_sp)
                    o1 = 2048 + r * 512 + hp * 256
                    last = mm(b.t[:, :].rearrange("p (h q) -> p h q", q=256)[:, :, 128:256], D("negones"),
                              ez[:, o1:o1 + 256].rearrange("p (h q) -> p h q", q=128), False, True)
                    op = vtt(zs[:, o:o + 512], b.t[:, :], zs[:, o:o + 512], ALU.add, last)
                    free(b, op)
                    t_e.append(op)
                    yield
                b = bank()
                last = mm(b.t[:, :], D("negtri"), ez[:, seg(1, r)], True, True, b.rel)
                op = vtt(zs[:, seg(1, r)], b.t[:, :], zs[:, seg(1, r)], ALU.add, last)
                free(b, op)
                t_e.append(op)
            yield
            a = act(zs[:, :], zs[:, :], ACT.Exp, t_e)
            yield
            t_a = [vtt(diag(zs, kb), diag(zs, kb), bc(D("maskS"), 1, 8), ALU.mult, a) for kb in range(2)]
            yield "memory"
            for hp in range(2):
                b = bank()
                for q in range(2):
                    i = hp * 2 + q
                    for r in range(2):
                        h = 2 * i + r
                        o = b.t[64 * r:64 * r + 64, q * 256:q * 256 + 256]
                        mm(o, vs[:, 0, h * 64:h * 64 + 64], zs[:, r * 1024 + i * 256:r * 1024 + i * 256 + 256],
                           True, False, b.rel, t_a, t_v["vs"])
                        o1 = 2048 + r * 512 + i * 128
                        last = mm(o[:, 128:256], vs[:, 1, h * 64:h * 64 + 64], zs[:, o1:o1 + 128], False, True)
                op = evac_hl([t[:, 4 + hp * 2:6 + hp * 2, :] for t in yT], b.t[:, :].rearrange("p (a b) -> p a b", a=2), last, R["km"])
                free(b, op[1])
                yield
                t_yT[4 + hp * 2] = t_yT[5 + hp * 2] = op


        def differential():
            t_w = []
            for qb, Pq, w in ((0, P0, t_s0), (1, P1, t_s1)):
                k = Pq.shape[2]
                a, v = yield from softmax(Pq[:, :, :], 8, w, mlr[:, qb, 0, :], mlr[:, qb, 1, :])
                yield
                v = V(lambda e, qb=qb: e.reciprocal(mlr[:, qb, 2, :], mlr[:, qb, 1, :]), v)
                v = vts1(mlr[:, qb, 2, 4:8], mlr[:, qb, 2, 4:8], nlam, ALU.mult, v, t_lam)
                v = vtt(Pq[:, :, :], Pq[:, :, :], bc(mlr[:, qb, 2, :], 2, k), ALU.mult, v)
                yield
                t_w.append(vtt(Pq[:, 0:4, :], Pq[:, 0:4, :], Pq[:, 4:8, :], ALU.add, v))
            yield
            t_wT = []
            for j in range(2):
                b = bank()
                for q in range(4):
                    i = j * 4 + q
                    last = tp(b.t[:, q * 128:q * 128 + 128], P1[:, i // 2, (i % 2) * 128:(i % 2) * 128 + 128], b.rel, t_w[1])
                op = copy(W1T[:, j * 4:j * 4 + 4, :], b.t[:, :].rearrange("p (a b) -> p a b", a=4), last)
                free(b, op)
                t_wT.append(op)
                yield
            b = bank()
            for h in range(4):
                last = tp(b.t[:, h * 128:h * 128 + 128], P0[:, h, :], b.rel, t_w[0])
            op = copy(W0T[:, :, :], b.t[:, :].rearrange("p (a b) -> p a b", a=4), last)
            free(b, op)
            t_w0 = op
            t_on = []
            for qb in range(2):
                b = bank()
                for h in range(4):
                    hs = slice(h * 128, h * 128 + 128)
                    if qb == 0:
                        last = mm(b.t[:, hs], W0T[:, h, :], va[:, 0, hs], True, True, b.rel, t_w0, t_v["va"])
                    else:
                        mm(b.t[:, hs], W1T[:, h * 2, :], va[:, 0, hs], True, False, b.rel, t_wT, t_v["va"])
                        last = mm(b.t[:, hs], W1T[:, h * 2 + 1, :], va[:, 1, hs], False, True)
                v = vcopy(od[:, qb, :], b.t[:, :], last)
                free(b, v)
                v4 = lambda t: t[:, qb, :].rearrange("p (a b) -> p a b", a=4)
                yield
                q = vtt(osq[:, qb, :], od[:, qb, :], od[:, qb, :], ALU.mult, v)
                q = vred(ost[:, qb, 0:4], v4(osq), ALU.add, q)
                q = vts(ost[:, qb, 4:8], ost[:, qb, 0:4], 1.0 / 128, 1e-6, ALU.mult, ALU.add, q)
                q = rsqrt(ost[:, qb, 4:8], ost[:, qb, 4:8], q)
                q = vts1(ost[:, qb, 4:8], ost[:, qb, 4:8], 1.0 - (0.8 - 0.6 * math.exp(0.0)), ALU.mult, q)
                t_on.append(vtt(v4(od), v4(od), bc(ost[:, qb, 4:8], 2, 128), ALU.mult, q))
            R["on"] = t_on

        mem_ = memory()
        next(mem_)
        sides = [stick(), differential()]
        held = set()
        for _ in mem_:
            for g in sides:
                if g not in held and next(g, "memory") == "memory":
                    held.add(g)
        for g in sides:
            for _ in g:
                pass
        t_on = R["on"]
        t_yT[0:4] = to_T(tbs(od), yT, 4, gcols("g_subln") * 4, t_on, R["km"])
        t_h1 = residual(hB, hA, yT, t_yT, "w_out", t_x)
        if stop == 1:
            return finish(nc, Q, sems, ctx, outs, hB, t_h1, load)

        SB = S.sub()
        PX = sbuf(SB, "PX", [128, 2, 4, 256])
        PXT = sbuf(SB, "PXT", [128, 2, 4, 256])
        mx = sbuf(SB, "mx", [128, 2, 3, 4])
        t_kmT, t_vm = R["kmT"], R["vm"]
        n_h = norm(tbs(hB), tbs(xn), t_h1)
        w_xT = to_T(tbs(xn), xT, 8, gcols("g_cross"), n_h)
        t_sT = [None] * 8
        projT(xT, w_xT, "w_xq", 8, ev_sT)
        t_pT = []
        t_p = []
        for tb in range(2):
            ts = slice(tb * 128, tb * 128 + 128)
            sc = []
            for hp in range(2):
                b = bank()
                for q in range(2):
                    h = hp * 2 + q
                    for k in range(2):
                        last = mm(b.t[:, q * 256:q * 256 + 256], sT[:, 2 * h + k, ts], kmT[:, 2 * h + k, :], k == 0, k == 1,
                                  b.rel, t_sT, t_kmT)
                op = vts1(PX[:, tb, hp * 2:hp * 2 + 2, :], b.t[:, :].rearrange("p (a b) -> p a b", a=2), 1.0 / 16, ALU.mult, last)
                free(b, op)
                sc.append(op)
            a, v = run(softmax(PX[:, tb, :, :], 4, sc, mx[:, tb, 0, :], mx[:, tb, 1, :]))
            v = V(lambda e, tb=tb: e.reciprocal(mx[:, tb, 2, :], mx[:, tb, 1, :]), v)
            t_p.append(vtt(PX[:, tb, :, :], PX[:, tb, :, :], bc(mx[:, tb, 2, :], 2, 256), ALU.mult, v))
        for tb in range(2):
            for kb in range(2):
                b = bank()
                for h in range(4):
                    last = tp(b.t[:, h * 128:h * 128 + 128], PX[:, tb, h, kb * 128:kb * 128 + 128], b.rel, t_p[tb])
                op = copy(PXT[:, kb, :, tb * 128:tb * 128 + 128], b.t[:, :].rearrange("p (a b) -> p a b", a=4), last)
                free(b, op)
                t_pT.append(op)
        t_oT = []
        for j in range(4):
            b = bank()
            for q in range(2):
                n = 2 * j + q
                for kb in range(2):
                    last = mm(b.t[:, q * 256:q * 256 + 256], vm[:, kb, n * 128:n * 128 + 128], PXT[:, kb, j, :], kb == 0, kb == 1,
                              b.rel, t_vm, t_pT)
            op = evac_hl([t[:, 2 * j:2 * j + 2, :] for t in yT], b.t[:, :].rearrange("p (a b) -> p a b", a=2), last)
            free(b, op[1])
            t_oT += [op, op]
        t_h2 = residual(hA, hB, yT, t_oT, "w_xo", t_h1)
        if stop == 2:
            return finish(nc, Q, sems, ctx, outs, hA, t_h2, load)

        SC = S_AD.sub()
        ahl = sbuf(SC, "ahl", [128, 2, 32, 256], F32R)
        ar = sbuf(SC, "ar", [128, 2, 2, 256])
        as_ = sbuf(SC, "as_", [128, 2, 2, 256])
        n_h = norm(tbs(hA), tbs(xn), t_h2)
        w_xT = to_T(tbs(xn), xT, 8, gcols("g_mlp"), n_h)
        t_aT = [None] * 32

        def ev_up(b, j, c, last):
            u = j // 2 % 2
            w = t_aT[j - 4] if j >= 4 else None
            a = act(ar[:, u, :, :], b.t[:, :].rearrange("p (a b) -> p a b", a=2), ACT.Relu, last, w)
            v = vtt(as_[:, u, :, :], ar[:, u, :, :], ar[:, u, :, :], ALU.mult, a, w)
            h, l = (ahl[:, q, j:j + 2, :] for q in range(2))
            c_ = acopy(h, as_[:, u, :, :], v)
            t_aT[j] = t_aT[j + 1] = [c_, vtt(l, as_[:, u, :, :], h.bitcast(F32), ALU.subtract, c_)]
            return a
        projT(xT, w_xT, "w_up", 32, ev_up)
        bb = [bank() for _ in range(4)]
        for k in range(32):
            wh, wl, tk, i = wnext("w_down", k)
            for tb in range(2):
                for g in range(2):
                    b = bb[tb * 2 + g]
                    cs = slice(g * 512, g * 512 + 512)
                    last = mm3(b.t[:, :], tuple(ahl[:, q, k, tb * 128:tb * 128 + 128] for q in range(2)), (wh[:, cs], wl[:, cs]),
                               k == 0, k == 31, b.rel, tk, t_aT[k])
            wdone(i, last)
        t_h3 = [[], []]
        for tb in range(2):
            for g in range(2):
                gs = slice(g * 512, g * 512 + 512)
                op = vtt(hB[:, tb, gs], bb[tb * 2 + g].t[:, :], hA[:, tb, gs], ALU.add, last)
                free(bb[tb * 2 + g], op)
                t_h3[tb].append(op)
        t_x2 = []
        for tb in range(2):
            s, v = rstd(hB[:, tb, :], 1024, t_h3[tb])
            t_x2.append(vstt(hA[:, tb, :], hB[:, tb, :], s, rows[:, 0:1024], ALU.mult, ALU.mult, v, t_rows))
        if stop == 3:
            return finish(nc, Q, sems, ctx, outs, hA, t_x2, load)

        SD = S_AD.sub()
        n_h = norm(tbs(hA), tbs(xn), t_x2)
        w_xT = to_T(tbs(xn), xT, 8, gcols("g_mix_2"), n_h)
        yA = sbuf(SD, "yA", [128, 2, 512])
        pR = sbuf(SD, "pR", [128, 14, 257])
        SM = SD.sub()
        cq = sbuf(SM, "cq", [128, 2, 672])
        cn = sbuf(SM, "cn", [128, 2, 640])
        chl = sbuf(SM, "chl", [128, 2, 5, 256], F32R)
        cT = (chl[:, 0, :, :], chl[:, 1, :, :])
        QK = sbuf(SM, "QK", [128, 2, 2, 8, 96])
        QKs = sbuf(SM, "QKs", [128, 2, 2, 8, 96])
        qst = sbuf(SM, "qst", [128, 2, 2, 16])
        vM = sbuf(SM, "vM", [128, 2, 512])
        qT2 = sbuf(SM, "qT2", [96, 2, 8, 256])
        cnf = cn[:, :, :].rearrange("p t n -> p (t n)")
        rt2 = cnf[:, 0:1024].rearrange("p (i n d) -> p i n d", i=4, n=16)
        QKf = lambda t: t[:, :, :, :, :].rearrange("p t j h d -> p (t j h d)")
        M1 = QKf(QKs)[:, 0:2048].rearrange("p (h k) -> p h k", h=8)
        M0 = QKf(QKs)[:, 2048:3072].rearrange("p (h k) -> p h k", h=8)
        MT1 = QKf(QK)[:, 0:2048].rearrange("p (h k q) -> p h k q", h=8, k=2)
        MT0 = QKf(QK)[:, 2048:3072].rearrange("p (h q) -> p h q", h=8)
        mst = sbuf(SM, "mst", [128, 2, 3, 8])

        bq = [bank() for _ in range(4)]
        for k in range(8):
            wh, wl, tk, i = wnext("w_mla", k)
            for tb in range(2):
                xs = tuple(t[:, k, tb * 128:tb * 128 + 128] for t in xT)
                mm3(bq[tb].t[:, 0:384], xs, (wh[:, 0:384], wl[:, 0:384]), k == 0, k == 7, bq[tb].rel, tk, w_xT[k])
                last = mm3(bq[2 + tb].t[:, 0:288], xs, (wh[:, 384:672], wl[:, 384:672]), k == 0, k == 7, bq[2 + tb].rel)
            wdone(i, last)
        t_cq = [[], []]
        for tb in range(2):
            for j, lo, hi in ((0, 0, 384), (1, 384, 672)):
                b = bq[2 * j + tb]
                op = copy(cq[:, tb, lo:hi], b.t[:, 0:hi - lo], last)
                free(b, op)
                t_cq[tb].append(op)
        n_q = norm([cq[:, tb, 0:384] for tb in range(2)], [cn[:, tb, 0:384] for tb in range(2)], t_cq)
        n_kv = norm([cq[:, tb, 384:640] for tb in range(2)], [cn[:, tb, 384:640] for tb in range(2)], t_cq)
        w_cT = to_T(tbs(cn), cT, 5, gcols("g_cq") + gcols("g_ckv"), [[n_q[tb], n_kv[tb]] for tb in range(2)])
        t_mz = V(lambda e: e.memset(pR[:, :, 0:1], 0.0), t_x2)
        t_pR = []

        def ev_p(b, j, c, last):
            op = copy(pR[:, j:j + c, 1:257], b.t[:, :].rearrange("p (a b) -> p a b", a=2), last)
            t_pR.append(op)
            return op
        projT(xT, w_xT, "w_rwkv", 14, ev_p)
        bq = [bank() for _ in range(4)]
        for k in range(3):
            wh, wl, tk, i = wnext("w_uq", k)
            for tb in range(2):
                xs = tuple(t[:, k, tb * 128:tb * 128 + 128] for t in cT)
                mm3(bq[tb].t[:, 0:480], xs, (wh[:, 0:480], wl[:, 0:480]), k == 0, k == 2, bq[tb].rel, tk, w_cT[k])
                last = mm3(bq[2 + tb].t[:, 0:288], xs, (wh[:, 480:768], wl[:, 480:768]), k == 0, k == 2, bq[2 + tb].rel)
            wdone(i, last)
        t_q = [[], []]
        for tb in range(2):
            for j, lo, hi in ((0, 0, 5), (1, 5, 8)):
                b = bq[2 * j + tb]
                op = copy(QK[:, tb, 0, lo:hi, :], b.t[:, 0:(hi - lo) * 96].rearrange("p (a b) -> p a b", b=96), last)
                free(b, op)
                t_q[tb].append(op)
        bq = [bank() for _ in range(4)]
        for k in range(2):
            wh, wl, tk, i = wnext("w_ukv", k)
            for tb in range(2):
                xs = tuple(t[:, 3 + k, tb * 128:tb * 128 + 128] for t in cT)
                mm3(bq[tb].t[:, :], xs, (wh[:, 0:512], wl[:, 0:512]), k == 0, k == 1, bq[tb].rel, tk, w_cT[3 + k])
                last = mm3(bq[2 + tb].t[:, :], xs, (wh[:, 512:1024], wl[:, 512:1024]), k == 0, k == 1, bq[2 + tb].rel)
            wdone(i, last)
        t_vM = []
        for tb in range(2):
            op = copy(QK[:, tb, 1, :, 0:64], bq[tb].t[:, :].rearrange("p (a b) -> p a b", b=64), last)
            free(bq[tb], op)
            t_q[tb].append(op)
            op = copy(vM[:, tb, :], bq[2 + tb].t[:, :], last)
            free(bq[2 + tb], op)
            t_vM.append(op)
            t_q[tb].append(G(lambda e, tb=tb: e.tensor_copy(QK[:, tb, 1, :, 64:96], bc(cq[:, tb, 640:672], 1, 8)), t_cq[tb]))
        t_qT = []
        for tb in range(2):
            h16 = lambda t: t[:, tb, :, :, :].rearrange("p a b c -> p (a b) c")
            v = vtt(h16(QKs), h16(QK), h16(QK), ALU.mult, t_q[tb])
            v = vred(qst[:, tb, 0, :], h16(QKs), ALU.add, v)
            v = vts(qst[:, tb, 1, :], qst[:, tb, 0, :], 1.0 / 96, 1e-6, ALU.mult, ALU.add, v)
            v = rsqrt(qst[:, tb, 1, :], qst[:, tb, 1, :], v)
            v = vtt(h16(QK), h16(QK), bc(qst[:, tb, 1, :], 2, 96), ALU.mult, v)
            v = [vtt(QK[:, tb, j, :, :], QK[:, tb, j, :, :], bc(rows[:, 2048 + 96 * j:2144 + 96 * j], 1, 8), ALU.mult, v, t_rows)
                 for j in range(2)]
            v = rope(h16(QK)[:, :, 64:80], h16(QK)[:, :, 80:96], trig[:, 1, tb, 8:24], trig[:, 0, tb, 8:24],
                     [rt2[:, i, :, :] for i in range(4)], v)
            for j in range(2):
                for hp in range(2):
                    b = bank()
                    for q in range(4):
                        last = tp(b.t[0:96, q * 128:q * 128 + 128], QK[:, tb, j, hp * 4 + q, :], b.rel, v)
                    op = copy(qT2[:, j, hp * 4:hp * 4 + 4, tb * 128:tb * 128 + 128],
                              b.t[0:96, :].rearrange("p (a b) -> p a b", a=4), last)
                    free(b, op)
                    t_qT.append(op)
        isq = 96 ** -0.5
        t_m1, t_m0 = [], []
        for hp in range(4):
            b = bank()
            for q in range(2):
                h = hp * 2 + q
                last = mm(b.t[:, q * 256:q * 256 + 256], qT2[:, 0, h, 128:256], qT2[:, 1, h, :], True, True, b.rel, t_qT)
            op = vstt(M1[:, hp * 2:hp * 2 + 2, :], b.t[:, :].rearrange("p (a b) -> p a b", a=2), isq,
                      bc(D("maskM"), 1, 2), ALU.mult, ALU.add, last)
            free(b, op)
            t_m1.append(op)
        for hp in range(2):
            b = bank()
            for q in range(4):
                h = hp * 4 + q
                last = mm(b.t[:, q * 128:q * 128 + 128], qT2[:, 0, h, 0:128], qT2[:, 1, h, 0:128], True, True, b.rel, t_qT)
            op = vstt(M0[:, hp * 4:hp * 4 + 4, :], b.t[:, :].rearrange("p (a b) -> p a b", a=4), isq,
                      bc(D("maskM")[:, 128:256], 1, 4), ALU.mult, ALU.add, last)
            free(b, op)
            t_m0.append(op)
        t_sm, t_l = [], []
        for qb, Mq, w in ((0, M0, t_m0), (1, M1, t_m1)):
            a, v = run(softmax(Mq[:, :, :], 8, w, mst[:, qb, 0, :], mst[:, qb, 1, :]))
            t_sm.append(a)
            t_l.append(V(lambda e, qb=qb: e.reciprocal(mst[:, qb, 2, :], mst[:, qb, 1, :]), v))
        t_mT = [[], []]
        for j in range(2):
            b = bank()
            for q in range(4):
                last = tp(b.t[:, q * 128:q * 128 + 128], M0[:, j * 4 + q, :], b.rel, t_sm[0])
            op = copy(MT0[:, j * 4:j * 4 + 4, :], b.t[:, :].rearrange("p (a b) -> p a b", a=4), last)
            free(b, op)
            t_mT[0].append(op)
        for j in range(4):
            b = bank()
            for q in range(4):
                h, kb = j * 2 + q // 2, q % 2
                last = tp(b.t[:, q * 128:q * 128 + 128], M1[:, h, kb * 128:kb * 128 + 128], b.rel, t_sm[1])
            op = copy(MT1[:, j * 2:j * 2 + 2, :, :], b.t[:, :].rearrange("p (a k b) -> p a k b", a=2, k=2), last)
            free(b, op)
            t_mT[1].append(op)
        t_ya = []
        for qb in range(2):
            b = bank()
            for h in range(8):
                hs = slice(h * 64, h * 64 + 64)
                if qb == 0:
                    last = mm(b.t[:, hs], MT0[:, h, :], vM[:, 0, hs], True, True, b.rel, t_mT[0], t_vM)
                else:
                    mm(b.t[:, hs], MT1[:, h, 0, :], vM[:, 0, hs], True, False, b.rel, t_mT[1], t_vM)
                    last = mm(b.t[:, hs], MT1[:, h, 1, :], vM[:, 1, hs], False, True)
            o = yA[:, qb, :].rearrange("p (a b) -> p a b", a=8)
            v = vtt(o, b.t[:, :].rearrange("p (a b) -> p a b", a=8), bc(mst[:, qb, 2, :], 2, 64), ALU.mult, last, t_l)
            free(b, v)
            js = junk[:, qb * 512:qb * 512 + 512].rearrange("p (a b) -> p a b", a=8)
            q = vtt(js, o, o, ALU.mult, v, n_kv)
            q = vred(mst[:, qb, 0, :], js, ALU.add, q)
            q = vts(mst[:, qb, 1, :], mst[:, qb, 0, :], 1.0 / 64, 1e-6, ALU.mult, ALU.add, q)
            q = rsqrt(mst[:, qb, 1, :], mst[:, qb, 1, :], q)
            t_ya.append(vtt(o, o, bc(mst[:, qb, 1, :], 2, 64), ALU.mult, q))
        SR = SD.sub()
        pm = sbuf(SR, "pm", [128, 14, 256])
        prep_at = SR.at
        prep = sbuf(SR, "prep", [128, 5, 4, 256])
        ld, aa, cum, t0, t1 = (prep[:, i, :, :] for i in range(5))
        Pc = sbuf(SR, "Pc", [128, 4, 256])
        ARt = sbuf(SR, "ARt", [128, 4, 2, 256])
        be = sbuf(SR, "be", [128, 4, 256])
        ka = sbuf(SR, "ka", [128, 4, 256])
        atok = sbuf(SR, "atok", [128, 2, 512])
        btok = sbuf(SR, "btok", [128, 2, 512])
        ktok = sbuf(SR, "ktok", [128, 2, 512])
        vtok = sbuf(SR, "vtok", [128, 2, 512])
        gtok = rows[:, 0:1024].rearrange("p (t n) -> p t n", t=2)
        bon = sbuf(SR, "bon", [128, 16])
        mu = gcols("rwkv_mu")
        v = vtt(pm[:, :, :], pR[:, :, 0:256], pR[:, :, 1:257], ALU.subtract, t_pR, t_mz)
        t_pm = [vstt(pm[:, i, :], pm[:, i, :], mu[i], pR[:, i, 1:257], ALU.mult, ALU.add, v) for i in range(14)]
        sg = pR[:, 0, 0:256]
        wt, _, t_lw, i_lw = wnext("w_lora", 0)
        w2s, a2s, g2s = wt[0:64, 0:512], wt[64:128, 0:512], wt[:, 512:1024]
        t_tw = act(t0[0:64, 0, :], pm[0:64, 12, :], ACT.Tanh, t_pm)
        t_sg = act(sg[:, :], pm[:, 13, :], ACT.Sigmoid, t_pm)
        t_ld, t_aa = [], []
        for j in range(2):
            b = bank()
            for q in range(2):
                i = 2 * j + q
                last = mm(b.t[:, q * 256:q * 256 + 256], w2s[:, i * 128:i * 128 + 128], t0[0:64, 0, :], True, True,
                          b.rel, t_lw, t_tw)
            for q in range(2):
                i = 2 * j + q
                op = act(ld[:, i, :], b.t[:, q * 256:q * 256 + 256], ACT.Sigmoid, last, bias=gcols("w0")[i])
                t_ld.append(op)
            free(b, op)
        for j in range(2):
            b = bank()
            for q in range(2):
                i = 2 * j + q
                last = mm(b.t[:, q * 256:q * 256 + 256], a2s[:, i * 128:i * 128 + 128], pm[64:128, 12, :], True, True,
                          b.rel, t_lw, t_pm)
            for q in range(2):
                i = 2 * j + q
                op = act(aa[:, i, :], b.t[:, q * 256:q * 256 + 256], ACT.Sigmoid, last, bias=gcols("a0")[i])
                t_aa.append(op)
            free(b, op)
        t_g = []
        for tb in range(2):
            b = bank()
            last = mm(b.t[:, :], sg[:, tb * 128:tb * 128 + 128], g2s, True, True, b.rel, t_sg)
            op = acopy(gtok[:, tb, :], b.t[:, :], last)
            free(b, op)
            t_g.append(op)
        wdone(i_lw, last)
        v = vts1(ld[:, :, :], ld[:, :, :], -math.exp(-0.5), ALU.mult, t_ld)
        f2 = lambda t: t[:, :, :].rearrange("p a b -> p (a b)")
        t_cum = []
        for i in range(4):
            t_cum.append(V(lambda e, i=i: e.tensor_tensor_scan(cum[:, i, :], D("rst"), ld[:, i, :], 0.0, ALU.mult, ALU.add), v))
        kkc, kac, rkc = gcols("k_k"), gcols("k_a"), gcols("r_k")
        vk = [vts1(t1[:, i, :], pm[:, 4 + i, :], kkc[i], ALU.mult, t_pm) for i in range(4)]
        v = vtt(f2(be), f2(t1), f2(t1), ALU.mult, vk)
        t_rn = []
        ld2 = pR[:, :, :].rearrange("p a b -> p (a b)")[:, 512:1536].rearrange("p (a b) -> p a b", b=256)
        for j in range(2):
            b = bank()
            last = mm(b.t[:, :], D("blk"), be[:, 2 * j:2 * j + 2, :], True, True, b.rel, v)
            x2 = ld2[:, 2 * j:2 * j + 2, :]
            op = vts1(x2, b.t[:, :].rearrange("p (a b) -> p a b", a=2), 1e-24, ALU.max, last)
            free(b, op)
            y = ka[:, 2 * j:2 * j + 2, :]
            z = be[:, 2 * j:2 * j + 2, :]
            q = act(y, x2, ACT.Sqrt, op)
            q = V(lambda e, y=y: e.reciprocal(y, y), q)
            r_ = vtt(z, y, y, ALU.mult, q, last)
            r_ = vtt(z, z, x2, ALU.mult, r_, op)
            r_ = vts(z, z, -0.5, 1.5, ALU.mult, ALU.add, r_)
            t_rn.append(vtt(y, y, z, ALU.mult, r_))
        t_kk = vtt(f2(t1), f2(t1), f2(ka), ALU.mult, t_rn)
        t_P = act(Pc[:, :, :], cum[:, :, :], ACT.Exp, t_cum)
        v = vtt(ld[:, :, :], cum[:, :, :], ld[:, :, :], ALU.subtract, t_cum)
        t_Pp = act(ld[:, :, :], ld[:, :, :], ACT.Exp, v)
        t_Pi = act(cum[:, :, :], cum[:, :, :], ACT.Exp, t_P, v, scale=-1.0)
        t_al = vtt(ARt[:, :, 0, :], t1[:, :, :], ld[:, :, :], ALU.mult, t_kk, t_Pp)
        t_rho = vtt(ARt[:, :, 1, :], pm[:, 0:4, :], Pc[:, :, :], ALU.mult, t_P)
        v = vtt(f2(be), f2(t1), f2(aa), ALU.mult, t_kk, t_aa, last)
        t_be = vtt(f2(be), f2(be), f2(cum), ALU.mult, v, t_Pi)
        vk = [vts(t1[:, i, :], aa[:, i, :], 1.0, kac[i], ALU.subtract, ALU.mult, t_be, t_al) for i in range(4)]
        t_kp = vstt(f2(t1), f2(t1), 1.0, pm[:, 4:8, :].rearrange("p a b -> p (a b)"), ALU.add, ALU.mult, vk)
        t_ka = vtt(f2(ka), f2(t1), f2(cum), ALU.mult, t_kp, t_Pi)
        vk = [vstt(t0[:, i, :], pm[:, i, :], rkc[i], t1[:, i, :], ALU.mult, ALU.mult, t_kp, t_ld) for i in range(4)]
        b = bank()
        for tb in range(2):
            for i in range(4):
                last = mm(b.t[:, tb * 8 + 2 * i:tb * 8 + 2 * i + 2], t0[:, i, tb * 128:tb * 128 + 128], D("hsel"), True, True, b.rel, vk)
        t_bon = vcopy(bon[:, :], b.t[:, 0:16], last)
        free(b, t_bon)
        t_tok = {}
        for nm, src, dt_, w in (("v", pm[:, 8:12, :], vtok, t_pm), ("a", ARt[:, :, 0, :], atok, t_al),
                                ("b", be[:, :, :], btok, t_be), ("k", ka[:, :, :], ktok, t_ka)):
            t_tok[nm] = []
            for tb in range(2):
                b = bank()
                for i in range(4):
                    last = tp(b.t[:, i * 128:i * 128 + 128], src[:, i, tb * 128:tb * 128 + 128], b.rel, w)
                op = copy(dt_[:, tb, :], b.t[:, :], last)
                free(b, op)
                t_tok[nm].append(op)

        SI = SR.sub()
        GB = hx[:, :, :, :].rearrange("p i t n -> p (i t n)").rearrange("p (n d) -> p n d", d=256)
        GK = prep[:, 0:4, :, :].rearrange("p a b c -> p (a b) c")
        xm = Mem(nc, x_at, P.end)
        ysq, TAT, nU = xm("ysq", [128, 16, 64]), xm("TAT", [128, 4, 256]), xm("nU", [128, 2, 512])
        Y = sbuf(SI, "rwY", [128, 16, 128])
        t_Y0 = G(lambda e: e.memset(Y[:, :, :], 0.0), t_ya)
        pRf = pR[:, :, :].rearrange("p a b -> p (a b)")
        pmf = pm[:, 0:8, :].rearrange("p a b -> p (a b)")
        c64 = lambda t, k: t[:, 1024 * k:1024 * k + 1024].rearrange("p (n d) -> p n d", d=64)
        QX, Xc, Yc = c64(pRf, 0), c64(pmf, 0), c64(pmf, 1)
        prob = lambda b_, r, i: (b_ * 2 + r) * 4 + i
        t_GB, t_GK = [], []
        for kind in range(2):
            for b_ in range(2):
                ts = slice(b_ * 128, b_ * 128 + 128)
                for r in range(2):
                    rs = slice(64 * r, 64 * r + 64)
                    for hp in range(2):
                        b = bank()
                        for q in range(2):
                            i = hp * 2 + q
                            src, w = ((be, t_be), (ka, t_ka))[kind]
                            last = mm(b.t[:, q * 256:q * 256 + 256].rearrange("p (a b) -> p a b", a=2), src[rs, i, ts],
                                      ARt[rs, i, :, ts], True, True, b.rel, w, t_al, t_rho)
                        p0 = prob(b_, r, hp * 2)
                        op = vtt((GB, GK)[kind][:, p0:p0 + 2, :], b.t[:, :].rearrange("p (a b) -> p a b", a=2),
                                 bc(D("m2"), 1, 2), ALU.mult, last)
                        free(b, op)
                        (t_GB, t_GK)[kind].append(op)
        halves = [slice(64 * c, 64 * c + 64) for c in range(2)]
        t_Xc, t_Yc = [None, None], [None, None]
        for j in range(2):
            js = slice(8 * j, 8 * j + 8)
            v = [vstt(Yc[hs, js, :], GB[hs, js, 64 * c:64 * c + 64], -1.0, bc(D("ly0")[hs, :], 1, 8), ALU.mult, ALU.mult,
                      t_GB, t_bon, t_rho) for c, hs in enumerate(halves)]
            t_Yc[j] = vtt(Yc[:, js, :], Yc[:, js, :], bc(D("eye2"), 1, 8), ALU.add, v)
            t_Xc[j] = V(lambda e, js=js: e.transpose(Xc[:, js, :].rearrange("p a b -> p (a b)"),
                                                     Yc[:, js, :].rearrange("p a b -> p (a b)")), t_Yc[j], t_bon)

        def quads(j, lt, rt, *w):
            bs = [bank(), bank()]
            for q in range(8):
                for c, hs in enumerate(halves):
                    last = mm(bs[c].t[hs, q * 64:q * 64 + 64], lt(c, hs, 8 * j + q), rt(hs, 8 * j + q), True, True, bs[c].rel, *w)
            return bs, last

        pv = lambda b, hs: b.t[hs, :].rearrange("p (a b) -> p a b", a=8)
        t_use = [None, None]
        for l in range(1, 6):
            t_Q = [None, None]
            for j in range(2):
                js = slice(8 * j, 8 * j + 8)
                bs, last = quads(j, lambda c, hs, p: GB[hs, p, 64 * c:64 * c + 64], lambda hs, p: Xc[hs, p, :], t_Xc[j], t_GB)
                t_Q[j] = []
                for c, hs in enumerate(halves):
                    op = vtt(QX[hs, js, :], pv(bs[c], hs), bc(D(f"lx{l}")[hs, :], 1, 8), ALU.mult, last, t_use[j], t_rn, t_g)
                    free(bs[c], op)
                    t_Q[j].append(op)
            for j in range(2):
                js = slice(8 * j, 8 * j + 8)
                if l < 5:
                    M, (bs, last) = Xc, quads(j, lambda c, hs, p: Yc[hs, p, :], lambda hs, p: QX[hs, p, :], t_Yc[j], t_Q[j])
                else:
                    M, (bs, last) = Yc, quads(j, lambda c, hs, p: QX[hs, p, :], lambda hs, p: Yc[hs, p, :], t_Yc[j], t_Q[j])
                t_use[j] = last
                v = []
                for c, hs in enumerate(halves):
                    v.append(vtt(M[hs, js, :], M[hs, js, :], pv(bs[c], hs), ALU.subtract, last, t_Xc[j], t_Yc[j]))
                    free(bs[c], v[-1])
                if l < 5:
                    t_Xc[j] = v
                    t_Yc[j] = V(lambda e, js=js: e.transpose(Yc[:, js, :].rearrange("p a b -> p (a b)"),
                                                             Xc[:, js, :].rearrange("p a b -> p (a b)")), v)
                else:
                    t_Yc[j] = v
        t_inv = t_use[1]
        t_Y = [t_Y0, acopy(Y[0:64, :, 0:64], Yc[0:64, :, :], t_Yc, t_Y0), vcopy(Y[64:128, :, 64:128], Yc[64:128, :, :], t_Yc, t_Y0)]
        MV, Ut = (pRf[:, 1024 * k:1024 * k + 1024].rearrange("p (t n) -> p t n", t=2) for k in range(2))
        t_MV, t_Ut, t_TA = [], [], []
        for b_ in range(2):
            b = bank()
            for h in range(8):
                p = prob(b_, h % 2, h // 2)
                last = mm(b.t[:, h * 64:h * 64 + 64], GK[:, p, 0:128], vtok[:, b_, h * 64:h * 64 + 64], True, True,
                          b.rel, t_GK, t_tok["v"])
            op = vcopy(MV[:, b_, :], b.t[:, :], last, t_inv)
            free(b, op)
            t_MV.append(op)
        for b_ in range(2):
            b = bank()
            for h in range(8):
                p = prob(b_, h % 2, h // 2)
                last = mm(b.t[:, h * 64:h * 64 + 64], Y[:, p, :], MV[:, b_, h * 64:h * 64 + 64], True, True, b.rel, t_Y, t_MV)
            op = vts1(Ut[:, b_, :], b.t[:, :], -1.0, ALU.mult, last, t_inv)
            free(b, op)
            t_Ut.append(op)
        for j in range(2):
            b = bank()
            for q in range(2):
                i = 2 * j + q
                for b_ in range(2):
                    for r in range(2):
                        h = 2 * i + r
                        last = mm(b.t[64 * r:64 * r + 64, q * 256 + b_ * 128:q * 256 + b_ * 128 + 128],
                                  atok[:, b_, h * 64:h * 64 + 64], Y[:, prob(b_, r, i), :], True, True, b.rel, t_Y, t_tok["a"])
            op = vcopy(TAT[:, 2 * j:2 * j + 2, :], b.t[:, :].rearrange("p (a b) -> p a b", a=2), last, t_inv)
            free(b, op)
            t_TA.append(op)
        ST = pRf[:, 2048:3328].rearrange("p (c i d) -> p c i d", c=5, i=4)
        yB = t1.rearrange("p a b -> p (a b)").rearrange("p (t n) -> p t n", t=2)
        yr = junk[:, :].rearrange("p (t n) -> p t n", t=2)
        yst = sbuf(SI, "yst", [128, 3, 16])
        t_S = V(lambda e: e.memset(ST[:, 0, :, :], 0.0))
        t_nU = []
        t_yr = [[], []]
        for b_ in range(2):
            by = [bank(), bank()]
            for hf in range(2):
                c = 2 * b_ + hf
                ps = slice(64 * hf, 64 * hf + 64)
                cs = slice(64 * c, 64 * c + 64)
                bu = [bank(), bank()]
                for r in range(2):
                    rs = slice(64 * r, 64 * r + 64)
                    for i in range(4):
                        last = mm(bu[r].t[ps, i * 64:i * 64 + 64], TAT[rs, i, cs], ST[rs, c, i, :], True, True,
                                  bu[r].rel, t_TA, t_S)
                    hv = lambda t: t[ps, b_, :].rearrange("p (i r d) -> p i r d", r=2, d=64)[:, :, r, :]
                    op = vtt(hv(nU), hv(Ut), bu[r].t[ps, 0:256].rearrange("p (i d) -> p i d", d=64), ALU.subtract, last, t_Ut, t_inv)
                    free(bu[r], op)
                    t_nU.append(op)
                    for i in range(4):
                        ly = mm(by[r].t[ps, i * 64:i * 64 + 64], ARt[rs, i, 1, cs], ST[rs, c, i, :], True, True, by[r].rel, t_S)
                b = bank()
                for r in range(2):
                    rs = slice(64 * r, 64 * r + 64)
                    for i in range(4):
                        hs = slice((2 * i + r) * 64, (2 * i + r) * 64 + 64)
                        o = b.t[rs, i * 64:i * 64 + 64]
                        mm(o, ktok[ps, b_, hs], vtok[ps, b_, hs], True, False, b.rel, t_tok["k"], t_tok["v"])
                        last = mm(o, btok[ps, b_, hs], nU[ps, b_, hs], False, True, t_tok["b"], t_nU)
                v = vtt(ST[:, c + 1, :, :], b.t[:, 0:256].rearrange("p (i d) -> p i d", d=64), ST[:, c, :, :], ALU.add, last, t_S)
                free(b, v)
                t_S = vtt(ST[:, c + 1, :, :], ST[:, c + 1, :, :], bc(Pc[:, :, 64 * c + 63], 2, 64), ALU.mult, v)
            for r in range(2):
                hv = lambda t: t[:, b_, :].rearrange("p (i r d) -> p i r d", r=2, d=64)[:, :, r, :]
                op = vcopy(hv(yr), by[r].t[:, 0:256].rearrange("p (i d) -> p i d", d=64), ly)
                free(by[r], op)
            b = bank()
            for h in range(8):
                hs = slice(h * 64, h * 64 + 64)
                p = prob(b_, h % 2, h // 2)
                mm(b.t[:, hs], GB[:, p, 128:256], nU[:, b_, hs], True, False, b.rel, t_nU)
                last = mm(b.t[:, hs], GK[:, p, 128:256], vtok[:, b_, hs], False, True)
            v = vtt(yr[:, b_, :], b.t[:, :], yr[:, b_, :], ALU.add, last, op)
            free(b, v)
            t_yr[b_] = v
        y16 = yr[:, :, :].rearrange("p t (n d) -> p (t n) d", d=64)
        yf = yr[:, :, :]
        v = vred(yst[:, 0, :], y16, ALU.add, t_yr)
        v = vts1(yst[:, 0, :], yst[:, 0, :], 1.0 / 64, ALU.mult, v)
        v = vtt(y16, y16, bc(yst[:, 0, :], 2, 64), ALU.subtract, v)
        q = vtt(ysq[:, :, :], y16, y16, ALU.mult, v)
        q = vred(yst[:, 1, :], ysq[:, :, :], ALU.add, q)
        q = vts(yst[:, 1, :], yst[:, 1, :], 1.0 / 64, 64e-5, ALU.mult, ALU.add, q)
        q = rsqrt(yst[:, 1, :], yst[:, 1, :], q)
        v = vtt(y16, y16, bc(yst[:, 1, :], 2, 64), ALU.mult, q)
        v = vtt(yf, yf, bc(rows[:, 1024:1536], 1, 2), ALU.mult, v, t_rows)
        v = vtt(yf, yf, bc(rows[:, 1536:2048], 1, 2), ALU.add, v)
        q = [vtt(ysq[:, tb * 8:tb * 8 + 8, :], vtok[:, tb, :].rearrange("p (n d) -> p n d", d=64),
                 bc(bon[:, tb * 8:tb * 8 + 8], 2, 64), ALU.mult, t_bon, t_tok["v"]) for tb in range(2)]
        v = vtt(y16, y16, ysq[:, :, :], ALU.add, v, q)
        t_yb = vtt(yB, yf, gtok[:, :, :], ALU.mult, v, t_g)
        SY = Mem(nc, prep_at, P.end)
        yhl2 = SY("yhl2", [128, 2, 8, 256], F32R)
        t_yT = to_T(tbs(yA), [yhl2[:, q, 0:4, :] for q in range(2)], 4, gcols("g_attn_out"), t_ya, t_yr)
        t_yT += to_T([yB[:, tb, :] for tb in range(2)], [yhl2[:, q, 4:8, :] for q in range(2)], 4, None, [t_yb, t_yb], t_yr)
        t_x3 = residual(hB, hA, (yhl2[:, 0, :, :], yhl2[:, 1, :, :]), t_yT, "w_o", t_x2)
        if stop == 5:
            return finish(nc, Q, sems, ctx, outs, hB, t_x3, load)

        t_dead = [t_yb, t_x3]
        n_n = norm(tbs(hB), tbs(xn), t_x3)
        w_xT = to_T(tbs(xn), xT, 8, gcols("g_ffn"), n_n, t_x3)
        bo = [bank() for _ in range(4)]
        for tb in range(2):
            for g in range(2):
                b = bo[2 * tb + g]
                t_seed = mm(b.t[:, :], ident, hB[:, tb, g * 512:g * 512 + 512], True, False, b.rel, t_x3[tb])
        t_dead = [t_dead, w_xT, n_n, t_seed]
        SE = P.sub()
        slT = sbuf(SE, "slT", [128, 3, 256])
        gp = sbuf(SE, "gp", [128, 3, 256], BF16)
        Wr = sbuf(SE, "Wr", [128, 2, 2, 256], F32R)
        Bo = sbuf(SE, "Bo", [128, 2, 8, 128], BF16)
        SO = Mem(nc, hA_at, x_at)
        Ao = sbuf(SO, "Ao", [128, 2, 3, 8, 64], BF16)
        Eo = sbuf(SO, "Eo", [128, 8, 64], BF16)
        ge_at = SE.at
        GE = sbuf(SE, "GE", [128, 128, 256])
        ST_ = Mem(nc, ge_at + 65536, ge_at + 131072)
        qP = sbuf(ST_, "qP", [128, 16, 256])
        sS = sbuf(ST_, "sS", [128, 2, 16, 128])
        sS2 = sbuf(ST_, "sS2", [128, 16, 128])
        m16 = sbuf(ST_, "m16", [128, 16, 16])
        ix = sbuf(ST_, "ix", [128, 16, 16], U32)
        ixf = sbuf(ST_, "ixf", [128, 16, 16])
        top = sbuf(ST_, "top", [128, 8, 16])
        pst = sbuf(ST_, "pst", [128, 8, 16], U32)
        psi = sbuf(ST_, "psi", [128, 2, 128], U32)
        psf = sbuf(ST_, "psf", [128, 2, 128])
        sel = sbuf(ST_, "sel", [128, 2, 3, 128])
        gs = sbuf(ST_, "gs", [128, 2, 2, 8])
        cand = qP[:, 0:8, :].rearrange("p h (a b) -> p h a b", b=16)
        cand2 = qP[:, 8:16, :]
        t_qP = []

        def ev_q(b, j, c, last):
            op = copy(qP[:, j:j + 2, :], b.t[:, :].rearrange("p (a b) -> p a b", a=2), last, t_dead)
            t_qP.append(op)
            return op
        projT(xT, w_xT, "w_pq", 16, ev_q)
        t_s = [[], []]
        for half in range(2):
            wt, _, tk, i_k = wnext("sub_keys", half)
            for tb in range(2):
                for j in range(2):
                    b = bank()
                    for q in range(4):
                        hp = 8 * half + 4 * j + q
                        last = mm(b.t[:, q * 128:q * 128 + 128], qP[:, hp, tb * 128:tb * 128 + 128],
                                  wt[:, (hp % 8) * 128:(hp % 8) * 128 + 128], True, True, b.rel, tk, t_qP)
                    h0 = 8 * half + 4 * j
                    op = copy(sS[:, tb, h0:h0 + 4, :], b.t[:, :].rearrange("p (a b) -> p a b", a=4), last, t_dead)
                    free(b, op)
                    t_s[tb].append(op)
            wdone(i_k, last)
        t_scores = last

        def top16(n, src, src2, m, xi, w):
            a = [V(lambda e, i=i: e.max(m[:, i, 0:8], src(i)), w) for i in range(n)]
            b1 = [V(lambda e, i=i: e.max_index(xi[:, i, 0:8], m[:, i, 0:8], src(i)), a[i]) for i in range(n)]
            c1 = [V(lambda e, i=i: e.match_replace(src2(i), m[:, i, 0:8], src(i), -3.0e38), a[i]) for i in range(n)]
            d1 = [V(lambda e, i=i: e.max(m[:, i, 8:16], src2(i)), c1[i]) for i in range(n)]
            e1 = [V(lambda e, i=i: e.max_index(xi[:, i, 8:16], m[:, i, 8:16], src2(i)), d1[i]) for i in range(n)]
            return [e1[-1], b1[-1], d1[-1]]

        t_sl = []
        t_end = [t_scores]

        def choose(tb):
            v = top16(16, lambda i: sS[:, tb, i, :], lambda i: sS2[:, i, :], m16, ix, [t_s[tb], t_end[0]])
            v1 = vcopy(ixf[:, :, :], ix[:, :, :], v)
            mv = m16[:, :, :].rearrange("p (h c) k -> p h c k", c=2)
            xv = ixf[:, :, :].rearrange("p (h c) k -> p h c k", c=2)
            v = vtt(cand, bc(mv[:, :, 0, :], 3, 16), bc(mv[:, :, 1, :], 2, 16), ALU.add, v, t_end[0])
            v = top16(8, lambda i: cand[:, i, :, :].rearrange("p a b -> p (a b)"), lambda i: cand2[:, i, :], top, pst, v)
            sg_ = sel[:, tb, 2, :].rearrange("p (h k) -> p h k", k=16)
            g = vtt(sg_, top[:, :, :], bc(top[:, :, 0], 2, 16), ALU.subtract, v)
            pf = pst[:, :, :].rearrange("p h k -> p (h k)")
            s0 = vts1(psi[:, 0, :], pf, 4, ALU.logical_shift_right, v)
            s1 = vts1(psi[:, 1, :], pf, 15, ALU.bitwise_and, v)
            s0 = vcopy(psf[:, :, :], psi[:, :, :], s0, s1)
            eqf = cand.rearrange("p h a b -> p (h a) b")
            for j in range(2):
                q = vtt(eqf, bc(psf[:, j, :], 2, 16), bc(C("iota16"), 1, 128), ALU.is_equal, s0, v)
                q = vtt(cand, cand, bc(xv[:, :, j, :], 2, 16), ALU.mult, q, v1)
                s0 = vred(sel[:, tb, j, :], eqf, ALU.add, q)
            yield
            g = act(sg_, sg_, ACT.Exp, g)
            g = vred(gs[:, tb, 0, :], sg_, ALU.add, g)
            g = V(lambda e: e.reciprocal(gs[:, tb, 1, :], gs[:, tb, 0, :]), g)
            g = vtt(sg_, sg_, bc(gs[:, tb, 1, :], 2, 16), ALU.mult, g)
            t_end[0] = [s0, g]
            yield
            b = bank()
            for j in range(3):
                last = tp(b.t[:, j * 128:j * 128 + 128], sel[:, tb, j, :], b.rel, s0, g)
            op = vcopy(slT[:, :, tb * 128:tb * 128 + 128], b.t[:, 0:384].rearrange("p (a b) -> p a b", a=3), last, t_dead)
            free(b, op)
            t_sl.append(op)
            t_end[0] = [t_end[0], last]

        t_ge = {}

        def scores(c):
            wh, wl, tk, i = wnext("eu", c)
            b = bank()
            for k in range(8):
                cs = slice(k * 128, k * 128 + 128)
                last = mm3(b.t[:, 0:256], (wh[:, cs], wl[:, cs]), tuple(t[:, k, :] for t in xT), k == 0, k == 7, tk, b.rel, w_xT[k])
            wdone(i, last)
            t_ge[c] = act(GE[:, c, :], b.t[:, 0:256], ACT.Gelu, last, t_dead, t_end[0] if c >= 64 else None)
            free(b, t_ge[c])

        t_G = [[], []]
        n_b = [0]
        used = [None, None]
        t_eo = [None]

        def gates(h):
            for t8 in range(32):
                u = n_b[0] % 2
                n_b[0] += 1
                ts = slice(8 * t8, 8 * t8 + 8)
                vb = vtt(Bo[:, u, :, :], bc(slT[:, 1, ts], 2, 128), bc(C("iota"), 1, 8), ALU.is_equal, t_sl, used[u], t_dead)
                ve = vtt(Eo[:, :, :], bc(slT[:, 0, ts], 2, 64), bc(C("iota")[:, 64 * h:64 * h + 64], 1, 8), ALU.is_equal, t_sl, t_eo[0])
                va_ = [vtt(Ao[:, u, k, :, :], Eo[:, :, :], bc(gp[:, k, ts], 2, 64), ALU.mult, ve, t_gp, used[u]) for k in range(3)]
                t_eo[0] = va_[-1]
                yield
                b = bank()
                for q in range(8):
                    for k in range(3):
                        last = mm(b.t[:, q * 64:q * 64 + 64], Bo[:, u, q, :], Ao[:, u, k, q, :], k == 0, k == 2, b.rel, vb, va_)
                used[u] = last
                o = GE[:, 64 * h:64 * h + 64, ts]
                op = vtt(o, o, b.t[:, :].rearrange("p (t i) -> p i t", t=8), ALU.mult, last, [t_ge[c] for c in range(64 * h, 64 * h + 64)])
                free(b, op)
                t_G[h].append(op)
                yield

        t_O = {}
        t_Wd = {}

        def weight(c):
            h, l = Wr[:, c % 2, 0, :], Wr[:, c % 2, 1, :]
            a = acopy(h, GE[:, c, :], t_G[c // 64], t_O.get(c - 2), t_dead)
            t_Wd[c] = [a, vtt(l, GE[:, c, :], h.bitcast(F32), ALU.subtract, a, t_G[c // 64], t_O.get(c - 2), t_dead)]

        def apply(c):
            wh, wl, tk, i = wnext("ev", c)
            for tb in range(2):
                for g in range(2):
                    cs = slice(g * 512, g * 512 + 512)
                    x = tuple(Wr[:, c % 2, q, tb * 128:tb * 128 + 128] for q in range(2))
                    last = mm3(bo[tb * 2 + g].t[:, :], x, (wh[:, cs], wl[:, cs]), False, c == 127, tk, t_Wd[c])
            wdone(i, last)
            t_O[c] = last

        ch = [choose(0), choose(1)]
        next(ch[0])
        for c in range(64):
            scores(c)
            if c == 20:
                next(ch[0])
            if c == 26:
                next(ch[0], None)
                next(ch[1])
            if c == 52:
                next(ch[1])
            if c == 56:
                next(ch[1], None)
        t_gp = []
        r_ = slT[:, 2, :]
        w = t_sl
        for k in range(3):
            t_gp.append(vcopy(gp[:, k, :], r_, w, t_dead))
            if k < 2:
                w = vtt(r_, r_, gp[:, k, :], ALU.subtract, t_gp[-1])
        g_ = gates(0)
        for c in range(64, 128):
            next(g_, None)
            scores(c)
        for _ in g_:
            pass
        g_ = gates(1)
        weight(0)
        for c in range(128):
            if c < 64:
                next(g_, None)
            if c == 63:
                for _ in g_:
                    pass
            if c + 1 < 128:
                weight(c + 1)
            apply(c)
        fin = [[], []]
        o = GE[:, 0:8, :].rearrange("p a b -> p (a b)").rearrange("p (t n) -> p t n", t=2)
        for tb in range(2):
            for g in range(2):
                gsl = slice(g * 512, g * 512 + 512)
                fin[tb].append(copy(o[:, tb, gsl], bo[tb * 2 + g].t[:, :], t_O[127]))
        return finish(nc, Q, sems, ctx, outs, o, fin, load)


def finish(nc, Q, sems, ctx, out, src, toks, load):
    o = out.rearrange("b (t p) d -> p (b t) d", p=128)
    d = load("sp", o, src[:, :, :] if len(src.shape) == 3 else src, toks)
    Q.add("sp", lambda e: e.nop(), d)
    Q.number(sems)
    block = ctx.enter_context(nc.Block())

    @block.tensor
    def _(e):
        Q.emit("pe", e)

    @block.vector
    def _(e):
        Q.emit("dve", e)

    @block.scalar
    def _(e):
        Q.emit("act", e)

    @block.gpsimd
    def _(e):
        Q.emit("pool", e)

    @block.sync
    def _(e):
        Q.emit("sp", e)


def layout(inputs):
    I = {k: np.asarray(v) for k, v in inputs.items()}
    c, d = constants()

    def w_t(W):
        K, N = W.shape
        return np.ascontiguousarray(W.reshape(K // 128, 128, N // 128, 128).transpose(2, 1, 0, 3)).reshape(N // 128, 128, K)

    def w_g(W):
        N = W.shape[1]
        return np.ascontiguousarray(W.reshape(4, 2, 128, N // 512, 512).transpose(3, 0, 2, 1, 4)).reshape(-1, 128, 1024)

    def w_k(W):
        return np.ascontiguousarray(W.reshape(-1, 128, W.shape[1]))

    def cols(v):
        return v.reshape(-1, 128).T

    def row(v):
        return np.broadcast_to(v.reshape(1, -1), (128, v.size))

    w_in = I["w_in"][0]
    w2 = I["w_in_2"][0]
    pk = {"g_mix": I["g_mix"], "g_cross": I["g_cross"], "g_mem": I["g_mem"], "g_mlp": I["g_mlp"], "g_subln": I["g_subln"],
          "g_mix_2": I["g_mix_2"], "g_cq": I["g_cq_2"], "g_ckv": I["g_ckv_2"], "g_attn_out": I["g_attn_out_2"],
          "rwkv_mu": I["rwkv_mu_2"], "w0": I["w0_2"], "a0": I["a0_2"], "k_k": I["k_k_2"], "k_a": I["k_a_2"], "r_k": I["r_k_2"],
          "g_ffn": I["g_ffn_2"]}
    pk = {k: cols(v) for k, v in pk.items()}
    poff, _ = offsets(pk)
    rows = np.concatenate([row(I[k]) for k in ("g_final", "ln_x_w_2", "ln_x_b_2", "g_qnorm_2", "g_knorm_2", "lambda_q1",
                                                "lambda_k1", "lambda_q2", "lambda_k2")], 1)
    T = {
        "x": I["x"][0], "mem": I["mem"][0], "cst": np.concatenate(list(c.values()), 1), "dst": np.concatenate(list(d.values()), 1),
        "par": np.concatenate(list(pk.values()), 1), "rows": rows,
        "pos": np.concatenate([I["positions"].reshape(2, 128).T, I["positions_2"].reshape(2, 128).T], 1),
        "w_in_a": w_g(np.concatenate([w_in[:, 0:1536], w_in[:, 2560:3072]], 1)), "w_in_t": w_t(w_in[:, 1536:2560]),
        "w_out": w_g(I["w_out"][0]), "w_xk": w_t(I["w_xkv"][0][:, 0:1024]), "w_xv": w_g(I["w_xkv"][0][:, 1024:2048]),
        "w_xq": w_t(I["w_xq"][0]), "w_xo": w_g(I["w_xo"][0]), "w_up": w_t(I["w_up"][0]), "w_down": w_k(I["w_down"][0]),
        "w_mla": w_k(w2[:, 0:672]), "w_rwkv": w_t(w2[:, 672:2464]), "w_uq": w_k(I["w_uq_2"][0]),
        "w_ukv": w_k(np.concatenate([I["w_uk_2"][0], I["w_uv_2"][0]], 1)),
        "w_lora": np.concatenate([np.concatenate([I["w2_2"][0], I["a2_2"][0]], 0), I["g2_2"][0]], 1)[None],
        "w_o": w_g(I["w_o_2"][0]), "w_pq": w_t(I["w_pq_2"][0]),
        "sub_keys": I["sub_keys_2"][0].transpose(3, 0, 1, 2).reshape(128, 2, 1024).transpose(1, 0, 2),
        "eu": np.ascontiguousarray(I["expert_u_2"][0].reshape(128, 128, 8, 128).transpose(0, 3, 2, 1)).reshape(128, 128, 1024),
        "ev": I["expert_v_2"][0].reshape(128, 128, 1024),
    }
    return {k: np.ascontiguousarray(v) for k, v in T.items()}, poff


def kernel(**inputs):
    import concourse.bacc as _bacc
    from concourse import mybir as _mybir
    from concourse.bass_utils import run_bass_kernel_spmd as _run

    nc = _bacc.Bacc("TRN2", target_bir_lowering=False, num_devices=1)
    T, poff = layout(inputs)
    arrays, args = {}, {}
    for name, a in T.items():
        arrays[f"in_{name}"] = a
        args[name] = nc.dram_tensor(f"in_{name}", a.shape, _mybir.dt.from_np(a.dtype), kind="ExternalInput").ap()
    out = nc.dram_tensor("out_0", (1, 256, 1024), _mybir.dt.from_np(np.dtype("float32")), kind="ExternalOutput").ap()
    build(nc, args, poff, out, STOP)
    r = _run(nc, [arrays], core_ids=[0])
    return r.results[0]["out_0"]


STOP = 99
```

```python
import math
from collections import deque
from contextlib import ExitStack

import numpy as np
import concourse.bass as bass
from concourse import mybir

F32 = mybir.dt.float32
F32R = mybir.dt.float32r
BF16 = mybir.dt.bfloat16
I32 = mybir.dt.int32
U32 = mybir.dt.uint32
ALU = mybir.AluOpType
ACT = mybir.ActivationFunctionType
AX = mybir.AxisListType.X
NRAW, NSP = 4, 3
ORDER = [("w_in_a", 16, 1024, 1), ("w_in_t", 8, 1024, 1), ("w_xk", 8, 1024, 1), ("w_xv", 8, 1024, 1), ("w_out", 8, 1024, 1),
         ("w_xq", 8, 1024, 1), ("w_xo", 8, 1024, 1), ("w_up", 32, 1024, 1), ("w_down", 32, 1024, 1), ("w_rwkv_0", 8, 1024, 1),
         ("w_lora", 1, 1024, 0), ("w_rwkv_1", 6, 1024, 1), ("w_mla", 8, 672, 1), ("w_uq", 3, 768, 1), ("w_ukv", 2, 1024, 1), ("w_o", 8, 1024, 1),
         ("w_pq", 16, 1024, 1), ("sub_keys", 2, 1024, 0), ("eu", 128, 1024, 1), ("ev", 128, 1024, 1)]
ON_POOL = ("w_pq", "w_o", "w_xk", "w_xv", "w_rwkv_0", "w_rwkv_1", "w_mla", "eu", "ev")
NEG = -1e30
PLAN = ["mt", "mt", "mtm", "mt", "t", "", "t", "tmtm", "m", "mm", "m", "mmm", "mm", "mm", "m", "mm", "km", "kkmk", "kkm", "kkm"] + ["m"] * 18


class Op:

    def __init__(self, eng):
        self.eng, self.sem, self.val, self.need, self.dma = eng, None, 0, False, False


class Queues:

    def __init__(self):
        self.q = {e: [] for e in ("pe", "dve", "act", "pool", "sp")}

    def add(self, eng, fn, *waits):
        op = Op(eng)
        ws = []
        todo = list(waits)
        while todo:
            w = todo.pop()
            if w is None:
                continue
            if isinstance(w, (list, tuple)):
                todo += w
            else:
                w.need = True
                ws.append(w)
        self.q[eng].append((op, fn, ws))
        return op

    def dma(self, eng, out, in_, sem, val, *waits):
        op = self.add(eng, lambda e: e.dma_start(out, in_), *waits)
        op.sem, op.val, op.dma = sem, val, True
        return op

    def number(self, sems):
        for eng, q in self.q.items():
            n = 0
            for op, _, _ in q:
                if op.need and not op.dma:
                    n += 1
                    op.sem, op.val = sems[eng], n

    def emit(self, eng, e):
        seen = {}
        for op, fn, ws in self.q[eng]:
            want = {}
            for w in ws:
                if eng == "pe" and w.eng == "pe":
                    continue
                k = id(w.sem)
                if want.get(k, (None, 0))[1] < w.val:
                    want[k] = (w.sem, w.val)
            for k, (s, v) in want.items():
                if seen.get(k, 0) < v:
                    e.wait_ge(s, v)
                    seen[k] = v
            ins = fn(e)
            if op.dma:
                ins.then_inc(op.sem, 16)
            elif op.need:
                ins.then_inc(op.sem, 1)


SIZE = {F32: 4, F32R: 4, I32: 4, U32: 4, BF16: 2}


class Mem:

    def __init__(self, nc, at, end):
        self.nc, self.at, self.end = nc, at, end

    def sub(self):
        return Mem(self.nc, self.at, self.end)

    def __call__(self, name, shape, dt=F32):
        t = self.nc.alloc_sbuf_tensor_at(name, shape, dt, offset=self.at)
        self.at += int(np.prod(shape[1:])) * SIZE[dt]
        self.at = (self.at + 31) // 32 * 32
        assert self.at <= self.end, (name, self.at, self.end)
        return t


def bc(ap, axis, n):
    u = ap.unsqueeze(axis)
    shape = list(u.shape)
    shape[axis] = n
    return u.to_broadcast(shape)


def constants():
    p = np.arange(128)[:, None]
    f = np.arange(128)[None, :]
    one = lambda m: m.astype(np.float32)
    add = lambda m: np.where(m, 0.0, NEG).astype(np.float32)
    c = {"ident": one(p == f), "iota": np.broadcast_to(np.arange(128, dtype=np.float32), (128, 128)),
         "iota16": np.broadcast_to(np.arange(16, dtype=np.float32), (128, 16))}
    d = {}
    z = np.zeros((128, 128), np.float32)
    d["maskA"] = np.concatenate([z, add(f <= p)], 1)
    d["maskM"] = np.concatenate([z, add(f // 64 <= p // 64)], 1)
    d["maskS"] = one(p < f)
    d["negtri"] = -one(p >= f)
    d["negones"] = -np.ones((128, 128), np.float32)
    d["blk"] = one(p // 64 == f // 64)
    d["hsel"] = one(p // 64 == np.arange(2)[None, :])
    same = p // 64 == f // 64
    d["m2"] = np.concatenate([one(same & (p < f)), one(same & (p <= f))], 1)
    d["eye2"] = one(p % 64 == np.arange(64)[None, :])
    for l in range(6):
        m = 1 << l
        lev = (p // (2 * m) == f // (2 * m)) & (p // m % 2 == 1) & (f // m % 2 == 0)
        d[f"lx{l}"] = one(lev)[:, 0:64] + one(lev)[:, 64:128]
        d[f"ly{l}"] = one(lev.T)[:, 0:64] + one(lev.T)[:, 64:128]
    d["rst"] = np.broadcast_to(one(np.arange(256)[None, :] % 64 != 0), (128, 256))
    f1 = np.float32(500000.0) ** (-np.arange(0, 16, 2, dtype=np.float32) / np.float32(16))
    f2 = np.float32(10000.0) ** (-np.arange(16, dtype=np.float32) / np.float32(16))
    d["invf"] = np.broadcast_to(np.concatenate([f1, f2]).astype(np.float32), (128, 24))
    return c, d


def offsets(d):
    off, n = {}, 0
    for k, v in d.items():
        off[k] = (n, n + v.shape[1])
        n += v.shape[1]
    return off, n


def build(nc, T, poff, outs, stop=99):
    coff, ncc = offsets(constants()[0])
    doff, ncd = offsets(constants()[1])
    npar = max(b for _, b in poff.values())
    Q = Queues()
    ctx = ExitStack()
    with ctx:
        sems = {e: ctx.enter_context(nc.semaphore("s_" + e)) for e in Q.q}

        base = (nc.sbuf_base + 31) // 32 * 32
        fence = ctx.enter_context(nc.sbuf_tensor("fence", [128, (nc.sbuf_bytes_remaining - 64) // 4], F32))
        P = Mem(nc, base, nc.sbuf_base // 32 * 32)

        def sbuf(m, name, shape, dt=F32):
            return m(name, shape, dt)

        def PE(fn, *w): return Q.add("pe", fn, *w)
        def V(fn, *w): return Q.add("dve", fn, *w)
        def A(fn, *w): return Q.add("act", fn, *w)
        def G(fn, *w): return Q.add("pool", fn, *w)

        nload = [0]

        def load(eng, out, in_, *w):
            nload[0] += 1
            return Q.dma(eng, out, in_, ctx.enter_context(nc.semaphore(f"ld{nload[0]}")), 16, *w)

        class Bank:
            pass
        banks = deque()
        for i in range(8):
            b = Bank()
            b.t = ctx.enter_context(nc.psum_tensor(f"ps{i}", [128, 512], F32))
            b.rel = []
            banks.append(b)

        def bank(): return banks.popleft()

        def free(b, *ops):
            b.rel = list(ops)
            banks.append(b)

        raw = sbuf(P, "raw", [128, NRAW, 1024])
        spl_at = P.at
        spl = sbuf(P, "spl", [128, NSP, 2, 1024], F32R)
        rsem = [ctx.enter_context(nc.semaphore(f"raw{i}")) for i in range(NRAW)]
        pieces = [(nm, j, n, sp) for nm, cnt, n, sp in ORDER for j in range(cnt)]
        nsplit = [0]
        state = {"split": 0, "use": 0, "stop": len(pieces)}
        t_dma, t_hl, slot_of, wfree, rawfree = {}, {}, {}, {}, {}
        last_in_slot = {}

        def issue(i):
            nm, j, n, _ = pieces[i]
            t_dma[i] = Q.dma("sp", raw[:, i % NRAW, 0:n], T[nm][j], rsem[i % NRAW], 16 * (i // NRAW + 1), rawfree.get(i - NRAW))

        def raw_done(i, op):
            rawfree[i] = op
            if i + NRAW < len(pieces):
                issue(i + NRAW)

        def split(i):
            nm, j, n, sp = pieces[i]
            if not sp:
                return
            k = nsplit[0]
            nsplit[0] += 1
            s_ = k % NSP
            slot_of[i] = s_
            before = last_in_slot.get(s_)
            r, h, l = raw[:, i % NRAW, 0:n], spl[:, s_, 0, 0:n], spl[:, s_, 1, 0:n]
            w = wfree[before] if before is not None else None
            a = A(lambda e: e.activation(h, r, ACT.Copy), t_dma[i], w)
            f = G if nm in ON_POOL else V
            b = f(lambda e: e.tensor_tensor(l, r, h.bitcast(F32), ALU.subtract), a, w)
            last_in_slot[s_] = i
            t_hl[i] = (a, b)
            raw_done(i, b)

        def ahead():
            while state["split"] < state["stop"] and state["split"] <= state["use"] + NSP - 1:
                i = state["split"]
                if i not in t_dma:
                    break
                if pieces[i][3]:
                    before = last_in_slot.get(nsplit[0] % NSP)
                    if before is not None and before not in wfree:
                        break
                split(i)
                state["split"] += 1

        def lend(nm):
            state["stop"] = next(i for i, p in enumerate(pieces) if p[0] == nm)

        def take_back(*ops):
            for i in last_in_slot.values():
                wfree[i] = [wfree[i], ops]
            state["stop"] = len(pieces)
            ahead()

        def wnext(nm, j):
            i = state["use"]
            assert pieces[i][:2] == (nm, j), (pieces[i], nm, j)
            ahead()
            assert state["split"] > i
            state["use"] += 1
            n = pieces[i][2]
            if not pieces[i][3]:
                return raw[:, i % NRAW, 0:n], None, t_dma[i], i
            return spl[:, slot_of[i], 0, 0:n], spl[:, slot_of[i], 1, 0:n], t_hl[i], i

        def wdone(i, op):
            wfree[i] = op
            if not pieces[i][3]:
                raw_done(i, op)
            ahead()

        cst = sbuf(P, "cst", [128, ncc])
        par = sbuf(P, "par", [128, npar])
        hA_at = P.at
        hA = sbuf(P, "hA", [128, 2, 1024])
        x_at = P.at
        xhl = sbuf(P, "xhl", [128, 2, 8, 256], F32R)
        xT = (xhl[:, 0, :, :], xhl[:, 1, :, :])
        stats = sbuf(P, "stats", [128, 96])
        neghalf = sbuf(P, "neghalf", [128, 1])
        S_AD = P.sub()
        dst = sbuf(S_AD, "dst", [128, ncd])
        rows = sbuf(S_AD, "rows", [128, 2496])
        hx = sbuf(S_AD, "hx", [128, 2, 2, 1024])
        hB, xn = hx[:, 0, :, :], hx[:, 1, :, :]
        junk = sbuf(S_AD, "junk", [128, 1024])
        pos = sbuf(S_AD, "pos", [128, 4], I32)

        def C(k): return cst[:, coff[k][0]:coff[k][1]]
        def D(k): return dst[:, doff[k][0]:doff[k][1]]
        def par_(k): return par[:, poff[k][0]:poff[k][1]]

        ident = C("ident")
        t_half = G(lambda e: e.memset(neghalf[:, :], -0.5))
        x_r = T["x"].rearrange("(t p) d -> p t d", p=128)
        t_c = load("act", cst[:, :], T["cst"])
        t_x = [load(e, hA[:, tb, :], x_r[:, tb, :]) for tb, e in enumerate(("act", "sp"))]
        t_par = load("act", par[:, :], T["par"])
        for i in range(NRAW):
            issue(i)
        nstat = [0]

        def stat():
            nstat[0] += 1
            return stats[:, nstat[0] - 1:nstat[0]]

        def mm(out, l, r, st, sp, *w):
            return PE(lambda e: e.matmul(out, l, r, start=st, stop=sp), *w)

        def tp(out, in_, *w):
            n = in_.shape[0]
            return PE(lambda e: e.transpose(out, in_, ident[0:n, 0:n]), t_c, *w)

        def vts(out, a, s1, s2, o0, o1, *w):
            return V(lambda e: e.tensor_scalar(out, a, s1, s2, o0, o1), *w)

        def vts1(out, a, s1, o0, *w):
            return V(lambda e: e.tensor_scalar(out, a, s1, None, o0), *w)

        def rsqrt(out, a, *w):
            h = neghalf[:, 0:1].to_broadcast(list(a.shape)) if len(a.shape) == 2 else bc(neghalf[:, 0:1], 1, a.shape[1]).to_broadcast(list(a.shape))
            return G(lambda e: e.tensor_tensor(out, a, h, ALU.pow), t_half, *w)

        def vtt(out, a, b, op, *w):
            return V(lambda e: e.tensor_tensor(out, a, b, op), *w)

        def vstt(out, a, s, b, o0, o1, *w):
            return V(lambda e: e.scalar_tensor_tensor(out, a, s, b, o0, o1), *w)

        def vcopy(out, a, *w):
            return V(lambda e: e.tensor_copy(out, a), *w)

        def vred(out, a, op, *w):
            return V(lambda e: e.tensor_reduce(out, a, AX, op), *w)

        def act(out, a, f, *w, scale=1.0, bias=0.0, acc=None):
            return A(lambda e: e.activation(out, a, f, bias=bias, scale=scale, accum_out=acc), *w)

        def acopy(out, a, *w):
            return A(lambda e: e.activation(out, a, ACT.Copy), *w)

        flip = [0]

        def copy(out, a, *w):
            flip[0] ^= 1
            return (vcopy if flip[0] else acopy)(out, a, *w)

        t_junk = [None]

        def rstd(src, n, w):
            s, s2 = stat(), stat()
            a = act(junk[:, 0:src.shape[1]], src, ACT.Square, w, t_junk[0], acc=s)
            t_junk[0] = a
            v = vts(s2, s, 1.0 / n, 1e-6, ALU.mult, ALU.add, a)
            return s2, rsqrt(s2, s2, v)

        def norm(src, out, w):
            r = []
            for tb in range(2):
                s, v = rstd(src[tb], src[tb].shape[1], w[tb])
                r.append(vts1(out[tb], src[tb], s, ALU.mult, v, w[tb]))
            return r

        def to_T(src, out, nk, g, w, w2=None):
            toks = []
            for j in range(0, nk, 2):
                b = bank()
                n = min(2, nk - j)
                for k in range(n):
                    for tb in range(2):
                        last = tp(b.t[:, k * 256 + tb * 128:k * 256 + tb * 128 + 128],
                                  src[tb][:, (j + k) * 128:(j + k + 1) * 128], b.rel, w[tb])
                hl = []
                for k in range(n):
                    o = tuple(t[:, j + k, :] for t in out)
                    i = b.t[:, k * 256:(k + 1) * 256]
                    s = g[j + k] if g is not None else None
                    h, l = o
                    if s is None:
                        hl.append((acopy(h, i, last, w2), lambda a_, h=h, l=l, i=i: vtt(l, i, h.bitcast(F32), ALU.subtract, a_, w2)))
                    else:
                        hl.append((act(h, i, ACT.Copy, last, t_par, w2, scale=s),
                                   lambda a_, h=h, l=l, i=i, s=s: vstt(l, i, s, h.bitcast(F32), ALU.mult, ALU.subtract, a_, w2)))
                fin_ = hl[-1][0]
                for a_, f in hl:
                    op = f([a_, fin_])
                    toks.append([a_, op])
                free(b, op)
            return toks

        def rows_of(sc, w):
            d = [vts(dg[:, tb * 128:tb * 128 + 128], ident, sc[tb], -1.0, ALU.mult, ALU.mult, t_c, t_d, w[tb], R.get("rows")) for tb in range(2)]
            yield
            b = bank()
            last = mm(b.t[:, 0:256], D("negones"), dg, True, True, b.rel, d)
            op = vcopy(rw[:, :], b.t[:, 0:256], last, R.get("rows_used"))
            free(b, op)
            R["rows"] = op
            return op

        def scaled(out, a, sc, *w):
            flip[0] ^= 1
            return vts1(out, a, sc, ALU.mult, *w) if flip[0] else act(out, a, ACT.Copy, *w, scale=sc)

        def to_T32(src, out, nk, w):
            toks = []
            for j in range(0, nk, 2):
                b = bank()
                for k in range(2):
                    for tb in range(2):
                        last = tp(b.t[:, k * 256 + tb * 128:k * 256 + tb * 128 + 128],
                                  src[tb][:, (j + k) * 128:(j + k + 1) * 128], b.rel, w[tb])
                op = copy(out[:, j:j + 2, :], b.t[:, :].rearrange("p (a b) -> p a b", a=2), last)
                free(b, op)
                toks += [op, op]
            return toks

        def gcols(k):
            return [par[:, c:c + 1] for c in range(*poff[k])]

        def evac_hl(out, a, last, *w):
            h, l = out
            x = acopy(h, a, last, *w)
            return [x, vtt(l, a, h.bitcast(F32), ALU.subtract, x, last, *w)]

        def mm3(out, l, r, st, sp, *w):
            mm(out, l[0], r[0], st, False, *w)
            mm(out, l[0], r[1], False, False, *w)
            return mm(out, l[1], r[0], False, sp, *w)

        def proj512(inT, w, W, g):
            b = [bank(), bank()]
            for j in range(4):
                wh, wl, tk, i = wnext(W, g * 4 + j)
                for k in range(2):
                    for tb in range(2):
                        cs = slice(k * 512, k * 512 + 512)
                        x = tuple(t[:, 2 * j + k, tb * 128:tb * 128 + 128] for t in inT)
                        last = mm3(b[tb].t[:, :], x, (wh[:, cs], wl[:, cs]), j + k == 0, 2 * j + k == 7,
                                   tk, w[2 * j + k], b[tb].rel if j + k == 0 else None)
                wdone(i, last)
            return b, last

        def projT(inT, w, W, n, evac):
            for j in range(0, n, 2):
                b = bank()
                c = min(2, n - j)
                for q in range(c):
                    wh, wl, tk, i = wnext(W, j + q)
                    for k in range(8):
                        cs = slice(k * 128, k * 128 + 128)
                        last = mm3(b.t[:, q * 256:q * 256 + 256], (wh[:, cs], wl[:, cs]), tuple(t[:, k, :] for t in inT),
                                   k == 0, k == 7, tk, w[k], b.rel)
                    if q < c - 1:
                        wdone(i, last)
                free(b, evac(b, j, c, last))
                wdone(i, last)

        def residual(out, base, inT, w, W, wb, pairs=((0, 1), (2, 3)), between=None):
            bs = [[bank(), bank()] for _ in range(2)]
            r = [[], []]
            for n, js in enumerate(pairs):
                if n and between:
                    between()
                for g in range(2):
                    p = [wnext(W, 4 * n + 2 * g + q) for q in range(2)]
                    last = {}
                    steps = [(tb, q, k) for tb in range(2) for q in range(2) for k in range(2)]
                    if n == 0 or g == 0:
                        steps.sort(key=lambda x: (x[1], x[2], x[0]))
                    for tb, q, k in steps:
                        wh, wl, tk, i = p[q]
                        cs = slice(k * 512, k * 512 + 512)
                        kt = 2 * js[q] + k
                        b = bs[tb][g]
                        x = tuple(t[:, kt % 4, tb * 128:tb * 128 + 128] for t in inT[kt // 4]) if between else \
                            tuple(t[:, kt, tb * 128:tb * 128 + 128] for t in inT)
                        last[tb] = mm3(b.t[:, :], x, (wh[:, cs], wl[:, cs]), n + q + k == 0, n == 1 and q + k == 2,
                                       tk, w[kt], b.rel if n == 0 else None)
                        if n == 1 and q + k == 2:
                            op = vtt(out[:, tb, g * 512:g * 512 + 512], b.t[:, :], base[:, tb, g * 512:g * 512 + 512], ALU.add, last[tb], wb)
                            free(b, op)
                            r[tb].append(op)
                        if (tb, q, k) == (1, 0, 1) and (n, g) != (1, 1):
                            wdone(i, last[1])
                    if (n, g) == (1, 1):
                        wdone(p[0][3], last[1])
                    wdone(p[1][3], last[1])
            return r

        def softmax(S, n, w, M, L):
            v = vred(M, S, ALU.max, w)
            yield
            v = vts1(M, M, -1.0, ALU.mult, v)
            yield
            a = [act(S[:, h, :], S[:, h, :], ACT.Exp, v, bias=M[:, h:h + 1], acc=L[:, h:h + 1]) for h in range(n)]
            return a, a

        def run(g):
            while True:
                try:
                    next(g)
                except StopIteration as e:
                    return e.value

        trig = sbuf(S_AD, "trig", [128, 2, 2, 24])
        ang = sbuf(S_AD, "ang", [128, 2, 2, 24])
        kq = xn[:, 1, 128:224].rearrange("p (a b c) -> p a b c", a=2, b=2)
        posf = sbuf(S_AD, "posf", [128, 4])
        lam = sbuf(S_AD, "lam", [128, 8])
        lj = xn[:, 1, 0:128]
        dg = xn[:, 0, 0:256]
        rw = sbuf(S_AD, "rw", [128, 256])
        R = {}
        t_tmp = [None]

        def rope(x1, x2, cos, sin, tmp, w):
            n = x1.shape[1]
            c, s = bc(cos, 1, n), bc(sin, 1, n)
            a = vtt(tmp[0], x1, c, ALU.mult, w, R["trig"], t_tmp[0])
            a = vtt(tmp[1], x2, s, ALU.mult, w)
            b = vtt(tmp[2], x2, c, ALU.mult, w)
            b = vtt(tmp[3], x1, s, ALU.mult, w)
            a = vtt(x1, tmp[0], tmp[1], ALU.subtract, a, b)
            t_tmp[0] = vtt(x2, tmp[2], tmp[3], ALU.add, b)
            return [a, t_tmp[0]]

        tbs = lambda t: [t[:, tb, :] for tb in range(2)]
        S = S_AD.sub()
        qk = sbuf(S, "qk", [128, 2, 1024])
        qkT = sbuf(S, "qkT", [128, 8, 256])
        va = sbuf(S, "va", [128, 2, 512])
        vs = sbuf(S, "vs", [128, 2, 512])
        sT = sbuf(S, "sT", [128, 8, 256])
        yhl = sbuf(S, "yhl", [128, 2, 8, 256], F32R)
        yT = (yhl[:, 0, :, :], yhl[:, 1, :, :])
        kmT = sbuf(S, "kmT", [128, 8, 256])
        vm = sbuf(S, "vm", [128, 2, 1024])
        S2 = S.sub()
        P0 = sbuf(S2, "P0", [128, 8, 128])
        P1 = qk[:, :, :].rearrange("p t n -> p (t n)").rearrange("p (a b) -> p a b", b=256)
        rt = P0[:, :, :].rearrange("p a b -> p (a b)").rearrange("p (i n d) -> p i n d", i=4, n=16)
        qkf = qkT[:, :, :].rearrange("p a b -> p (a b)").rearrange("p (a b) -> p a b", b=128)
        W1T, W0T = qkf[:, 0:8, :], qkf[:, 8:12, :]
        zs = sbuf(S2, "zs", [128, 3072])
        ez = sbuf(S2, "ez", [128, 3072])
        mlr = sbuf(S2, "mlr", [128, 2, 3, 8])
        xn4 = xn.rearrange("p t n -> p (t n)").rearrange("p (i t n) -> p i t n", i=2, t=2)
        od, osq = xn4[:, 0, :, :], xn4[:, 1, :, :]
        ost = sbuf(S2, "ost", [128, 2, 8])

        state["stop"] = 1
        ahead()
        w_xT = to_T(tbs(hA), xT, 8, gcols("g_mix"), t_x)
        state["stop"] = len(pieces)
        ahead()
        sx = [rstd(hA[:, tb, :], 1024, t_x[tb]) for tb in range(2)]
        t_pos = load("act", pos[:, :], T["pos"])
        t_d = load("act", dst[:, :], T["dst"])
        t_lrow = load("act", rows[:, 2240:2496], T["rows"][:, 2240:2496])
        def tables():
            v = vcopy(posf[:, :], pos[:, :], t_pos)
            last = None
            for tr in range(2):
                for tb in range(2):
                    for bl, lo, hi in ((0, 0, 8), (1, 8, 24)):
                        last = vts1(ang[:, tr, tb, lo:hi], D("invf")[:, lo:hi], posf[:, 2 * bl + tb:2 * bl + tb + 1],
                                    ALU.mult, v, t_d)
            v = last
            two_pi = 2 * math.pi
            C1 = 6.28125
            C2 = float(np.float32(round((two_pi - C1) * 2 ** 20) / 2 ** 20))
            C3 = float(np.float32(two_pi - C1 - C2))
            MAGIC = 12582912.0
            vs_ = []
            for tr in range(2):
                vs_.append(vts(kq[:, tr, :, :], ang[:, tr, :, :], 1.0 / two_pi, 0.25 * tr, ALU.mult, ALU.add, v))
            v = vts1(kq[:, :, :, :], kq[:, :, :, :], MAGIC, ALU.add, vs_)
            v = vts1(kq[:, :, :, :], kq[:, :, :, :], MAGIC, ALU.subtract, v)
            fl = lambda t: t[:, :, :, :].rearrange("p a b c -> p (a b c)")
            for cc in (C1, C2, C3):
                v = vstt(fl(ang), fl(kq), -cc, fl(ang), ALU.mult, ALU.add, v)
            v = vts1(ang[:, 1, :, :], ang[:, 1, :, :], math.pi / 2, ALU.add, v)
            v = vts(fl(ang), fl(ang), 3.1415925, -3.1415925, ALU.min, ALU.max, v)
            rl = lambda i: rows[:, 2240 + 64 * i:2304 + 64 * i]
            v1 = vtt(lj[:, 0:64], rl(0), rl(1), ALU.mult, t_lrow)
            v2 = vtt(lj[:, 64:128], rl(2), rl(3), ALU.mult, t_lrow)
            v2 = vred(lam[:, 0:2], lj.rearrange("p (a b) -> p a b", a=2), ALU.add, v1, v2)
            yield
            t_trig = act(fl(trig), fl(ang), ACT.Sin, v)
            v = v2
            a = act(lam[:, 2:4], lam[:, 0:2], ACT.Exp, v)
            v = vtt(lam[:, 4:5], lam[:, 3:4], lam[:, 2:3], ALU.subtract, a)
            t_lam = vts1(lam[:, 5:6], lam[:, 4:5], -(0.8 - 0.6 * math.exp(0.0)), ALU.add, v)
            nlam = lam[:, 5:6]
            return t_trig, t_lam, nlam

        t_qk = [[], []]
        for g in range(2):
            b, last = proj512(xT, w_xT, "w_in_a", g)
            for tb in range(2):
                op = scaled(qk[:, tb, g * 512:g * 512 + 512], b[tb].t[:, :], sx[tb][0], last, sx[tb][1])
                free(b[tb], op)
                t_qk[tb].append(op)
            if g == 0:
                rows_ = rows_of([v[0] for v in sx], [v[1] for v in sx])
                next(rows_)
                tables_ = tables()
                next(tables_)
                t_mem = load("sp", hB[:, :, :], T["mem"].rearrange("(t p) d -> p t d", p=128))
        t_rw = run(rows_)
        t_v = {}
        for g, dstt, nm in ((2, va, "va"), (3, vs, "vs")):
            b, last = proj512(xT, w_xT, "w_in_a", g)
            t_v[nm] = []
            for tb in range(2):
                op = scaled(dstt[:, tb, :], b[tb].t[:, :], sx[tb][0], last, sx[tb][1])
                free(b[tb], op)
                t_v[nm].append(op)
            if g == 2:
                t_trig, t_lam, nlam = run(tables_)
                R["trig"] = t_trig
        sm = [rstd(hB[:, tb, :], 1024, t_mem) for tb in range(2)]
        t_rope = []
        for tb in range(2):
            xv = qk[:, tb, :].rearrange("p (n d) -> p n d", d=64)
            t_rope.append(rope(xv[:, :, 0:8], xv[:, :, 8:16], trig[:, 1, tb, 0:8], trig[:, 0, tb, 0:8],
                               [rt[:, i, :, 0:8] for i in range(4)], t_qk[tb]))
        t_rows = load("sp", rows[:, 0:2240], T["rows"][:, 0:2240])
        n_m = [vts1(xn[:, tb, :], hB[:, tb, :], sm[tb][0], ALU.mult, sm[tb][1], t_rw, t_lam, t_trig) for tb in range(2)]
        t_sT = [None] * 8

        def ev_sT(b, j, c, last):
            op = copy(sT[:, j:j + c, :], b.t[:, 0:c * 256].rearrange("p (a b) -> p a b", a=c), last)
            for q in range(c):
                t_sT[j + q] = op
            return op
        def ev_sTr(b, j, c, last):
            op = vtt(sT[:, j:j + c, :], b.t[:, 0:c * 256].rearrange("p (a b) -> p a b", a=c), bc(rw[:, :], 1, c), ALU.mult, last, t_rw)
            for q in range(c):
                t_sT[j + q] = op
            return op
        projT(xT, w_xT, "w_in_t", 8, ev_sTr)
        R["rows_used"] = list(t_sT)

        def memory():
            w_mT = to_T(tbs(xn), yT, 8, gcols("g_mem"), n_m)
            R["nm"] = w_mT[-1]
            yield
            t_kmT = [None] * 8
            for j in range(0, 8, 2):
                b = bank()
                for q in range(2):
                    wh, wl, tk, i = wnext("w_xk", j + q)
                    for k in range(8):
                        cs = slice(k * 128, k * 128 + 128)
                        last = mm3(b.t[:, q * 256:q * 256 + 256], (wh[:, cs], wl[:, cs]), tuple(t[:, k, :] for t in yT),
                                   k == 0, k == 7, tk, w_mT[k], b.rel)
                    wdone(i, last)
                    if q == 0:
                        yield
                op = acopy(kmT[:, j:j + 2, :], b.t[:, :].rearrange("p (a b) -> p a b", a=2), last)
                free(b, op)
                t_kmT[j] = t_kmT[j + 1] = op
                yield
            t_vm = []
            for g in range(2):
                b = [bank(), bank()]
                for j in range(4):
                    wh, wl, tk, i = wnext("w_xv", g * 4 + j)
                    for k in range(2):
                        for tb in range(2):
                            cs = slice(k * 512, k * 512 + 512)
                            x = tuple(t[:, 2 * j + k, tb * 128:tb * 128 + 128] for t in yT)
                            last = mm3(b[tb].t[:, :], x, (wh[:, cs], wl[:, cs]), j + k == 0, 2 * j + k == 7,
                                       tk, w_mT[2 * j + k], b[tb].rel)
                    wdone(i, last)
                    if j < 3:
                        yield
                for tb in range(2):
                    op = acopy(vm[:, tb, g * 512:g * 512 + 512], b[tb].t[:, :], last)
                    free(b[tb], op)
                    t_vm.append(op)
                yield
            R["kmT"], R["vm"], R["km"] = t_kmT, t_vm, last

        t_yT = [None] * 8

        def seg(kb, r):
            return slice(r * 1024, r * 1024 + 1024) if kb == 0 else slice(2048 + r * 512, 2560 + r * 512)
        t_z = []
        for r in range(2):
            for hp in range(2):
                b = bank()
                for q in range(2):
                    i = hp * 2 + q
                    last = mm(b.t[:, q * 256:q * 256 + 256], sT[64 * r:64 * r + 64, 4 + i, 0:128],
                              sT[64 * r:64 * r + 64, i, :], True, True, b.rel, t_sT[i], t_sT[4 + i])
                op = vts1(zs[:, r * 1024 + hp * 512:r * 1024 + hp * 512 + 512], b.t[:, :], 0.125, ALU.mult, last)
                free(b, op)
                t_z.append(op)
            b = bank()
            for i in range(4):
                last = mm(b.t[:, i * 128:i * 128 + 128], sT[64 * r:64 * r + 64, 4 + i, 128:256],
                          sT[64 * r:64 * r + 64, i, 128:256], True, True, b.rel)
            op = vts1(zs[:, seg(1, r)], b.t[:, :], 0.125, ALU.mult, last)
            free(b, op)
            t_z.append(op)
        t_qkT = to_T32(tbs(qk), qkT, 8, t_rope)

        t_s1, t_s0 = [], []
        for c in range(2):
            rs = slice(64 * c, 64 * c + 64)
            for hp in range(2):
                b = bank()
                for q in range(2):
                    h = hp * 2 + q
                    last = mm(b.t[:, q * 256:q * 256 + 256], qkT[rs, h, 128:256], qkT[rs, 4 + h, :], True, True,
                              b.rel, t_qkT[h], t_qkT[4 + h])
                op = vstt(P1[:, c * 4 + hp * 2:c * 4 + hp * 2 + 2, :], b.t[:, :].rearrange("p (a b) -> p a b", a=2),
                          0.125, bc(D("maskA"), 1, 2), ALU.mult, ALU.add, last, t_d)
                free(b, op)
                t_s1.append(op)
            b = bank()
            for h in range(4):
                last = mm(b.t[:, h * 128:h * 128 + 128], qkT[rs, h, 0:128], qkT[rs, 4 + h, 0:128], True, True, b.rel)
            op = vstt(P0[:, c * 4:c * 4 + 4, :], b.t[:, :].rearrange("p (a b) -> p a b", a=4),
                      0.125, bc(D("maskA")[:, 128:256], 1, 4), ALU.mult, ALU.add, last)
            free(b, op)
            t_s0.append(op)
        def stick():
            thirds = [slice(1024 * k, 1024 * k + 1024) for k in range(3)]
            a = [None] * 3
            for f, kw in ((ACT.Abs, {}), (ACT.Exp, {"scale": -1.0}), (ACT.Ln, {"bias": 1.0})):
                for k, th in enumerate(thirds):
                    a[k] = act(ez[:, th], (zs if f == ACT.Abs else ez)[:, th], f, t_z, a[k], **kw)
                    yield
            v = []
            for k, th in enumerate(thirds):
                v.append(vstt(ez[:, th], zs[:, th], 0.0, ez[:, th], ALU.max, ALU.add, a[k]))
                if k < 2:
                    yield

            def diag(t, kb):
                if kb == 0:
                    return t[:, 0:2048].rearrange("p (h q) -> p h q", q=256)[:, :, 0:128]
                return t[:, 2048:3072].rearrange("p (h q) -> p h q", q=128)
            yield
            t_sp = [vtt(diag(ez, kb), diag(ez, kb), bc(D("maskS"), 1, 8), ALU.mult, v, t_d) for kb in range(2)]
            yield
            t_e = []
            for r in range(2):
                for hp in range(2):
                    b = bank()
                    o = r * 1024 + hp * 512
                    mm(b.t[:, :], D("negtri"), ez[:, o:o + 512], True, False, b.rel, t_sp)
                    o1 = 2048 + r * 512 + hp * 256
                    last = mm(b.t[:, :].rearrange("p (h q) -> p h q", q=256)[:, :, 128:256], D("negones"),
                              ez[:, o1:o1 + 256].rearrange("p (h q) -> p h q", q=128), False, True)
                    op = vtt(zs[:, o:o + 512], b.t[:, :], zs[:, o:o + 512], ALU.add, last)
                    free(b, op)
                    t_e.append(op)
                    yield
                b = bank()
                last = mm(b.t[:, :], D("negtri"), ez[:, seg(1, r)], True, True, b.rel)
                op = vtt(zs[:, seg(1, r)], b.t[:, :], zs[:, seg(1, r)], ALU.add, last)
                free(b, op)
                t_e.append(op)
            yield
            a = []
            for th in thirds:
                a.append(act(zs[:, th], zs[:, th], ACT.Exp, t_e))
                yield
            t_a = [vtt(diag(zs, kb), diag(zs, kb), bc(D("maskS"), 1, 8), ALU.mult, a) for kb in range(2)]
            yield "memory"
            for hp in range(2):
                b = bank()
                for q in range(2):
                    i = hp * 2 + q
                    for r in range(2):
                        h = 2 * i + r
                        o = b.t[64 * r:64 * r + 64, q * 256:q * 256 + 256]
                        mm(o, vs[:, 0, h * 64:h * 64 + 64], zs[:, r * 1024 + i * 256:r * 1024 + i * 256 + 256],
                           True, False, b.rel, t_a, t_v["vs"])
                        o1 = 2048 + r * 512 + i * 128
                        last = mm(o[:, 128:256], vs[:, 1, h * 64:h * 64 + 64], zs[:, o1:o1 + 128], False, True)
                op = evac_hl([t[:, 4 + hp * 2:6 + hp * 2, :] for t in yT], b.t[:, :].rearrange("p (a b) -> p a b", a=2), last, R["km"])
                free(b, op[1])
                yield
                t_yT[4 + hp * 2] = t_yT[5 + hp * 2] = op


        def differential():
            t_w = []
            for qb, Pq, w in ((0, P0, t_s0), (1, P1, t_s1)):
                k = Pq.shape[2]
                a, v = yield from softmax(Pq[:, :, :], 8, w, mlr[:, qb, 0, :], mlr[:, qb, 1, :])
                yield
                v = V(lambda e, qb=qb: e.reciprocal(mlr[:, qb, 2, :], mlr[:, qb, 1, :]), v)
                v = vts1(mlr[:, qb, 2, 4:8], mlr[:, qb, 2, 4:8], nlam, ALU.mult, v, t_lam)
                v = vtt(Pq[:, :, :], Pq[:, :, :], bc(mlr[:, qb, 2, :], 2, k), ALU.mult, v)
                yield
                t_w.append(vtt(Pq[:, 0:4, :], Pq[:, 0:4, :], Pq[:, 4:8, :], ALU.add, v))
            yield
            t_wT = []
            for j in range(2):
                b = bank()
                for q in range(4):
                    i = j * 4 + q
                    last = tp(b.t[:, q * 128:q * 128 + 128], P1[:, i // 2, (i % 2) * 128:(i % 2) * 128 + 128], b.rel, t_w[1])
                op = copy(W1T[:, j * 4:j * 4 + 4, :], b.t[:, :].rearrange("p (a b) -> p a b", a=4), last)
                free(b, op)
                t_wT.append(op)
                yield
            b = bank()
            for h in range(4):
                last = tp(b.t[:, h * 128:h * 128 + 128], P0[:, h, :], b.rel, t_w[0])
            op = copy(W0T[:, :, :], b.t[:, :].rearrange("p (a b) -> p a b", a=4), last)
            free(b, op)
            t_w0 = op
            t_on = []
            for qb in range(2):
                b = bank()
                for h in range(4):
                    hs = slice(h * 128, h * 128 + 128)
                    if qb == 0:
                        last = mm(b.t[:, hs], W0T[:, h, :], va[:, 0, hs], True, True, b.rel, t_w0, t_v["va"])
                    else:
                        mm(b.t[:, hs], W1T[:, h * 2, :], va[:, 0, hs], True, False, b.rel, t_wT, t_v["va"])
                        last = mm(b.t[:, hs], W1T[:, h * 2 + 1, :], va[:, 1, hs], False, True)
                v = vcopy(od[:, qb, :], b.t[:, :], last)
                free(b, v)
                v4 = lambda t: t[:, qb, :].rearrange("p (a b) -> p a b", a=4)
                yield
                q = vtt(osq[:, qb, :], od[:, qb, :], od[:, qb, :], ALU.mult, v)
                q = vred(ost[:, qb, 0:4], v4(osq), ALU.add, q)
                q = vts(ost[:, qb, 4:8], ost[:, qb, 0:4], 1.0 / 128, 1e-6, ALU.mult, ALU.add, q)
                q = rsqrt(ost[:, qb, 4:8], ost[:, qb, 4:8], q)
                q = vts1(ost[:, qb, 4:8], ost[:, qb, 4:8], 1.0 - (0.8 - 0.6 * math.exp(0.0)), ALU.mult, q)
                t_on.append(vtt(v4(od), v4(od), bc(ost[:, qb, 4:8], 2, 128), ALU.mult, q))
            R["on"] = t_on

        mem_ = memory()
        next(mem_)
        sides = [stick(), differential()]
        held = set()
        for _ in mem_:
            for g in (sides[0], sides[1], sides[0]):
                if g not in held and next(g, "memory") == "memory":
                    held.add(g)
        for g in sides:
            for _ in g:
                pass
        t_on = R["on"]
        t_yT[0:4] = to_T(tbs(od), yT, 4, gcols("g_subln") * 4, t_on, R["km"])
        t_h1 = residual(hB, hA, yT, t_yT, "w_out", t_x, ((2, 3), (0, 1)))
        if stop == 1:
            return finish(nc, Q, sems, ctx, outs, hB, t_h1, load)

        SB = S.sub()
        PX = sbuf(SB, "PX", [128, 2, 4, 256])
        PXT = sbuf(SB, "PXT", [128, 2, 4, 256])
        mx = sbuf(SB, "mx", [128, 2, 3, 4])
        t_kmT, t_vm = R["kmT"], R["vm"]
        w_xT = to_T(tbs(hB), xT, 8, gcols("g_cross"), t_h1)
        sx = [rstd(hB[:, tb, :], 1024, t_h1[tb]) for tb in range(2)]
        s16 = [stat(), stat()]
        t_s16 = [vts1(s16[tb], sx[tb][0], 1.0 / 16, ALU.mult, sx[tb][1]) for tb in range(2)]
        t_sT = [None] * 8
        projT(xT, w_xT, "w_xq", 8, ev_sT)
        t_pT = []
        t_p = []
        for tb in range(2):
            ts = slice(tb * 128, tb * 128 + 128)
            for hp in range(2):
                hs = slice(2 * hp, 2 * hp + 2)
                b = bank()
                for q in range(2):
                    h = hp * 2 + q
                    for k in range(2):
                        last = mm(b.t[:, q * 256:q * 256 + 256], sT[:, 2 * h + k, ts], kmT[:, 2 * h + k, :], k == 0, k == 1,
                                  b.rel, t_sT, t_kmT)
                m = mx[:, tb, 0, hs]
                op = vred(m, b.t[:, :].rearrange("p (a b) -> p a b", a=2), ALU.max, last)
                op = vts(m, m, s16[tb], -1.0, ALU.mult, ALU.mult, op, t_s16[tb])
                v = []
                for q in range(2):
                    h = hp * 2 + q
                    v.append(act(PX[:, tb, h, :], b.t[:, q * 256:q * 256 + 256], ACT.Exp, op, last, t_s16[tb], scale=s16[tb],
                                 bias=mx[:, tb, 0, h:h + 1], acc=mx[:, tb, 1, h:h + 1]))
                free(b, v[-1])
                t_p.append((tb, hp, hs, v))
        norms = []
        for tb, hp, hs, v in t_p:
            v = V(lambda e, tb=tb, hs=hs: e.reciprocal(mx[:, tb, 2, hs], mx[:, tb, 1, hs]), v)
            norms.append(vtt(PX[:, tb, hs, :], PX[:, tb, hs, :], bc(mx[:, tb, 2, hs], 2, 256), ALU.mult, v))
        t_pT = [[], []]
        for (tb, hp, hs, _), v in zip(t_p, norms):
            b = bank()
            for kb in range(2):
                for q in range(2):
                    last = tp(b.t[:, kb * 256 + q * 128:kb * 256 + q * 128 + 128], PX[:, tb, 2 * hp + q, kb * 128:kb * 128 + 128], b.rel, v)
            op = copy(PXT[:, :, hs, tb * 128:tb * 128 + 128], b.t[:, :].rearrange("p (a b c) -> p a b c", a=2, b=2), last)
            free(b, op)
            t_pT[hp].append(op)
        t_oT = []
        for j in range(4):
            b = bank()
            for q in range(2):
                n = 2 * j + q
                for kb in range(2):
                    last = mm(b.t[:, q * 256:q * 256 + 256], vm[:, kb, n * 128:n * 128 + 128], PXT[:, kb, j, :], kb == 0, kb == 1,
                              b.rel, t_vm, t_pT[j // 2])
            op = evac_hl([t[:, 2 * j:2 * j + 2, :] for t in yT], b.t[:, :].rearrange("p (a b) -> p a b", a=2), last)
            free(b, op[1])
            t_oT += [op, op]
        t_h2 = residual(hA, hB, yT, t_oT, "w_xo", t_h1)
        if stop == 2:
            return finish(nc, Q, sems, ctx, outs, hA, t_h2, load)

        SC = S_AD.sub()
        ahl = sbuf(SC, "ahl", [128, 2, 32, 256], F32R)
        ar = sbuf(SC, "ar", [128, 2, 2, 256])
        as_ = sbuf(SC, "as_", [128, 2, 2, 256])
        w_xT = to_T(tbs(hA), xT, 8, gcols("g_mlp"), t_h2)
        sx = [rstd(hA[:, tb, :], 1024, t_h2[tb]) for tb in range(2)]
        s2 = [stat(), stat()]
        t_s2 = [vtt(s2[tb], sx[tb][0], sx[tb][0], ALU.mult, sx[tb][1]) for tb in range(2)]
        t_aT = [None] * 32

        def ev_up(b, j, c, last):
            u = j // 2 % 2
            w = t_aT[j - 4] if j >= 4 else None
            a = act(ar[:, u, :, :], b.t[:, :].rearrange("p (a b) -> p a b", a=2), ACT.Relu, last, w)
            v = vtt(as_[:, u, :, :], ar[:, u, :, :], ar[:, u, :, :], ALU.mult, a, w)
            h, l = (ahl[:, q, j:j + 2, :] for q in range(2))
            c_ = acopy(h, as_[:, u, :, :], v)
            t_aT[j] = t_aT[j + 1] = [c_, vtt(l, as_[:, u, :, :], h.bitcast(F32), ALU.subtract, c_)]
            return a
        projT(xT, w_xT, "w_up", 32, ev_up)
        bb = [bank() for _ in range(4)]
        for k0 in (*range(30), 30):
            ks = (30, 31) if k0 == 30 else (k0,)
            p = {k: wnext("w_down", k) for k in ks}
            last = {}
            for tb in range(2):
                for k in ks:
                    wh, wl, tk, i = p[k]
                    for g in range(2):
                        b = bb[tb * 2 + g]
                        cs = slice(g * 512, g * 512 + 512)
                        last[tb] = mm3(b.t[:, :], tuple(ahl[:, q, k, tb * 128:tb * 128 + 128] for q in range(2)), (wh[:, cs], wl[:, cs]),
                                       k == 0, k == 31, b.rel, tk, t_aT[k])
                    if tb:
                        wdone(i, last[1])
        t_h3 = [[], []]
        for tb in range(2):
            for g in range(2):
                gs = slice(g * 512, g * 512 + 512)
                op = vstt(hB[:, tb, gs], bb[tb * 2 + g].t[:, :], s2[tb], hA[:, tb, gs], ALU.mult, ALU.add, last[tb], t_s2[tb])
                free(bb[tb * 2 + g], op)
                t_h3[tb].append(op)
        gg = stats[:, 88:96]
        t_gg = vtt(gg, par_("g_final"), par_("g_mix_2"), ALU.mult, t_par)
        w_xT = to_T(tbs(hB), xT, 8, [gg[:, k:k + 1] for k in range(8)], [[v, t_gg] for v in t_h3])
        sq = stats[:, 76:84]
        t_q = [vtt(hA[:, tb, :], hB[:, tb, :], rows[:, 0:1024], ALU.mult, t_h3[tb], t_rows) for tb in range(2)]
        v = []
        for k, src, w in ((0, hB, t_h3), (2, hA, t_q)):
            for tb in range(2):
                t_junk[0] = act(junk[:, :], src[:, tb, :], ACT.Square, w[tb], t_junk[0], acc=sq[:, k + tb:k + tb + 1])
                v.append(t_junk[0])
        r1, r2 = sq[:, 4:6], sq[:, 6:8]
        v1 = vts(r1, sq[:, 0:2], 1.0 / 1024, 1e-6, ALU.mult, ALU.add, v[0:2])
        v1 = rsqrt(r1, r1, v1)
        v2 = vtt(r2, r1, r1, ALU.mult, v1)
        v2 = vtt(r2, r2, sq[:, 2:4], ALU.mult, v2, v)
        v2 = vts(r2, r2, 1.0 / 1024, 1e-6, ALU.mult, ALU.add, v2)
        v2 = rsqrt(r2, r2, v2)
        v2 = vtt(r2, r2, r1, ALU.mult, v2)
        sx = [(r2[:, tb:tb + 1], v2) for tb in range(2)]
        rows_ = rows_of([r2[:, tb:tb + 1] for tb in range(2)], [v2, v2])
        next(rows_)
        t_x2 = [vts1(hA[:, tb, :], hA[:, tb, :], r1[:, tb:tb + 1], ALU.mult, v1, v) for tb in range(2)]
        if stop == 3:
            return finish(nc, Q, sems, ctx, outs, hA, t_x2, load)

        SD = S_AD.sub()
        yA = sbuf(SD, "yA", [128, 2, 512])
        pR = sbuf(SD, "pR", [128, 14, 257])
        SR = SD.sub()
        pm = sbuf(SR, "pm", [128, 14, 256])
        prep_at = SR.at
        prep = sbuf(SR, "prep", [128, 5, 4, 256])
        Pc = sbuf(SR, "Pc", [128, 4, 256])
        ARt = sbuf(SR, "ARt", [128, 4, 2, 256])
        be_at = SR.at
        be = sbuf(SR, "be", [128, 4, 256])
        ka = sbuf(SR, "ka", [128, 4, 256])
        bon = sbuf(SR, "bon", [128, 16])
        SI = SR.sub()
        tok_at = SI.at
        atok = sbuf(SI, "atok", [128, 2, 512])
        btok = sbuf(SI, "btok", [128, 2, 512])
        ktok = sbuf(SI, "ktok", [128, 2, 512])
        vtok = sbuf(SI, "vtok", [128, 2, 512])
        Y = sbuf(SI, "rwY", [128, 16, 128])
        vM = sbuf(SI, "vM", [128, 2, 512])
        mst = sbuf(SI, "mst", [128, 2, 3, 8])
        qst = sbuf(SI, "qst", [128, 2, 2, 16])
        yst = sbuf(SI, "yst", [128, 3, 16])
        SM = Mem(nc, tok_at, P.end)
        cq = sbuf(SM, "cq", [128, 2, 672])
        cn = sbuf(SM, "cn", [128, 2, 640])
        chl = sbuf(SM, "chl", [128, 2, 5, 256], F32R)
        cT = (chl[:, 0, :, :], chl[:, 1, :, :])
        SL = Mem(nc, spl_at, spl_at + NSP * 8192)
        QK = sbuf(SL, "QK", [128, 2, 2, 8, 96])
        Mx = sbuf(SL, "Mx", [128, 3072])
        qT2 = sbuf(Mem(nc, prep_at, P.end), "qT2", [96, 2, 8, 256])
        M1 = Mx[:, 0:2048].rearrange("p (h k) -> p h k", h=8)
        M0 = Mx[:, 2048:3072].rearrange("p (h k) -> p h k", h=8)
        sq_ = Mx[:, :].rearrange("p (t j d) -> p t j d", t=2, j=16)
        QKf = QK[:, :, :, :, :].rearrange("p t j h d -> p (t j h d)")
        MT1 = QKf[:, 0:2048].rearrange("p (h k q) -> p h k q", h=8, k=2)
        MT0 = QKf[:, 2048:3072].rearrange("p (h q) -> p h q", h=8)
        rt2 = junk[:, :].rearrange("p (i n d) -> p i n d", i=4, n=16)
        ld, aa, cum, t0, t1 = (prep[:, i, :, :] for i in range(5))
        gtok = rows[:, 0:1024].rearrange("p (t n) -> p t n", t=2)
        mu, kkc, kac, rkc = (gcols(k) for k in ("rwkv_mu", "k_k", "k_a", "r_k"))
        pRf = pR[:, :, :].rearrange("p a b -> p (a b)")
        f2 = lambda t: t[:, :, :].rearrange("p a b -> p (a b)")
        sg, x2_, y_ = hx[:, 0, 0, 0:256], ARt[:, :, 0, :], hx[:, 0, 1, :].rearrange("p (a b) -> p a b", b=256)
        t_dx = [t_x2, w_xT]
        lend("w_o")

        t_mz = V(lambda e: e.memset(pR[:, :, 0:1], 0.0), t_x2)
        t_pR, t_pm = [None] * 14, [None] * 14

        def columns(nm, j, f):
            col_end(f, *col_mm(nm, j))

        def col_mm(nm, j):
            b = bank()
            for q in range(2):
                wh, wl, tk, i = wnext(nm, j + q)
                for k in range(8):
                    cs = slice(k * 128, k * 128 + 128)
                    last = mm3(b.t[:, q * 256:q * 256 + 256], (wh[:, cs], wl[:, cs]), tuple(t[:, k, :] for t in xT),
                               k == 0, k == 7, tk, w_xT[k], b.rel)
                wdone(i, last)
            return b, last

        def col_end(f, b, last):
            op = vtt(pR[:, f:f + 2, 1:257], b.t[:, :].rearrange("p (a b) -> p a b", a=2), bc(rw[:, :], 1, 2), ALU.mult, last, t_rw)
            free(b, op)
            t_pR[f] = t_pR[f + 1] = op

        def mix(f0, f1):
            v = vtt(pm[:, f0:f1, :], pR[:, f0:f1, 0:256], pR[:, f0:f1, 1:257], ALU.subtract, t_pR[f0:f1], t_mz)
            for i in range(f0, f1):
                t_pm[i] = vstt(pm[:, i, :], pm[:, i, :], mu[i], pR[:, i, 1:257], ALU.mult, ALU.add, v)
        c0, c1 = col_mm("w_rwkv_0", 0), col_mm("w_rwkv_0", 2)
        t_rw = run(rows_)
        col_end(12, *c0)
        mix(12, 14)
        t_tw = act(t0[0:64, 0, :], pm[0:64, 12, :], ACT.Tanh, t_pm[12])
        t_sg = act(sg[:, :], pm[:, 13, :], ACT.Sigmoid, t_pm[13], t_dx)
        col_end(4, *c1)
        mix(4, 6)
        columns("w_rwkv_0", 4, 6)
        mix(6, 8)
        vk = [vts1(t1[:, i, :], pm[:, 4 + i, :], kkc[i], ALU.mult, t_pm[4 + i]) for i in range(4)]
        t_sq = vtt(f2(be), f2(t1), f2(t1), ALU.mult, vk)
        columns("w_rwkv_0", 6, 0)
        mix(0, 2)
        wt, _, t_lw, i_lw = wnext("w_lora", 0)
        w2s, a2s, g2s = wt[0:64, 0:512], wt[64:128, 0:512], wt[:, 512:1024]
        t_ld, t_aa, t_g, t_x2_ = [], [], [], []
        for j in range(2):
            b = bank()
            for q in range(2):
                i = 2 * j + q
                last = mm(b.t[:, q * 256:q * 256 + 256], w2s[:, i * 128:i * 128 + 128], t0[0:64, 0, :], True, True,
                          b.rel, t_lw, t_tw)
            for q in range(2):
                i = 2 * j + q
                op = act(ld[:, i, :], b.t[:, q * 256:q * 256 + 256], ACT.Sigmoid, last, bias=gcols("w0")[i])
                t_ld.append(op)
            free(b, op)
        for j in range(2):
            b = bank()
            last = mm(b.t[:, :], D("blk"), be[:, 2 * j:2 * j + 2, :], True, True, b.rel, t_sq)
            op = vts1(x2_[:, 2 * j:2 * j + 2, :], b.t[:, :].rearrange("p (a b) -> p a b", a=2), 1e-24, ALU.max, last)
            free(b, op)
            t_x2_.append([op, last])
        t_l2 = last
        for j in range(2):
            b = bank()
            for q in range(2):
                i = 2 * j + q
                last = mm(b.t[:, q * 256:q * 256 + 256], a2s[:, i * 128:i * 128 + 128], pm[64:128, 12, :], True, True,
                          b.rel, t_lw, t_pm[12])
            for q in range(2):
                i = 2 * j + q
                op = act(aa[:, i, :], b.t[:, q * 256:q * 256 + 256], ACT.Sigmoid, last, bias=gcols("a0")[i])
                t_aa.append(op)
            free(b, op)
        for tb in range(2):
            b = bank()
            last = mm(b.t[:, :], sg[:, tb * 128:tb * 128 + 128], g2s, True, True, b.rel, t_sg)
            op = acopy(gtok[:, tb, :], b.t[:, :], last)
            free(b, op)
            t_g.append(op)
        wdone(i_lw, last)
        R["rows_used"] = t_pR
        v = [vts1(ld[:, i, :], ld[:, i, :], -math.exp(-0.5), ALU.mult, t_ld[i]) for i in range(4)]
        t_cum = [V(lambda e, i=i: e.tensor_tensor_scan(cum[:, i, :], D("rst"), ld[:, i, :], 0.0, ALU.mult, ALU.add), v[i])
                 for i in range(4)]
        v = vtt(f2(ld), f2(cum), f2(ld), ALU.subtract, t_cum)
        columns("w_rwkv_1", 0, 2)
        mix(2, 4)
        columns("w_rwkv_1", 2, 8)
        t_y0 = [act(y_[:, 2 * j:2 * j + 2, :], x2_[:, 2 * j:2 * j + 2, :], ACT.Ln, t_x2_[j], t_dx) for j in range(2)]
        t_y0 = [act(y_[:, 2 * j:2 * j + 2, :], y_[:, 2 * j:2 * j + 2, :], ACT.Exp, t_y0, scale=-0.5) for j in range(2)]
        columns("w_rwkv_1", 4, 10)
        t_P = act(Pc[:, :, :], cum[:, :, :], ACT.Exp, t_cum)
        t_Pp = act(ld[:, :, :], ld[:, :, :], ACT.Exp, v)
        t_Pi = act(cum[:, :, :], cum[:, :, :], ACT.Exp, t_P, v, scale=-1.0)
        vk = [vts(t0[:, i, :], aa[:, i, :], 1.0, kac[i], ALU.subtract, ALU.mult, t_aa[i], t_l2) for i in range(4)]
        t_kp = vstt(f2(t0), f2(t0), 1.0, pm[:, 4:8, :].rearrange("p a b -> p (a b)"), ALU.add, ALU.mult, vk, t_pm[4:8])
        t_ka = G(lambda e: e.tensor_tensor(f2(ka), f2(t0), f2(cum), ALU.mult), t_kp, t_Pi)
        t_kk, t_al, t_be, t_rho = [], [], [], []
        for j in range(2):
            js = slice(2 * j, 2 * j + 2)
            z, y, x = be[:, js, :], y_[:, js, :], x2_[:, js, :]
            t_rho.append(vtt(ARt[:, js, 1, :], pm[:, js, :], Pc[:, js, :], ALU.mult, t_P, t_pm[0:4]))
            api = vtt(aa[:, js, :], aa[:, js, :], cum[:, js, :], ALU.mult, t_aa, t_Pi, vk)
            r_ = vtt(z, y, y, ALU.mult, t_y0[j], t_x2_)
            r_ = vtt(z, z, x, ALU.mult, r_)
            r_ = vts(z, z, -0.5, 1.5, ALU.mult, ALU.add, r_)
            r_ = vtt(y, y, z, ALU.mult, r_)
            t_kk.append(vtt(t1[:, js, :], t1[:, js, :], y, ALU.mult, r_))
            t_al.append(vtt(ARt[:, js, 0, :], t1[:, js, :], ld[:, js, :], ALU.mult, t_kk[j], t_Pp))
            t_be.append(vtt(z, t1[:, js, :], aa[:, js, :], ALU.mult, t_kk[j], api, r_))
        bq = [bank() for _ in range(4)]
        for k in range(8):
            wh, wl, tk, i = wnext("w_mla", k)
            for tb in range(2):
                xs = tuple(t[:, k, tb * 128:tb * 128 + 128] for t in xT)
                mm3(bq[tb].t[:, 0:384], xs, (wh[:, 0:384], wl[:, 0:384]), k == 0, k == 7, bq[tb].rel, tk, w_xT[k])
                last = mm3(bq[2 + tb].t[:, 0:288], xs, (wh[:, 384:672], wl[:, 384:672]), k == 0, k == 7, bq[2 + tb].rel)
            wdone(i, last)
        t_cq = [[], []]
        for tb in range(2):
            for j, lo, hi in ((0, 0, 384), (1, 384, 672)):
                b = bq[2 * j + tb]
                op = act(cq[:, tb, lo:hi], b.t[:, 0:hi - lo], ACT.Copy, last, sx[tb][1], scale=sx[tb][0])
                free(b, op)
                t_cq[tb].append(op)
        GB = hx[:, :, :, :].rearrange("p i t n -> p (i t n)").rearrange("p (n d) -> p n d", d=256)
        GK = prep[:, 0:4, :, :].rearrange("p a b c -> p (a b) c")
        xm = Mem(nc, x_at, P.end)
        ysq, TAT, nU = xm("ysq", [128, 16, 64]), xm("TAT", [128, 4, 256]), xm("nU", [128, 2, 512])
        pmf = pm[:, 0:8, :].rearrange("p a b -> p (a b)")
        c64 = lambda t, k: t[:, 1024 * k:1024 * k + 1024].rearrange("p (n d) -> p n d", d=64)
        QX, Xc, Yc = c64(pRf, 0), c64(pmf, 0), c64(pmf, 1)
        prob = lambda b_, r, i: (b_ * 2 + r) * 4 + i
        t_GB, t_GK = [], []

        def products(kind, *w0):
            for hp in range(2):
                for b_ in range(2):
                    ts = slice(b_ * 128, b_ * 128 + 128)
                    for r in range(2):
                        rs = slice(64 * r, 64 * r + 64)
                        b = bank()
                        for q in range(2):
                            i = hp * 2 + q
                            src, w = ((be, t_be[hp]), (ka, t_ka))[kind]
                            last = mm(b.t[:, q * 256:q * 256 + 256].rearrange("p (a b) -> p a b", a=2), src[rs, i, ts],
                                      ARt[rs, i, :, ts], True, True, b.rel, w, t_al[hp], t_rho[hp])
                        p0 = prob(b_, r, hp * 2)
                        op = vtt((GB, GK)[kind][:, p0:p0 + 2, :], b.t[:, :].rearrange("p (a b) -> p a b", a=2),
                                 bc(D("m2"), 1, 2), ALU.mult, last, t_kk, t_g, *w0)
                        free(b, op)
                        (t_GB, t_GK)[kind].append(op)
                        yield
        vk = [vstt(ld[:, i, :], pm[:, i, :], rkc[i], t0[:, i, :], ALU.mult, ALU.mult, t_kp, t_al) for i in range(4)]
        parts = [(tb, lo, hi) for lo, hi in ((0, 384), (384, 640)) for tb in range(2)]
        rs_ = [rstd(cq[:, tb, lo:hi], hi - lo, t_cq[tb]) for tb, lo, hi in parts]
        n_c = [[], []]
        for (tb, lo, hi), (s, v) in zip(parts, rs_):
            n_c[tb].append(vts1(cn[:, tb, lo:hi], cq[:, tb, lo:hi], s, ALU.mult, v, t_cq[tb]))
        run(products(0))
        w_cT = to_T(tbs(cn), cT, 5, gcols("g_cq") + gcols("g_ckv"), n_c)
        b = bank()
        for tb in range(2):
            for i in range(4):
                last = mm(b.t[:, tb * 8 + 2 * i:tb * 8 + 2 * i + 2], ld[:, i, tb * 128:tb * 128 + 128], D("hsel"), True, True, b.rel, vk)
        t_bon = [vcopy(bon[:, :], b.t[:, 0:16], last)]
        free(b, t_bon)
        halves = [slice(64 * c, 64 * c + 64) for c in range(2)]
        t_Xc, t_Yc = [None, None], [None, None]
        for j in range(2):
            js = slice(8 * j, 8 * j + 8)
            v = [vstt(Yc[hs, js, :], GB[hs, js, 64 * c:64 * c + 64], -1.0, bc(D("ly0")[hs, :], 1, 8), ALU.mult, ALU.mult,
                      t_GB, t_bon, t_rho, t_kp) for c, hs in enumerate(halves)]
            t_Yc[j] = vtt(Yc[:, js, :], Yc[:, js, :], bc(D("eye2"), 1, 8), ALU.add, v)
            t_Xc[j] = V(lambda e, js=js: e.transpose(Xc[:, js, :].rearrange("p a b -> p (a b)"),
                                                     Yc[:, js, :].rearrange("p a b -> p (a b)")), t_Yc[j], t_bon)
        bq, bk = [bank() for _ in range(4)], [bank() for _ in range(4)]
        for k in range(3):
            wh, wl, tk, i = wnext("w_uq", k)
            for tb in range(2):
                xs = tuple(t[:, k, tb * 128:tb * 128 + 128] for t in cT)
                mm3(bq[tb].t[:, 0:480], xs, (wh[:, 0:480], wl[:, 0:480]), k == 0, k == 2, bq[tb].rel, tk, w_cT[k])
                last = mm3(bq[2 + tb].t[:, 0:288], xs, (wh[:, 480:768], wl[:, 480:768]), k == 0, k == 2, bq[2 + tb].rel)
            wdone(i, last)
        for k in range(2):
            wh, wl, tk, i = wnext("w_ukv", k)
            for tb in range(2):
                xs = tuple(t[:, 3 + k, tb * 128:tb * 128 + 128] for t in cT)
                mm3(bk[tb].t[:, :], xs, (wh[:, 0:512], wl[:, 0:512]), k == 0, k == 1, bk[tb].rel, tk, w_cT[3 + k])
                last = mm3(bk[2 + tb].t[:, :], xs, (wh[:, 512:1024], wl[:, 512:1024]), k == 0, k == 1, bk[2 + tb].rel)
            wdone(i, last)
        t_q, t_vM, t_kr = [[], []], [], []
        for tb in range(2):
            for j, lo, hi in ((0, 0, 5), (1, 5, 8)):
                b = bq[2 * j + tb]
                op = acopy(QK[:, tb, 0, lo:hi, :], b.t[:, 0:(hi - lo) * 96].rearrange("p (a b) -> p a b", b=96), last)
                free(b, op)
                t_q[tb].append(op)
            op = acopy(QK[:, tb, 1, :, 0:64], bk[tb].t[:, :].rearrange("p (a b) -> p a b", b=64), last)
            free(bk[tb], op)
            t_q[tb].append(op)
            op = vcopy(vM[:, tb, :], bk[2 + tb].t[:, :], last)
            free(bk[2 + tb], op)
            t_vM.append(op)
            t_kr.append(G(lambda e, tb=tb: e.tensor_copy(QK[:, tb, 1, :, 64:96], bc(cq[:, tb, 640:672], 1, 8)), t_cq[tb], last))
            t_q[tb].append(t_kr[-1])
        t_c = [t_kr, last]
        mix(8, 12)
        t_rn = t_pm
        xa = Mem(nc, be_at, P.end)("yha", [128, 2, 4, 256], F32R)
        xb = Mem(nc, prep_at, P.end)("yhb", [128, 2, 4, 256], F32R)
        yhA = [xa[:, q, :, :] for q in range(2)]
        yhB = [xb[:, q, :, :] for q in range(2)]
        t_yT = []
        t_qT, t_m1, t_m0, t_ya = [], [], [], []

        def mla():
            t_r, t_sq, t_n = [], [], []
            for tb in range(2):
                h16 = lambda t: t[:, tb, :, :, :].rearrange("p a b c -> p (a b) c")
                v = []
                for j in range(16):
                    v.append(act(sq_[:, tb, j, :], h16(QK)[:, j, :], ACT.Square, t_q[tb], acc=qst[:, tb, 0, j:j + 1]))
                    if j % 8 == 7:
                        yield
                t_sq.append(v)
            for tb in range(2):
                v = vts(qst[:, tb, 1, :], qst[:, tb, 0, :], 1.0 / 96, 1e-6, ALU.mult, ALU.add, t_sq[tb])
                t_r.append(rsqrt(qst[:, tb, 1, :], qst[:, tb, 1, :], v))
            for tb in range(2):
                h16 = lambda t: t[:, tb, :, :, :].rearrange("p a b c -> p (a b) c")
                v = [G(lambda e, j=j, tb=tb: e.tensor_tensor(QK[:, tb, j, :, :], QK[:, tb, j, :, :],
                                                      bc(rows[:, 2048 + 96 * j:2144 + 96 * j], 1, 8), ALU.mult), t_sq[tb], t_rows)
                     for j in range(2)]
                v = G(lambda e, x=h16(QK), r=qst[:, tb, 1, :]: e.tensor_tensor(x, x, bc(r, 2, 96), ALU.mult), v, t_r[tb])
                t_n.append(v)
            yield
            for tb in range(2):
                h16 = lambda t: t[:, tb, :, :, :].rearrange("p a b c -> p (a b) c")
                v = rope(h16(QK)[:, :, 64:80], h16(QK)[:, :, 80:96], trig[:, 1, tb, 8:24], trig[:, 0, tb, 8:24],
                         [rt2[:, i, :, :] for i in range(4)], [t_n[tb], n_c])
                yield
                for j in range(2):
                    for hp in range(2):
                        b = bank()
                        for q in range(4):
                            last = tp(b.t[0:96, q * 128:q * 128 + 128], QK[:, tb, j, hp * 4 + q, :], b.rel, v)
                        op = acopy(qT2[:, j, hp * 4:hp * 4 + 4, tb * 128:tb * 128 + 128],
                                   b.t[0:96, :].rearrange("p (a b) -> p a b", a=4), last, t_al, t_be, t_ka, t_bon)
                        free(b, op)
                        t_qT.append(op)
                        yield
            isq = 96 ** -0.5
            for hp in range(2):
                b = bank()
                for q in range(4):
                    h = hp * 4 + q
                    last = mm(b.t[:, q * 128:q * 128 + 128], qT2[:, 0, h, 0:128], qT2[:, 1, h, 0:128], True, True, b.rel, t_qT)
                op = vstt(M0[:, hp * 4:hp * 4 + 4, :], b.t[:, :].rearrange("p (a b) -> p a b", a=4), isq,
                          bc(D("maskM")[:, 128:256], 1, 4), ALU.mult, ALU.add, last, t_sq)
                free(b, op)
                t_m0.append(op)
                yield
            for hp in range(4):
                b = bank()
                for q in range(2):
                    h = hp * 2 + q
                    last = mm(b.t[:, q * 256:q * 256 + 256], qT2[:, 0, h, 128:256], qT2[:, 1, h, :], True, True, b.rel, t_qT)
                op = vstt(M1[:, hp * 2:hp * 2 + 2, :], b.t[:, :].rearrange("p (a b) -> p a b", a=2), isq,
                          bc(D("maskM"), 1, 2), ALU.mult, ALU.add, last, t_sq)
                free(b, op)
                t_m1.append(op)
                R["qT2"] = last
                yield
            t_sm = []
            for qb, Mq, w in ((0, M0, t_m0), (1, M1, t_m1)):
                a, _ = yield from softmax(Mq[:, :, :], 8, w, mst[:, qb, 0, :], mst[:, qb, 1, :])
                t_sm.append(a)
                yield
            t_mT = [[], []]
            for j in range(2):
                b = bank()
                for q in range(4):
                    last = tp(b.t[:, q * 128:q * 128 + 128], M0[:, j * 4 + q, :], b.rel, t_sm[0])
                op = acopy(MT0[:, j * 4:j * 4 + 4, :], b.t[:, :].rearrange("p (a b) -> p a b", a=4), last)
                free(b, op)
                t_mT[0].append(op)
                yield
            for j in range(4):
                b = bank()
                for q in range(4):
                    h, kb = j * 2 + q // 2, q % 2
                    last = tp(b.t[:, q * 128:q * 128 + 128], M1[:, h, kb * 128:kb * 128 + 128], b.rel, t_sm[1])
                op = acopy(MT1[:, j * 2:j * 2 + 2, :, :], b.t[:, :].rearrange("p (a k b) -> p a k b", a=2, k=2), last)
                free(b, op)
                t_mT[1].append(op)
                yield
            for qb in range(2):
                b = bank()
                for h in range(8):
                    hs = slice(h * 64, h * 64 + 64)
                    if qb == 0:
                        last = mm(b.t[:, hs], MT0[:, h, :], vM[:, 0, hs], True, True, b.rel, t_mT[0], t_vM)
                    else:
                        mm(b.t[:, hs], MT1[:, h, 0, :], vM[:, 0, hs], True, False, b.rel, t_mT[1], t_vM)
                        last = mm(b.t[:, hs], MT1[:, h, 1, :], vM[:, 1, hs], False, True)
                r_l = V(lambda e, qb=qb: e.reciprocal(mst[:, qb, 2, :], mst[:, qb, 1, :]), t_sm[qb])
                o = yA[:, qb, :].rearrange("p (a b) -> p a b", a=8)
                v = vtt(o, b.t[:, :].rearrange("p (a b) -> p a b", a=8), bc(mst[:, qb, 2, :], 2, 64), ALU.mult, last, r_l)
                free(b, v)
                yield
                js = Mx[:, qb * 512:qb * 512 + 512].rearrange("p (a b) -> p a b", a=8)
                q = act(js, o, ACT.Square, v)
                q = vred(mst[:, qb, 0, :], js, ALU.add, q)
                q = vts(mst[:, qb, 1, :], mst[:, qb, 0, :], 1.0 / 64, 1e-6, ALU.mult, ALU.add, q)
                q = rsqrt(mst[:, qb, 1, :], mst[:, qb, 1, :], q)
                t_ya.append(vtt(o, o, bc(mst[:, qb, 1, :], 2, 64), ALU.mult, q))
                yield
            take_back(last, t_ya)
            t_yT.extend(to_T(tbs(yA), yhA, 4, gcols("g_attn_out"), t_ya, [t_GB, t_GK, t_tok["b"], t_tok["k"]]))

        t_tok = {"v": [], "a": [], "b": [], "k": []}

        def tokens():
            for nm, src, dt_, w in (("a", ARt[:, :, 0, :], atok, t_al), ("b", be[:, :, :], btok, t_be),
                                    ("k", ka[:, :, :], ktok, t_ka), ("v", pm[:, 8:12, :], vtok, t_pm[8:12])):
                for tb in range(2):
                    b = bank()
                    for i in range(4):
                        last = tp(b.t[:, i * 128:i * 128 + 128], src[:, i, tb * 128:tb * 128 + 128], b.rel, w)
                    op = acopy(dt_[:, tb, :], b.t[:, :], last, t_c, w_cT)
                    free(b, op)
                    t_tok[nm].append(op)
                    yield

        t_Y0 = G(lambda e: e.memset(Y[:, :, :], 0.0), t_c, w_cT)
        g_mla, g_tok = mla(), tokens()
        g_gk = [None]

        def fill(what):
            for x in what:
                if x == "m":
                    next(g_mla, None)
                elif x == "t":
                    next(g_tok, None)
                else:
                    if g_gk[0] is None:
                        g_gk[0] = products(1, R["qT2"])
                    next(g_gk[0], None)
        plan = list(PLAN)

        def quads(j, lt, rt, *w):
            bs = [bank(), bank()]
            for q in range(8):
                for c, hs in enumerate(halves):
                    last = mm(bs[c].t[hs, q * 64:q * 64 + 64], lt(c, hs, 8 * j + q), rt(hs, 8 * j + q), True, True, bs[c].rel, *w)
            return bs, last

        pv = lambda b, hs: b.t[hs, :].rearrange("p (a b) -> p a b", a=8)
        t_use = [None, None]
        for l in range(1, 6):
            t_Q = [None, None]
            for j in range(2):
                js = slice(8 * j, 8 * j + 8)
                bs, last = quads(j, lambda c, hs, p: GB[hs, p, 64 * c:64 * c + 64], lambda hs, p: Xc[hs, p, :], t_Xc[j], t_GB)
                fill(plan.pop(0))
                t_Q[j] = []
                for c, hs in enumerate(halves):
                    op = vtt(QX[hs, js, :], pv(bs[c], hs), bc(D(f"lx{l}")[hs, :], 1, 8), ALU.mult, last, t_use[j], t_rn)
                    free(bs[c], op)
                    t_Q[j].append(op)
            for j in range(2):
                js = slice(8 * j, 8 * j + 8)
                if l < 5:
                    M, (bs, last) = Xc, quads(j, lambda c, hs, p: Yc[hs, p, :], lambda hs, p: QX[hs, p, :], t_Yc[j], t_Q[j])
                else:
                    M, (bs, last) = Yc, quads(j, lambda c, hs, p: QX[hs, p, :], lambda hs, p: Yc[hs, p, :], t_Yc[j], t_Q[j])
                t_use[j] = last
                fill(plan.pop(0))
                v = []
                for c, hs in enumerate(halves):
                    v.append(vtt(M[hs, js, :], M[hs, js, :], pv(bs[c], hs), ALU.subtract, last, t_Xc[j], t_Yc[j]))
                    free(bs[c], v[-1])
                if l < 5:
                    t_Xc[j] = v
                    t_Yc[j] = V(lambda e, js=js: e.transpose(Yc[:, js, :].rearrange("p a b -> p (a b)"),
                                                             Xc[:, js, :].rearrange("p a b -> p (a b)")), v)
                else:
                    t_Yc[j] = v
        run(g_tok)
        if g_gk[0] is None:
            g_gk[0] = products(1, R["qT2"])
        run(g_gk[0])
        t_inv = t_use[1]
        t_Y = [t_Y0, acopy(Y[0:64, :, 0:64], Yc[0:64, :, :], t_Yc, t_Y0), vcopy(Y[64:128, :, 64:128], Yc[64:128, :, :], t_Yc, t_Y0)]
        MV, Ut = (pRf[:, 1024 * k:1024 * k + 1024].rearrange("p (t n) -> p t n", t=2) for k in range(2))
        t_MV, t_Ut, t_TA = [], [], []
        for b_ in range(2):
            b = bank()
            for h in range(8):
                p = prob(b_, h % 2, h // 2)
                last = mm(b.t[:, h * 64:h * 64 + 64], GK[:, p, 0:128], vtok[:, b_, h * 64:h * 64 + 64], True, True,
                          b.rel, t_GK, t_tok["v"])
            op = vcopy(MV[:, b_, :], b.t[:, :], last, t_inv)
            free(b, op)
            t_MV.append(op)
            fill(plan.pop(0))
        for b_ in range(2):
            b = bank()
            for h in range(8):
                p = prob(b_, h % 2, h // 2)
                last = mm(b.t[:, h * 64:h * 64 + 64], Y[:, p, :], MV[:, b_, h * 64:h * 64 + 64], True, True, b.rel, t_Y, t_MV)
            op = vts1(Ut[:, b_, :], b.t[:, :], -1.0, ALU.mult, last, t_inv)
            free(b, op)
            t_Ut.append(op)
            fill(plan.pop(0))
        for j in range(2):
            b = bank()
            for q in range(2):
                i = 2 * j + q
                for b_ in range(2):
                    for r in range(2):
                        h = 2 * i + r
                        last = mm(b.t[64 * r:64 * r + 64, q * 256 + b_ * 128:q * 256 + b_ * 128 + 128],
                                  atok[:, b_, h * 64:h * 64 + 64], Y[:, prob(b_, r, i), :], True, True, b.rel, t_Y, t_tok["a"])
            op = vcopy(TAT[:, 2 * j:2 * j + 2, :], b.t[:, :].rearrange("p (a b) -> p a b", a=2), last, t_inv)
            free(b, op)
            t_TA.append(op)
            fill(plan.pop(0))
        ST = pRf[:, 2048:3328].rearrange("p (c i d) -> p c i d", c=5, i=4)
        yB = t1.rearrange("p a b -> p (a b)").rearrange("p (t n) -> p t n", t=2)
        yr = junk[:, :].rearrange("p (t n) -> p t n", t=2)
        ysb = pmf[:, 0:1024].rearrange("p (t n d) -> p t n d", t=2, d=64)
        t_S = V(lambda e: e.memset(ST[:, 0, :, :], 0.0), t_pm)
        t_nU = []

        def finish_y(tb, w, t_yb):
            y8 = yr[:, tb, :].rearrange("p (n d) -> p n d", d=64)
            q8, st = ysq[:, tb * 8:tb * 8 + 8, :], lambda i: yst[:, i, tb * 8:tb * 8 + 8]
            bo_ = G(lambda e: e.tensor_tensor(ysb[:, tb, :, :], vtok[:, tb, :].rearrange("p (n d) -> p n d", d=64),
                                              bc(bon[:, tb * 8:tb * 8 + 8], 2, 64), ALU.mult), t_bon, t_tok["v"], t_use)
            v = vred(st(0), y8, ALU.add, w)
            yield
            v = vts1(st(0), st(0), 1.0 / 64, ALU.mult, v)
            v = vtt(y8, y8, bc(st(0), 2, 64), ALU.subtract, v)
            yield
            q = vtt(q8, y8, y8, ALU.mult, v)
            yield
            q = vred(st(1), q8, ALU.add, q)
            yield
            q = vts(st(1), st(1), 1.0 / 64, 64e-5, ALU.mult, ALU.add, q)
            q = rsqrt(st(1), st(1), q)
            yield
            v = vtt(y8, y8, bc(st(1), 2, 64), ALU.mult, q)
            yield
            v = vtt(yr[:, tb, :], yr[:, tb, :], rows[:, 1024:1536], ALU.mult, v, t_rows)
            yield
            v = vtt(yr[:, tb, :], yr[:, tb, :], rows[:, 1536:2048], ALU.add, v)
            yield
            v = vtt(y8, y8, ysb[:, tb, :, :], ALU.add, v, bo_)
            yield
            t_yb.append(vtt(yB[:, tb, :], yr[:, tb, :], gtok[:, tb, :], ALU.mult, v, t_g))

        t_yb = []
        fy = iter(())
        for b_ in range(2):
            by = [bank(), bank()]
            for hf in range(2):
                c = 2 * b_ + hf
                ps = slice(64 * hf, 64 * hf + 64)
                cs = slice(64 * c, 64 * c + 64)
                bs = bank()
                so = lambda r, i: (bs.t[64 * r:64 * r + 64, i * 64:i * 64 + 64], slice((2 * i + r) * 64, (2 * i + r) * 64 + 64))
                bu = [bank(), bank()]
                t_n = []
                for r in range(2):
                    rs = slice(64 * r, 64 * r + 64)
                    for i in range(4):
                        last = mm(bu[r].t[ps, i * 64:i * 64 + 64], TAT[rs, i, cs], ST[rs, c, i, :], True, True,
                                  bu[r].rel, t_TA, t_S)
                    hv = lambda t: t[ps, b_, :].rearrange("p (i r d) -> p i r d", r=2, d=64)[:, :, r, :]
                    op = vtt(hv(nU), hv(Ut), bu[r].t[ps, 0:256].rearrange("p (i d) -> p i d", d=64), ALU.subtract, last, t_Ut, t_use)
                    free(bu[r], op)
                    t_n.append(op)
                    next(fy, None)
                    fill(plan.pop(0))
                t_nU += t_n
                for r in range(2):
                    rs = slice(64 * r, 64 * r + 64)
                    for i in range(4):
                        ly = mm(by[r].t[ps, i * 64:i * 64 + 64], ARt[rs, i, 1, cs], ST[rs, c, i, :], True, True, by[r].rel, t_S)
                fill(plan.pop(0))
                for r in range(2):
                    for i in range(4):
                        o, hs = so(r, i)
                        mm(o, ktok[ps, b_, hs], vtok[ps, b_, hs], True, False, bs.rel, t_tok["k"], t_tok["v"])
                        last = mm(o, btok[ps, b_, hs], nU[ps, b_, hs], False, True, t_tok["b"], t_n[r])
                v = vtt(ST[:, c + 1, :, :], bs.t[:, 0:256].rearrange("p (i d) -> p i d", d=64), ST[:, c, :, :], ALU.add, last, t_S)
                free(bs, v)
                t_S = vtt(ST[:, c + 1, :, :], ST[:, c + 1, :, :], bc(Pc[:, :, 64 * c + 63], 2, 64), ALU.mult, v)
                next(fy, None)
                next(fy, None)
            b = bank()
            for h in range(8):
                hs = slice(h * 64, h * 64 + 64)
                p = prob(b_, h % 2, h // 2)
                mm(b.t[:, hs], GK[:, p, 128:256], vtok[:, b_, hs], True, False, b.rel)
                last = mm(b.t[:, hs], GB[:, p, 128:256], nU[:, b_, hs], False, True, t_nU)
            for r in range(2):
                hv = lambda t: t[:, b_, :].rearrange("p (i r d) -> p i r d", r=2, d=64)[:, :, r, :]
                op = acopy(hv(yr), by[r].t[:, 0:256].rearrange("p (i d) -> p i d", d=64), ly, t_ya)
                free(by[r], op)
            v = vtt(yr[:, b_, :], b.t[:, :], yr[:, b_, :], ALU.add, last, op)
            free(b, v)
            t_end_y = last
            for _ in fy:
                pass
            fy = finish_y(b_, v, t_yb)
        run(g_mla)
        for _ in fy:
            pass

        def second_half():
            t_yT.extend(to_T([yB[:, tb, :] for tb in range(2)], yhB, 4, None, t_yb, t_end_y))
        t_x3 = residual(hB, hA, (yhA, yhB), t_yT, "w_o", t_x2, between=second_half)
        if stop == 5:
            return finish(nc, Q, sems, ctx, outs, hB, t_x3, load)

        t_dead = [t_yb, t_x3]
        w_xT = to_T(tbs(hB), xT, 8, gcols("g_ffn"), t_x3, t_x3)
        sx = [rstd(hB[:, tb, :], 1024, t_x3[tb]) for tb in range(2)]
        n_n = [v[1] for v in sx]
        bo = [bank() for _ in range(4)]
        for tb in range(2):
            for g in range(2):
                b = bo[2 * tb + g]
                t_seed = mm(b.t[:, :], ident, hB[:, tb, g * 512:g * 512 + 512], True, False, b.rel, t_x3[tb])
        rows_ = rows_of([v[0] for v in sx], n_n)
        next(rows_)
        t_dead = [t_dead, w_xT, n_n, t_seed]
        SE = P.sub()
        slT = sbuf(SE, "slT", [128, 3, 256])
        gp = sbuf(SE, "gp", [128, 3, 256], BF16)
        Wr = sbuf(SE, "Wr", [128, 2, 2, 256], F32R)
        Bo = sbuf(SE, "Bo", [128, 2, 8, 128], BF16)
        SO = Mem(nc, hA_at, x_at)
        Ao = sbuf(SO, "Ao", [128, 2, 3, 8, 64], BF16)
        Eo = sbuf(SO, "Eo", [128, 8, 64], BF16)
        ge_at = SE.at
        GE = sbuf(SE, "GE", [128, 128, 256])
        ST_ = Mem(nc, ge_at + 65536, ge_at + 131072)
        qP = sbuf(ST_, "qP", [128, 16, 256])
        sS = sbuf(ST_, "sS", [128, 2, 16, 128])
        sS2 = sbuf(ST_, "sS2", [128, 16, 128])
        m16 = sbuf(ST_, "m16", [128, 16, 16])
        ix = sbuf(ST_, "ix", [128, 16, 16], U32)
        ixf = sbuf(ST_, "ixf", [128, 16, 16])
        top = sbuf(ST_, "top", [128, 8, 16])
        pst = sbuf(ST_, "pst", [128, 8, 16], U32)
        psi = sbuf(ST_, "psi", [128, 2, 128], U32)
        psf = sbuf(ST_, "psf", [128, 2, 128])
        sel = sbuf(ST_, "sel", [128, 2, 3, 128])
        gs = sbuf(ST_, "gs", [128, 2, 2, 8])
        cand = qP[:, 0:8, :].rearrange("p h (a b) -> p h a b", b=16)
        cand2 = qP[:, 8:16, :]
        t_qP = []
        x32 = sS2[:, :, :].rearrange("p a b -> p (a b)").rearrange("p (k t) -> p k t", k=8)
        t_32 = []

        def ev_q(b, j, c, last):
            op = copy(qP[:, j:j + 2, :], b.t[:, :].rearrange("p (a b) -> p a b", a=2), last, t_dead)
            t_qP.append(op)
            if j == 4:
                t_rw = run(rows_)
                for k in range(0, 8, 4):
                    ks = slice(k, k + 4)
                    v = vtt(x32[:, ks, :], xT[0][:, ks, :].bitcast(F32), xT[1][:, ks, :].bitcast(F32), ALU.add, t_dead, w_xT)
                    t_32.append(vtt(x32[:, ks, :], x32[:, ks, :], bc(rw[:, :], 1, 4), ALU.mult, v, t_rw))
            return op
        projT(xT, w_xT, "w_pq", 16, ev_q)
        t_dead = [t_dead, t_32]
        t_pq = Q.q["pe"][-1][0]
        w_xT = []
        for k in range(8):
            h, l = xT[0][:, k, :], xT[1][:, k, :]
            a = acopy(h, x32[:, k, :], t_32, t_pq)
            w_xT.append([a, vtt(l, x32[:, k, :], h.bitcast(F32), ALU.subtract, a, t_pq)])
        t_s = [[], []]
        for half in range(2):
            wt, _, tk, i_k = wnext("sub_keys", half)
            for tb in range(2):
                for j in range(2):
                    b = bank()
                    for q in range(4):
                        hp = 8 * half + 4 * j + q
                        last = mm(b.t[:, q * 128:q * 128 + 128], qP[:, hp, tb * 128:tb * 128 + 128],
                                  wt[:, (hp % 8) * 128:(hp % 8) * 128 + 128], True, True, b.rel, tk, t_qP)
                    h0 = 8 * half + 4 * j
                    op = copy(sS[:, tb, h0:h0 + 4, :], b.t[:, :].rearrange("p (a b) -> p a b", a=4), last, t_dead)
                    free(b, op)
                    t_s[tb].append(op)
            wdone(i_k, last)
        t_scores = last

        def top16(n, src, src2, m, xi, w):
            a = [V(lambda e, i=i: e.max(m[:, i, 0:8], src(i)), w) for i in range(n)]
            b1 = [V(lambda e, i=i: e.max_index(xi[:, i, 0:8], m[:, i, 0:8], src(i)), a[i]) for i in range(n)]
            c1 = [V(lambda e, i=i: e.match_replace(src2(i), m[:, i, 0:8], src(i), -3.0e38), a[i]) for i in range(n)]
            d1 = [V(lambda e, i=i: e.max(m[:, i, 8:16], src2(i)), c1[i]) for i in range(n)]
            e1 = [V(lambda e, i=i: e.max_index(xi[:, i, 8:16], m[:, i, 8:16], src2(i)), d1[i]) for i in range(n)]
            return [e1[-1], b1[-1], d1[-1]]

        t_sl = []
        t_end = [[t_scores, w_xT]]

        def choose(tb):
            v = top16(16, lambda i: sS[:, tb, i, :], lambda i: sS2[:, i, :], m16, ix, [t_s[tb], t_end[0]])
            v1 = vcopy(ixf[:, :, :], ix[:, :, :], v)
            mv = m16[:, :, :].rearrange("p (h c) k -> p h c k", c=2)
            xv = ixf[:, :, :].rearrange("p (h c) k -> p h c k", c=2)
            v = vtt(cand, bc(mv[:, :, 0, :], 3, 16), bc(mv[:, :, 1, :], 2, 16), ALU.add, v, t_end[0])
            v = top16(8, lambda i: cand[:, i, :, :].rearrange("p a b -> p (a b)"), lambda i: cand2[:, i, :], top, pst, v)
            sg_ = sel[:, tb, 2, :].rearrange("p (h k) -> p h k", k=16)
            g = vtt(sg_, top[:, :, :], bc(top[:, :, 0], 2, 16), ALU.subtract, v)
            pf = pst[:, :, :].rearrange("p h k -> p (h k)")
            s0 = vts1(psi[:, 0, :], pf, 4, ALU.logical_shift_right, v)
            s1 = vts1(psi[:, 1, :], pf, 15, ALU.bitwise_and, v)
            s0 = vcopy(psf[:, :, :], psi[:, :, :], s0, s1)
            eqf = cand.rearrange("p h a b -> p (h a) b")
            for j in range(2):
                q = vtt(eqf, bc(psf[:, j, :], 2, 16), bc(C("iota16"), 1, 128), ALU.is_equal, s0, v)
                q = vtt(cand, cand, bc(xv[:, :, j, :], 2, 16), ALU.mult, q, v1)
                s0 = vred(sel[:, tb, j, :], eqf, ALU.add, q)
            yield
            g = act(sg_, sg_, ACT.Exp, g, n_n[tb], scale=sx[tb][0])
            g = vred(gs[:, tb, 0, :], sg_, ALU.add, g)
            g = V(lambda e: e.reciprocal(gs[:, tb, 1, :], gs[:, tb, 0, :]), g)
            g = vtt(sg_, sg_, bc(gs[:, tb, 1, :], 2, 16), ALU.mult, g)
            t_end[0] = [s0, g]
            yield
            b = bank()
            for j in range(3):
                last = tp(b.t[:, j * 128:j * 128 + 128], sel[:, tb, j, :], b.rel, s0, g)
            op = vcopy(slT[:, :, tb * 128:tb * 128 + 128], b.t[:, 0:384].rearrange("p (a b) -> p a b", a=3), last, t_dead)
            free(b, op)
            t_sl.append(op)
            t_end[0] = [t_end[0], last]

        t_ge = {}

        def scores(c):
            wh, wl, tk, i = wnext("eu", c)
            b = bank()
            for k in range(8):
                cs = slice(k * 128, k * 128 + 128)
                last = mm3(b.t[:, 0:256], (wh[:, cs], wl[:, cs]), tuple(t[:, k, :] for t in xT), k == 0, k == 7, tk, b.rel, w_xT[k])
            wdone(i, last)
            t_ge[c] = act(GE[:, c, :], b.t[:, 0:256], ACT.Gelu, last, t_dead, t_end[0] if c >= 64 else None)
            free(b, t_ge[c])

        t_G = [[], []]
        n_b = [0]
        used = [None, None]
        t_eo = [None]

        def gates(h):
            for t8 in range(32):
                u = n_b[0] % 2
                n_b[0] += 1
                ts = slice(8 * t8, 8 * t8 + 8)
                vb = vtt(Bo[:, u, :, :], bc(slT[:, 1, ts], 2, 128), bc(C("iota"), 1, 8), ALU.is_equal, t_sl, used[u], t_dead)
                ve = vtt(Eo[:, :, :], bc(slT[:, 0, ts], 2, 64), bc(C("iota")[:, 64 * h:64 * h + 64], 1, 8), ALU.is_equal, t_sl, t_eo[0])
                va_ = [vtt(Ao[:, u, k, :, :], Eo[:, :, :], bc(gp[:, k, ts], 2, 64), ALU.mult, ve, t_gp, used[u]) for k in range(3)]
                t_eo[0] = va_[-1]
                yield
                b = bank()
                for q in range(8):
                    for k in range(3):
                        last = mm(b.t[:, q * 64:q * 64 + 64], Bo[:, u, q, :], Ao[:, u, k, q, :], k == 0, k == 2, b.rel, vb, va_)
                used[u] = last
                o = GE[:, 64 * h:64 * h + 64, ts]
                op = vtt(o, o, b.t[:, :].rearrange("p (t i) -> p i t", t=8), ALU.mult, last, [t_ge[c] for c in range(64 * h, 64 * h + 64)])
                free(b, op)
                t_G[h].append(op)
                yield

        t_O = {}
        t_Wd = {}

        def weight(c):
            h, l = Wr[:, c % 2, 0, :], Wr[:, c % 2, 1, :]
            a = acopy(h, GE[:, c, :], t_G[c // 64], t_O.get(c - 2), t_dead)
            t_Wd[c] = [a, vtt(l, GE[:, c, :], h.bitcast(F32), ALU.subtract, a, t_G[c // 64], t_O.get(c - 2), t_dead)]

        def apply(c):
            wh, wl, tk, i = wnext("ev", c)
            for tb in range(2):
                for g in range(2):
                    cs = slice(g * 512, g * 512 + 512)
                    x = tuple(Wr[:, c % 2, q, tb * 128:tb * 128 + 128] for q in range(2))
                    last = mm3(bo[tb * 2 + g].t[:, :], x, (wh[:, cs], wl[:, cs]), False, c == 127, tk, t_Wd[c])
            wdone(i, last)
            t_O[c] = last

        ch = [choose(0), choose(1)]
        next(ch[0])
        for c in range(64):
            scores(c)
            if c == 20:
                next(ch[0])
            if c == 26:
                next(ch[0], None)
                next(ch[1])
            if c == 52:
                next(ch[1])
            if c == 56:
                next(ch[1], None)
            if c == 58:
                t_gp = []
                r_ = slT[:, 2, :]
                w = t_sl
                for k in range(3):
                    t_gp.append(vcopy(gp[:, k, :], r_, w, t_dead))
                    if k < 2:
                        w = vtt(r_, r_, gp[:, k, :], ALU.subtract, t_gp[-1])
                g_ = gates(0)
            if c == 63:
                next(g_)
        for c in range(64, 128):
            next(g_, None)
            if c == 127:
                weight(0)
            scores(c)
        g_ = gates(1)
        for c in range(128):
            if c < 64:
                next(g_, None)
            if c == 63:
                for _ in g_:
                    pass
            if c + 1 < 128:
                weight(c + 1)
            apply(c)
        fin = [[], []]
        o = GE[:, 0:8, :].rearrange("p a b -> p (a b)").rearrange("p (t n) -> p t n", t=2)
        for tb in range(2):
            for g in range(2):
                gsl = slice(g * 512, g * 512 + 512)
                fin[tb].append(copy(o[:, tb, gsl], bo[tb * 2 + g].t[:, :], t_O[127]))
        return finish(nc, Q, sems, ctx, outs, o, fin, load)


def finish(nc, Q, sems, ctx, out, src, toks, load):
    o = out.rearrange("b (t p) d -> p (b t) d", p=128)
    d = load("sp", o, src[:, :, :] if len(src.shape) == 3 else src, toks)
    Q.add("sp", lambda e: e.nop(), d)
    Q.number(sems)
    block = ctx.enter_context(nc.Block())

    @block.tensor
    def _(e):
        Q.emit("pe", e)

    @block.vector
    def _(e):
        Q.emit("dve", e)

    @block.scalar
    def _(e):
        Q.emit("act", e)

    @block.gpsimd
    def _(e):
        Q.emit("pool", e)

    @block.sync
    def _(e):
        Q.emit("sp", e)


def layout(inputs):
    I = {k: np.asarray(v) for k, v in inputs.items()}
    c, d = constants()

    def w_t(W):
        K, N = W.shape
        return np.ascontiguousarray(W.reshape(K // 128, 128, N // 128, 128).transpose(2, 1, 0, 3)).reshape(N // 128, 128, K)

    def w_g(W):
        N = W.shape[1]
        return np.ascontiguousarray(W.reshape(4, 2, 128, N // 512, 512).transpose(3, 0, 2, 1, 4)).reshape(-1, 128, 1024)

    def w_k(W):
        return np.ascontiguousarray(W.reshape(-1, 128, W.shape[1]))

    def cols(v):
        return v.reshape(-1, 128).T

    def row(v):
        return np.broadcast_to(v.reshape(1, -1), (128, v.size))

    w_in = I["w_in"][0]
    w2 = I["w_in_2"][0]
    pk = {"g_mix": I["g_mix"], "g_cross": I["g_cross"], "g_mem": I["g_mem"], "g_mlp": I["g_mlp"], "g_subln": I["g_subln"],
          "g_mix_2": I["g_mix_2"], "g_cq": I["g_cq_2"], "g_ckv": I["g_ckv_2"], "g_attn_out": I["g_attn_out_2"],
          "rwkv_mu": I["rwkv_mu_2"], "w0": I["w0_2"], "a0": I["a0_2"], "k_k": I["k_k_2"], "k_a": I["k_a_2"], "r_k": I["r_k_2"],
          "g_ffn": I["g_ffn_2"], "g_final": I["g_final"]}
    pk = {k: cols(v) for k, v in pk.items()}
    poff, _ = offsets(pk)
    rows = np.concatenate([row(I[k]) for k in ("g_final", "ln_x_w_2", "ln_x_b_2", "g_qnorm_2", "g_knorm_2", "lambda_q1",
                                                "lambda_k1", "lambda_q2", "lambda_k2")], 1)
    rw = w_t(w2[:, 672:2464])
    T = {
        "x": I["x"][0], "mem": I["mem"][0], "cst": np.concatenate(list(c.values()), 1), "dst": np.concatenate(list(d.values()), 1),
        "par": np.concatenate(list(pk.values()), 1), "rows": rows,
        "pos": np.concatenate([I["positions"].reshape(2, 128).T, I["positions_2"].reshape(2, 128).T], 1),
        "w_in_a": w_g(np.concatenate([w_in[:, 0:1536], w_in[:, 2560:3072]], 1)), "w_in_t": w_t(w_in[:, 1536:2560]),
        "w_out": w_g(I["w_out"][0])[[2, 3, 6, 7, 0, 1, 4, 5]], "w_xk": w_t(I["w_xkv"][0][:, 0:1024]), "w_xv": w_g(I["w_xkv"][0][:, 1024:2048]),
        "w_xq": w_t(I["w_xq"][0]), "w_xo": w_g(I["w_xo"][0])[[0, 1, 4, 5, 2, 3, 6, 7]], "w_up": w_t(I["w_up"][0]), "w_down": w_k(I["w_down"][0]),
        "w_mla": w_k(w2[:, 0:672]), "w_rwkv_0": rw[[12, 13, 4, 5, 6, 7, 0, 1]], "w_rwkv_1": rw[[2, 3, 8, 9, 10, 11]], "w_uq": w_k(I["w_uq_2"][0]),
        "w_ukv": w_k(np.concatenate([I["w_uk_2"][0], I["w_uv_2"][0]], 1)),
        "w_lora": np.concatenate([np.concatenate([I["w2_2"][0], I["a2_2"][0]], 0), I["g2_2"][0]], 1)[None],
        "w_o": w_g(I["w_o_2"][0])[[0, 1, 4, 5, 2, 3, 6, 7]], "w_pq": w_t(I["w_pq_2"][0]),
        "sub_keys": I["sub_keys_2"][0].transpose(3, 0, 1, 2).reshape(128, 2, 1024).transpose(1, 0, 2),
        "eu": np.ascontiguousarray(I["expert_u_2"][0].reshape(128, 128, 8, 128).transpose(0, 3, 2, 1)).reshape(128, 128, 1024),
        "ev": I["expert_v_2"][0].reshape(128, 128, 1024),
    }
    return {k: np.ascontiguousarray(v) for k, v in T.items()}, poff


def kernel(**inputs):
    import concourse.bacc as _bacc
    from concourse import mybir as _mybir
    from concourse.bass_utils import run_bass_kernel_spmd as _run

    nc = _bacc.Bacc("TRN2", target_bir_lowering=False, num_devices=1)
    T, poff = layout(inputs)
    arrays, args = {}, {}
    for name, a in T.items():
        arrays[f"in_{name}"] = a
        args[name] = nc.dram_tensor(f"in_{name}", a.shape, _mybir.dt.from_np(a.dtype), kind="ExternalInput").ap()
    out = nc.dram_tensor("out_0", (1, 256, 1024), _mybir.dt.from_np(np.dtype("float32")), kind="ExternalOutput").ap()
    build(nc, args, poff, out, STOP)
    r = _run(nc, [arrays], core_ids=[0])
    return r.results[0]["out_0"]


STOP = 99
```
